# Optimizing a Trainium2 kernel written in Bass

```python
import math
import jax, jax.numpy as jnp
from jax import lax
import numpy as np

D_MODEL = 1024
BATCH = 1
SEQ = 512
DEPTH = 1

N_META = 16
N_HEADS = 16
N_KV_HEADS = 4
HEAD_DIM = 64
Q_GROUP = N_HEADS // N_KV_HEADS
WINDOW = 128
BLOCK = 128
SSM_WIDTH = D_MODEL // 2
SSM_GROUP_CH = 16
SSM_GROUPS = SSM_WIDTH // SSM_GROUP_CH
SSM_STATE = 64
N_DIR = 2
DT_MIN = 1e-3
DT_MAX = 1e-1
D_FF = 2816
EPS = 1e-6
NEG = -1e30

ATTN_Q = N_HEADS * HEAD_DIM
ATTN_KV = N_KV_HEADS * HEAD_DIM
SPLITS = [ATTN_Q, ATTN_Q + ATTN_KV, ATTN_Q + 2 * ATTN_KV,
          ATTN_Q + 2 * ATTN_KV + SSM_WIDTH,
          ATTN_Q + 2 * ATTN_KV + SSM_WIDTH + D_MODEL]
IN_COLS = ATTN_Q + 2 * ATTN_KV + SSM_WIDTH + 2 * D_MODEL

kernel_name = "hybrid_s5_swa_macaron_encoder"

def alibi_slopes():
    s = 2.0 ** (-8.0 * np.arange(1, N_HEADS + 1) / N_HEADS)
    return jnp.asarray(s.reshape(N_KV_HEADS, Q_GROUP), dtype=jnp.float32)

def rmsnorm(x, g):
    xf = x.astype(jnp.float32)
    y = xf * lax.rsqrt(jnp.mean(xf * xf, axis=-1, keepdims=True) + EPS)
    return (y * g.astype(jnp.float32)).astype(x.dtype)

def swiglu(h, w_gate, w_up, w_down):
    return (jax.nn.silu(h @ w_gate) * (h @ w_up)) @ w_down

def s5_direction(ug, lam_re, lam_im, log_dt, b_re, b_im, c_re, c_im, reverse):
    f32 = jnp.float32
    lam = lax.complex(lam_re.astype(f32), lam_im.astype(f32))
    dt = jnp.exp(log_dt.astype(f32))[:, None]
    lam_bar = jnp.exp(lam * dt)
    b_bar = ((lam_bar - 1.0) / lam)[:, :, None] * lax.complex(b_re.astype(f32), b_im.astype(f32))
    c_mat = lax.complex(c_re.astype(f32), c_im.astype(f32))
    bu = jnp.einsum('blgc,gpc->blgp', ug, b_bar)
    a = jnp.broadcast_to(lam_bar, bu.shape)

    def combine(e1, e2):
        a1, b1 = e1
        a2, b2 = e2
        return a1 * a2, a2 * b1 + b2

    _, states = lax.associative_scan(combine, (a, bu), reverse=reverse, axis=1)
    return jnp.einsum('blgp,gcp->blgc', states, c_mat).real

def ssm_branch(u, lam_re, lam_im, log_dt, b_re, b_im, c_re, c_im, d, w_glu):
    B, L, _ = u.shape
    uf = u.astype(jnp.float32)
    ug = uf.reshape(B, L, SSM_GROUPS, SSM_GROUP_CH)
    y = jnp.zeros_like(ug)
    for dr in range(N_DIR):
        y = y + s5_direction(ug, lam_re[dr], lam_im[dr], log_dt[dr], b_re[dr], b_im[dr],
                             c_re[dr], c_im[dr], reverse=(dr == 1))
    y = y.reshape(B, L, SSM_WIDTH) + d.astype(jnp.float32) * uf
    z = jax.nn.gelu(y).astype(u.dtype)
    return z * jax.nn.sigmoid(z @ w_glu)

def windowed_gqa(q, k, v, sink):
    B, L = q.shape[:2]
    pad = BLOCK - N_META
    Lp = L + pad
    nb = Lp // BLOCK
    k_meta, v_meta = k[:, :N_META], v[:, :N_META]

    def to_blocks(t):
        tp = jnp.pad(t, ((0, 0), (pad, 0), (0, 0), (0, 0)))
        return tp.reshape(B, nb, BLOCK, *t.shape[2:])

    def band(t):
        tb = jnp.pad(to_blocks(t), ((0, 0), (1, 1), (0, 0), (0, 0), (0, 0)))
        return jnp.concatenate([tb[:, :-2], tb[:, 1:-1], tb[:, 2:]], axis=2)

    qb = to_blocks(q).reshape(B, nb, BLOCK, N_KV_HEADS, Q_GROUP, HEAD_DIM)
    kband, vband = band(k), band(v)
    scale = HEAD_DIM ** -0.5

    qi = jnp.arange(BLOCK)
    sj = jnp.arange(3 * BLOCK)
    dist = jnp.abs(qi[:, None] + BLOCK - sj[None, :])
    kpos = (jnp.arange(nb)[:, None] - 1) * BLOCK + sj[None, :]
    kvalid = (kpos >= BLOCK) & (kpos < Lp)
    valid = (dist <= WINDOW)[None] & kvalid[:, None, :]
    slopes = alibi_slopes()

    s_band = jnp.einsum('bnqkgd,bnskd->bnkgqs', qb, kband,
                        preferred_element_type=jnp.float32) * scale
    s_band = s_band - slopes[:, :, None, None] * dist.astype(jnp.float32)
    s_band = jnp.where(valid[None, :, None, None], s_band, NEG)
    s_meta = jnp.einsum('bnqkgd,bmkd->bnkgqm', qb, k_meta,
                        preferred_element_type=jnp.float32) * scale
    s_sink = jnp.broadcast_to(sink.astype(jnp.float32).reshape(N_KV_HEADS, Q_GROUP)[None, None, :, :, None, None],
                              (B, nb, N_KV_HEADS, Q_GROUP, BLOCK, 1))
    p = jax.nn.softmax(jnp.concatenate([s_band, s_meta, s_sink], axis=-1), axis=-1)
    p_band = p[..., :3 * BLOCK].astype(v.dtype)
    p_meta = p[..., 3 * BLOCK:3 * BLOCK + N_META].astype(v.dtype)
    out = (jnp.einsum('bnkgqs,bnskd->bnqkgd', p_band, vband)
           + jnp.einsum('bnkgqm,bmkd->bnqkgd', p_meta, v_meta))
    return out.reshape(B, Lp, N_HEADS * HEAD_DIM)[:, pad:]

def mixer(h, w_in, lam_re, lam_im, log_dt, b_re, b_im, c_re, c_im, d, w_glu, sink,
          w_branch_ssm, w_branch_attn, w_out):
    B, L, _ = h.shape
    proj = h @ w_in
    q, k, v, u, g_s, g_a = jnp.split(proj, SPLITS, axis=-1)
    y_attn = windowed_gqa(q.reshape(B, L, N_HEADS, HEAD_DIM),
                          k.reshape(B, L, N_KV_HEADS, HEAD_DIM),
                          v.reshape(B, L, N_KV_HEADS, HEAD_DIM), sink)
    y_ssm = ssm_branch(u, lam_re, lam_im, log_dt, b_re, b_im, c_re, c_im, d, w_glu)
    merged = (jax.nn.sigmoid(g_s) * (y_ssm @ w_branch_ssm)
              + jax.nn.sigmoid(g_a) * (y_attn @ w_branch_attn))
    return merged @ w_out

def setup_inputs(seed: int = 0) -> dict:
    key = jax.random.key(seed)
    ks = jax.random.split(key, 32)
    f32 = jnp.float32

    def nrm(k, shape, fan_in):
        return jax.random.normal(k, shape, f32) * fan_in ** -0.5

    def gain(k, shape):
        return 1.0 + 0.05 * jax.random.normal(k, shape, f32)

    G, P, CH = SSM_GROUPS, SSM_STATE, SSM_GROUP_CH
    n = jnp.arange(P, dtype=f32)
    return {
        "x": jax.random.normal(ks[0], (BATCH, SEQ, D_MODEL), f32),
        "meta_tokens": jax.random.normal(ks[1], (N_META, D_MODEL), f32),
        "ffn1_norm": gain(ks[2], (DEPTH, D_MODEL)),
        "ffn1_w_gate": nrm(ks[3], (DEPTH, D_MODEL, D_FF), D_MODEL),
        "ffn1_w_up": nrm(ks[4], (DEPTH, D_MODEL, D_FF), D_MODEL),
        "ffn1_w_down": nrm(ks[5], (DEPTH, D_FF, D_MODEL), D_FF),
        "mix_norm": gain(ks[6], (DEPTH, D_MODEL)),
        "w_in": nrm(ks[7], (DEPTH, D_MODEL, IN_COLS), D_MODEL),
        "ssm_lam_re": -0.5 + 0.01 * jax.random.normal(ks[8], (DEPTH, N_DIR, G, P), f32),
        "ssm_lam_im": math.pi * n + 0.01 * jax.random.normal(ks[9], (DEPTH, N_DIR, G, P), f32),
        "ssm_log_dt": jax.random.uniform(ks[10], (DEPTH, N_DIR, G), f32,
                                         minval=math.log(DT_MIN), maxval=math.log(DT_MAX)),
        "ssm_b_re": nrm(ks[11], (DEPTH, N_DIR, G, P, CH), 2 * CH),
        "ssm_b_im": nrm(ks[12], (DEPTH, N_DIR, G, P, CH), 2 * CH),
        "ssm_c_re": nrm(ks[13], (DEPTH, N_DIR, G, CH, P), 2 * P),
        "ssm_c_im": nrm(ks[14], (DEPTH, N_DIR, G, CH, P), 2 * P),
        "ssm_d": jax.random.normal(ks[15], (DEPTH, SSM_WIDTH), f32),
        "ssm_w_glu": nrm(ks[16], (DEPTH, SSM_WIDTH, SSM_WIDTH), SSM_WIDTH),
        "attn_sink": 0.5 * jax.random.normal(ks[17], (DEPTH, N_HEADS), f32),
        "w_branch_ssm": nrm(ks[18], (DEPTH, SSM_WIDTH, D_MODEL), SSM_WIDTH),
        "w_branch_attn": nrm(ks[19], (DEPTH, ATTN_Q, D_MODEL), ATTN_Q),
        "w_out": nrm(ks[20], (DEPTH, D_MODEL, D_MODEL), D_MODEL),
        "ffn2_norm": gain(ks[21], (DEPTH, D_MODEL)),
        "ffn2_w_gate": nrm(ks[22], (DEPTH, D_MODEL, D_FF), D_MODEL),
        "ffn2_w_up": nrm(ks[23], (DEPTH, D_MODEL, D_FF), D_MODEL),
        "ffn2_w_down": nrm(ks[24], (DEPTH, D_FF, D_MODEL), D_FF),
        "final_norm": gain(ks[25], (D_MODEL,)),
    }

def reference(x, meta_tokens, ffn1_norm, ffn1_w_gate, ffn1_w_up, ffn1_w_down,
              mix_norm, w_in, ssm_lam_re, ssm_lam_im, ssm_log_dt, ssm_b_re, ssm_b_im,
              ssm_c_re, ssm_c_im, ssm_d, ssm_w_glu, attn_sink, w_branch_ssm,
              w_branch_attn, w_out, ffn2_norm, ffn2_w_gate, ffn2_w_up, ffn2_w_down,
              final_norm):
    B = x.shape[0]
    meta = jnp.broadcast_to(meta_tokens.astype(x.dtype)[None], (B, N_META, D_MODEL))
    h = jnp.concatenate([meta, x], axis=1)
    for l in range(DEPTH):
        h = h + 0.5 * swiglu(rmsnorm(h, ffn1_norm[l]), ffn1_w_gate[l], ffn1_w_up[l], ffn1_w_down[l])
        h = h + mixer(rmsnorm(h, mix_norm[l]), w_in[l], ssm_lam_re[l], ssm_lam_im[l],
                      ssm_log_dt[l], ssm_b_re[l], ssm_b_im[l], ssm_c_re[l], ssm_c_im[l],
                      ssm_d[l], ssm_w_glu[l], attn_sink[l], w_branch_ssm[l],
                      w_branch_attn[l], w_out[l])
        h = h + 0.5 * swiglu(rmsnorm(h, ffn2_norm[l]), ffn2_w_gate[l], ffn2_w_up[l], ffn2_w_down[l])
    h = rmsnorm(h, final_norm)
    return h[:, N_META:]


_drawn_inputs = setup_inputs


def setup_inputs(seed=0):
    import zlib

    import numpy as np

    out = dict(_drawn_inputs(seed))
    spreads = {}
    factors = {'mix_norm': 3.856,
     'ssm_lam_re': 64.0,
     'ssm_lam_im': 26.564,
     'ssm_log_dt': 26.364,
     'ssm_b_re': 39.728,
     'ssm_b_im': 39.832,
     'ssm_c_re': 39.576,
     'ssm_c_im': 40.552,
     'attn_sink': 64.0,
     'ffn2_norm': 2.822}
    for name, (base, spread) in spreads.items():
        noise = np.random.default_rng([zlib.crc32(name.encode()), seed]).standard_normal(out[name].shape)
        drawn = base * np.exp(spread * noise) if base else spread * noise
        out[name] = __import__('jax').numpy.asarray(drawn.astype(out[name].dtype))
    for name, factor in factors.items():
        out[name] = (out[name] * factor).astype(out[name].dtype)
    return out
```

```python
import math
from contextlib import ExitStack

import numpy as np

import concourse.bass as bass
from concourse import mybir

F32 = mybir.dt.float32
F32R = mybir.dt.float32r
ALU = mybir.AluOpType
ACT = mybir.ActivationFunctionType
AX = mybir.AxisListType

P = 128
D = 1024
KD = D // P
SEQ, META = 512, 16
T = META + SEQ
FF = 2816
KF = FF // P
HALF = T // 2
EPS = 1e-6
HEADS, KVH, DH, QG = 16, 4, 64, 4
WINDOW = 128
NBLK = SEQ // WINDOW
FAR = 3e32
GROUPS, STATE, CH = 32, 64, 16
SSM = GROUPS * CH
KS = SSM // P
GB = P // CH
CHUNK = 8
NCH = T // CHUNK
MCH = META // CHUNK
OCH = NCH - MCH
COL_Q, COL_K, COL_V = 0, HEADS * DH, (HEADS + KVH) * DH
COL_U = (HEADS + 2 * KVH) * DH
COL_GS = COL_U + SSM
COL_GA = COL_GS + D
TILES = 16
LOAD = 80
OPEN = 2

(A_, TH, NR, R_, RH, AC, E1, M0, M1, EXPA, SINH, SINR, COSM1, COS, ER, LBR, LBI, X_, DEN, CR, CI,
 R8) = range(22)
SSM_STEPS = 19

C_UP1 = 0
C_DOWN1 = C_UP1 + KF
C_U = C_DOWN1 + 2 * KD
C_ATT = C_U + KS // 2
C_GLU = C_ATT + 8
C_MERGE = C_GLU + 1
C_OUT = C_MERGE + 2 * KD
C_UP2 = C_OUT + KD // 2
C_DOWN2 = C_UP2 + KF
C_END = C_DOWN2 + 2 * KD


def split_two_pi():
    c1 = 6.28125
    c2 = math.floor((2 * math.pi - c1) * 2 ** 21) / 2 ** 21
    return c1, c2, 2 * math.pi - c1 - c2


class At:

    def __init__(self, base, i=None, stride=0):
        self.base, self.i, self.stride = base, i, stride

    def plus(self, n):
        return self.base + n if self.i is None else self.i * self.stride + (self.base + n)

    def at(self, n):
        return At(self.base + n, self.i, self.stride)

    @property
    def slot(self):
        return self.base % 2

    def loads(self):
        if self.i is None:
            return LOAD * (self.base // 2 + 1)
        return self.i * (LOAD * self.stride // 2) + LOAD * (self.base // 2 + 1)


def at_end(base, times, stride, n, i):
    return At(base + (times - 1) * stride + n) if i is None else At(base + n, i, stride)


class Chain:

    def __init__(self, eng, sem):
        self.eng, self.sem, self.base, self.n = eng, sem, 0, 0

    def __call__(self, ins):
        self.n += 1
        ins.then_inc(self.sem, 1)
        self.eng.wait_ge(self.sem, self.base + self.n)

    def loop(self, i, steps):
        self.start = self.n
        self.base = i * steps
        self.steps = steps

    def end_loop(self, times):
        assert self.n - self.start == self.steps, (self.n - self.start, self.steps)
        self.base, self.n = 0, self.start + times * self.steps


def build(nc, x, meta_tokens, ffn1_norm, ffn1_w_gate, ffn1_w_up, ffn1_w_down, mix_norm, w_in,
          ssm_lam_re, ssm_lam_im, ssm_log_dt, ssm_b_re, ssm_b_im, ssm_c_re, ssm_c_im, ssm_d,
          ssm_w_glu, attn_sink, w_branch_ssm, w_branch_attn, w_out, ffn2_norm, ffn2_w_gate,
          ffn2_w_up, ffn2_w_down, final_norm, out):
    ds = bass.ds

    with ExitStack() as ctx:
        def sb(name, shape, dt=F32, stack=ctx):
            return stack.enter_context(nc.sbuf_tensor(name, shape, dt))

        def sem(name):
            return ctx.enter_context(nc.semaphore(name))

        hT = sb("hT", [P, KD, T])
        with ExitStack() as sx_:
            xh = sb("xh", [P, KD, T], F32R, sx_)
            xl = sb("xl", [P, KD, T], F32R, sx_)
        final_area = sb("final_area", [P, 2 * KD * T])
        hg = final_area[:, 0:KD * SEQ].rearrange("p (k n) -> p k n", k=KD)
        y_nat = final_area[:, KD * T:KD * T + 4 * D].rearrange("p (t n) -> p t n", t=4)
        wraw = sb("wraw", [P, 2, TILES, P])
        wh = sb("wh", [P, 2, TILES, P], F32R)
        wl = sb("wl", [P, 2, TILES, P], F32R)
        ident = sb("ident", [P, P])
        ones = sb("ones", [P, P])
        gains = sb("gains", [P, 4, KD])
        dskip = sb("dskip", [P, KS])
        ssum = sb("ssum", [P, T])
        sq = sb("sq", [P, T])
        rstd_b = sb("rstd_b", [P, T])
        rcol = sb("rcol", [P, 5])
        var = sb("var", [P, 5])
        expo = sb("expo", [P, 1])
        diag = sb("diag", [P, 5, P])
        PS = ctx.enter_context(nc.psum_tensor("PS", [P, 8, 512], F32))

        with ExitStack() as s0:
            x_nat = sb("x_nat", [P, 4, D], stack=s0)
            m_nat = sb("m_nat", [META, D], stack=s0)
        ffn_mem = []
        for n in (1, 2):
            with ExitStack() as s1:
                ffn_mem.append(dict(
                    gh=sb(f"g_hi{n}", [P, KF, T if n == 1 else SEQ], F32R, s1),
                    gl=sb(f"g_lo{n}", [P, KF, T if n == 1 else SEQ], F32R, s1),
                    t1=sb(f"gate_buf{n}", [P, 2, T], stack=s1), t2=sb(f"up_buf{n}", [P, 2, T], stack=s1)))
        with ExitStack() as s2:
            uT = sb("uT", [P, KS, CHUNK, NCH], stack=s2)
            with ExitStack() as s3:
                lam_raw = sb("lam_raw", [GROUPS, 3, 2, STATE], stack=s3)
                dt_raw = sb("dt_raw", [GROUPS, 2], stack=s3)
                prm = sb("prm", [P, 3, GROUPS], stack=s3)
                tiny = sb("tiny", [P, 24, GROUPS], stack=s3)
                pw = sb("pw", [P, 2, 9, GROUPS], stack=s3)
                ub = sb("ub", [P, 2, 9, GROUPS], stack=s3)
                ua = sb("ua", [P, 2, 9, GROUPS], stack=s3)
                cpw = sb("cpw", [P, 2, GROUPS, CHUNK], stack=s3)
                bpw = sb("bpw", [P, 2, GROUPS, CHUNK], stack=s3)
                c_raw = sb("c_raw", [P, 2, P], stack=s3)
                cT = sb("cT", [P, 2, P], stack=s3)
                b_raw = sb("b_raw", [P, 2, GB, CH], stack=s3)
                bb = sb("bb", [P, 3, GB, CH], stack=s3)
                cp = sb("cp", [P, 2, GB, CHUNK, CH], stack=s3)
                w1t = sb("w1t", [P, 2, GB, CHUNK, CH], stack=s3)
                w1 = sb("w1", [P, 2, GB, P], stack=s3)
                toep = sb("toep", [P, GB, P], stack=s3)
                krow = sb("krow", [CH, GB, 15 * CH], stack=s3)
                U = sb("U", [P, GB, NCH], stack=s3)
                E = sb("E", [P, 2, GB, 72], stack=s3)
                decay = sb("decay", [P, GB, NCH], stack=s3)
                sin_ = sb("sin_", [P, 2, GB, NCH], stack=s3)
                ta = sb("ta", [P, 2, GB * NCH], stack=s3)
                tb = sb("tb", [P, 2, GB * NCH], stack=s3)
                sx = sb("sx", [P, 2, GB, OCH], stack=s3)
                Y = sb("Y", [P, GB, OCH], stack=s3)
                yT = sb("yT", [P, CHUNK * OCH], stack=s3)
            yah = sb("yah", [P, KD, SEQ], F32R, s2)
            yal = sb("yal", [P, KD, SEQ], F32R, s2)
            with ExitStack() as s3:
                dist = sb("dist", [P, META + 3 * WINDOW], stack=s3)
                dist0 = sb("dist0", [P, META + 2 * WINDOW], stack=s3)
                negslope = sb("negslope", [P, HEADS], stack=s3)
                negsink = sb("negsink", [P, HEADS], stack=s3)
                kT = sb("kT", [P, T], stack=s3)
                vt = sb("vt", [P, 5, P], stack=s3)
                qT = sb("qT", [P, QG, SEQ], stack=s3)
                sc = sb("sc", [P, 2, QG, META + 3 * WINDOW], stack=s3)
                mx = sb("mx", [P, 2, QG], stack=s3)
                negm = sb("negm", [P, 2, QG], stack=s3)
                sk = sb("sk", [P, 2, QG], stack=s3)
                den = sb("den", [P, 2, QG], stack=s3)
                rs = sb("rs", [P, 2, QG], stack=s3)
                pt = sb("pt", [P, 2, 3, QG, P], stack=s3)
                ptm = sb("ptm", [META, 2, QG, P], stack=s3)
            ysh = sb("ysh", [P, KS, SEQ], F32R, s2)
            ysl = sb("ysl", [P, KS, SEQ], F32R, s2)
            gsig = sb("gsig", [P, 2, 2, SEQ], stack=s2)
            with ExitStack() as s3:
                zh = sb("zh", [P, KS, SEQ], F32R, s3)
                zl = sb("zl", [P, KS, SEQ], F32R, s3)
                sig = sb("sig", [P, 2, SEQ], stack=s3)
                ysf = sb("ysf", [P, 2, SEQ], stack=s3)
            with ExitStack() as s3:
                mgh = sb("mgh", [P, KD, SEQ], F32R, s3)
                mgl = sb("mgl", [P, KD, SEQ], F32R, s3)

        u_dram = nc.dram_tensor("u_regroup", [KS, GB, CH, CHUNK, NCH], F32, kind="Internal").ap()
        y_dram = nc.dram_tensor("y_regroup", [KS, CHUNK, CH, GB, OCH], F32, kind="Internal").ap()

        x_loaded, const_loaded, consts_made = sem("x_loaded"), sem("const_loaded"), sem("consts_made")
        w_loaded = [sem("w_loaded0"), sem("w_loaded1")]
        w_hi, w_lo, chunk_done = sem("w_hi"), sem("w_lo"), sem("chunk_done")
        chain_sem = sem("dve_chain")
        x_tr = sem("x_transposed")
        meta_in = sem("meta_in")
        dist_iota, dist_abs, dist_ready = sem("dist_iota"), sem("dist_abs"), sem("dist_ready")
        late_loaded = sem("late_loaded")
        sp_paced = sem("sp_paced")
        norms = [{k: sem(f"{k}_{n}") for k in ("h_ready", "sq_ready", "xh_ready", "sum_ready", "xl_ready",
                                               "ssq_mm", "var_ready", "rcol_ready", "diag_ready",
                                               "bcast_mm", "rstd_ready")} for n in range(4)]
        ups = [{k: sem(f"{k}_{n}") for k in ("gate_mm", "gate_scaled", "silu_done", "up_scaled",
                                             "gg_ready", "gh_ready", "gl_ready")} for n in (1, 2)]
        out_mm = sem("out_mm")
        u_mm, u_ready = sem("u_mm"), sem("u_ready")
        lam_tr, lam_ev, prep_done = sem("lam_tr"), sem("lam_ev"), sem("prep_done")
        act_small, act_small_done = sem("act_small"), sem("act_small_done")
        lam_dt = sem("lam_dt")
        u_out, y_out = sem("u_out"), sem("y_out")
        (ssm_in, ct_mm, ct_ev, kernels_ready, krow_mm, krow_ev, w1t_ready, w1t_mm, w1_ev, toep_in, u_in,
         sin_mm, sin_ev, sx_ready, y_mm, y_ev, y_in, gelu_arg, gelu_exp, z_ready) = (sem(n) for n in (
            "ssm_in", "ct_mm", "ct_ev", "kernels_ready", "krow_mm", "krow_ev", "w1t_ready", "w1t_mm", "w1_ev",
            "toep_in", "u_in", "sin_mm", "sin_ev", "sx_ready", "y_mm", "y_ev", "y_in", "gelu_arg",
            "gelu_exp", "z_ready"))
        (proj_mm, proj_ev, s_mm, sc_done, negm_ready, exp_done, p_ready, t_mm, pt_act, pt_dve, pv_mm,
         yah_ready, yal_ready) = (sem(n) for n in (
            "proj_mm", "proj_ev", "s_mm", "sc_done", "negm_ready", "exp_done", "p_ready", "t_mm", "pt_act",
            "pt_dve", "pv_mm", "yah_ready", "yal_ready"))
        zh_ready, zl_ready, glu_mm, glu_sig, ysf_ready, ysh_ready, ysl_ready = (sem(n) for n in (
            "zh_ready", "zl_ready", "glu_mm", "glu_sig", "ysf_ready", "ysh_ready", "ysl_ready"))
        gates_mm, branch_mm, gates_scaled, gates_sig, mg_ready, mgh_ready, mgl_ready = (sem(n) for n in (
            "gates_mm", "branch_mm", "gates_scaled", "gates_sig", "mg_ready", "mgh_ready", "mgl_ready"))
        hg_ready, fin_mm, fin_act, fin_dve, stored = (sem(n) for n in (
            "hg_ready", "fin_mm", "fin_act", "fin_dve", "stored"))

        block = ctx.enter_context(nc.Block())

        def halves(base_bank, wide):
            if wide:
                return [(PS[:, base_bank + a, 0:HALF], slice(a * HALF, (a + 1) * HALF)) for a in (0, 1)]
            return [(PS[:, base_bank, 0:SEQ], slice(META, T))]

        def psum_of(bank, wide):
            return PS[:, bank:bank + 2, 0:HALF] if wide else PS[:, bank, 0:SEQ]

        def tokens(row, wide):
            return row.rearrange("p (a n) -> p a n", a=2) if wide else row[:, META:T]

        @block.sync
        def _(sp):
            def weight_chunk(c, parts, settle=False):
                sp.wait_ge(w_lo, c.plus(OPEN - 1))
                if settle:
                    sp.sem_inc(sp_paced, 1)
                for n, (dst, src) in enumerate(parts):
                    inc = 16 if n + 1 < len(parts) else LOAD - 16 * n
                    sp.dma_start(dst, src).then_inc(w_loaded[c.slot], inc)

            def kview(w):
                return w.rearrange("(k p) n -> p k n", p=P)

            def tiles_of(c, t0, w, col):
                nk = w.shape[0] // P
                return wraw[:, c.slot, t0:t0 + nk, :], kview(w)[:, :, ds(col, P)]

            def ffn_stream(c_up, c_down, wg, wu, wd):
                with sp.Fori(0, KF // 2) as i:
                    for j in (0, 1):
                        c, col = At(c_up + j, i, 2), i * (2 * P) + j * P
                        weight_chunk(c, [tiles_of(c, 0, wg, col), tiles_of(c, KD, wu, col)])
                with sp.Fori(0, KD // 2) as i:
                    for j in range(4):
                        c = At(c_down + j, i, 4)
                        k0 = (j % 2) * (KF // 2)
                        src = kview(wd)[:, k0:k0 + KF // 2, ds(i * (2 * P) + (j // 2) * P, P)]
                        weight_chunk(c, [(wraw[:, c.slot, 0:6, :], src[:, 0:6, :]),
                                         (wraw[:, c.slot, 6:11, :], src[:, 6:11, :])])

            sp.dma_start(m_nat[:], meta_tokens).then_inc(x_loaded, 16)
            sp.dma_start(x_nat[:], x[0].rearrange("(t p) n -> p t n", p=P)).then_inc(x_loaded, 16)
            ffn_stream(C_UP1, C_DOWN1, ffn1_w_gate[0], ffn1_w_up[0], ffn1_w_down[0])
            win = w_in[0]
            for j in range(KS // 2):
                c, col = At(C_U + j), COL_U + 2 * j * P
                weight_chunk(c, [tiles_of(c, 0, win, col), tiles_of(c, KD, win, col + P)])

            sp.wait_ge(u_ready, KS)
            sp.dma_start(u_dram.rearrange("b g c s k -> (g c) b (s k)"),
                         uT[:].rearrange("p b s k -> p b (s k)")).then_inc(u_out, 16)
            with sp.Fori(0, KS) as i:
                sp.wait_ge(kernels_ready, i + 1)
                for ri, c_par in enumerate((ssm_c_re, ssm_c_im)):
                    for dr in (0, 1):
                        sp.dma_start(c_raw[:, ri, dr * STATE:(dr + 1) * STATE],
                                     c_par[0, dr].rearrange("g c p -> (g c) p")[ds(i * P, P), :]
                                     ).then_inc(ssm_in, 16)
                for ri, b_par in enumerate((ssm_b_re, ssm_b_im)):
                    for dr in (0, 1):
                        sp.dma_start(b_raw[dr * STATE:(dr + 1) * STATE, ri],
                                     b_par[0, dr].rearrange("g p c -> p g c")[:, ds(i * GB, GB), :]
                                     ).then_inc(ssm_in, 16)
                sp.wait_ge(y_mm, i + 1)
                sp.wait_ge(u_out, 16)
                for s in range(CHUNK):
                    sp.dma_start(U[s * CH:(s + 1) * CH, :, :],
                                 u_dram[ds(i, 1)].rearrange("o g c s k -> s c (o g) k")[s]).then_inc(u_in, 16)
                sp.wait_ge(krow_ev, i * 5 + 5)
                for s in range(CHUNK):
                    c0 = (CHUNK - 1 - s) * CH
                    sp.dma_start(toep[s * CH:(s + 1) * CH, :, :], krow[:, :, c0:c0 + P]).then_inc(toep_in, 16)
                sp.wait_ge(y_ev, i + 2)
                sp.dma_start(y_dram[ds(i, 1)].rearrange("o t c g k -> (o t c) (g k)"),
                             Y[:].rearrange("p g k -> p (g k)")).then_inc(y_out, 16)
                sp.wait_ge(y_out, i * 16 + 16)
                sp.wait_ge(z_ready, i + 1)
                for g in range(GB):
                    sp.dma_start(yT[g * CH:(g + 1) * CH, :].rearrange("c (t k) -> c t k", t=CHUNK),
                                 y_dram[ds(i, 1)].rearrange("o t c g k -> g c (o t) k")[g]).then_inc(y_in, 16)

            with sp.Fori(0, 2) as a:
                q_col = sp.snap(a * (2 * QG * DH))
                for j, col in enumerate((COL_K, COL_V)):
                    c = At(C_ATT + j, a, 4)
                    weight_chunk(c, [tiles_of(c, 0, win, a * P + col)])
                for j in (0, 1):
                    c = At(C_ATT + 2 + j, a, 4)
                    weight_chunk(c, [
                        (wraw[:, c.slot, t * KD:(t + 1) * KD, b * DH:(b + 1) * DH],
                         kview(win)[:, :, ds(q_col + (b * QG + 2 * j + t) * DH, DH)])
                        for t in (0, 1) for b in (0, 1)])

            c = At(C_GLU)
            weight_chunk(c, [(wraw[:, c.slot, m * KS:(m + 1) * KS, :],
                              kview(ssm_w_glu[0])[:, :, m * P:(m + 1) * P]) for m in range(KS)])
            with sp.Fori(0, KD // 2) as i:
                col_end = sp.snap(i * (2 * P) + 2 * P)
                for j in (0, 1):
                    col = col_end + (j - 2) * P
                    c = At(C_MERGE + 2 * j, i, 4)
                    weight_chunk(c, [tiles_of(c, 0, win, col + COL_GS), tiles_of(c, KD, win, col + COL_GA)])
                    c = At(C_MERGE + 2 * j + 1, i, 4)
                    wa = w_branch_attn[0].rearrange("(a b r d) n -> a b d r n", a=2, b=2, r=QG)
                    weight_chunk(c, [tiles_of(c, 0, w_branch_ssm[0], col)] + [
                        (wraw[b * DH:(b + 1) * DH, c.slot, KS + a * QG:KS + (a + 1) * QG, :],
                         wa[a, b][:, :, ds(col, P)]) for a in (0, 1) for b in (0, 1)], settle=True)
            with sp.Fori(0, KD // 4) as i:
                for j in (0, 1):
                    c, col = At(C_OUT + j, i, 2), i * (4 * P) + j * 2 * P
                    weight_chunk(c, [tiles_of(c, 0, w_out[0], col), tiles_of(c, KD, w_out[0], col + P)])
            ffn_stream(C_UP2, C_DOWN2, ffn2_w_gate[0], ffn2_w_up[0], ffn2_w_down[0])

            for t in range(4):
                sp.wait_ge(fin_act, t + 1)
                sp.wait_ge(fin_dve, t + 1)
                sp.dma_start(out[0, t * P:(t + 1) * P, :], y_nat[:, t, :]).then_inc(stored, 16)
            sp.wait_ge(stored, 64)

        @block.gpsimd
        def _(pool):
            pool.memset(ident[:], 0.0).then_inc(consts_made, 1)
            pool.memset(ones[:], 1.0).then_inc(consts_made, 1)
            pool.memset(expo[:], -0.5).then_inc(consts_made, 1)
            pool.wait_ge(consts_made, 3)
            pool.affine_select(out=ident[:], in_=ident[:], compare_op=ALU.not_equal, fill=1.0, base=0,
                               pattern=[[-1, P]], channel_multiplier=1).then_inc(consts_made, 1)

            def token_rstd(n):
                pool.wait_ge(norms[n]["var_ready"], 1)
                pool.tensor_tensor(rcol[:], var[:], expo[:].to_broadcast([P, 5]), ALU.pow
                                   ).then_inc(norms[n]["rcol_ready"], 1)

            token_rstd(0)
            token_rstd(1)
            pool.wait_ge(z_ready, KS + 1)
            for h in range(HEADS):
                pool.memset(negslope[:, h:h + 1], -float(np.float32(2.0 ** (-8.0 * (h + 1) / HEADS))))
            pool.memset(dist[:, 0:META], 0.0)
            pool.memset(dist0[:, 0:META], 0.0)
            band, band0 = dist[:, META:], dist0[:, META:]
            pool.iota(band, pattern=[[-1, 3 * WINDOW]], base=WINDOW, channel_multiplier=1,
                      allow_small_or_imprecise_dtypes=True)
            pool.iota(band0, pattern=[[-1, 2 * WINDOW]], base=0, channel_multiplier=1,
                      allow_small_or_imprecise_dtypes=True).then_inc(dist_iota, 1)
            pool.wait_ge(dist_abs, 1)
            pool.affine_select(out=band, in_=band, compare_op=ALU.is_ge, fill=FAR, base=0,
                               pattern=[[1, 3 * WINDOW]], channel_multiplier=-1).then_inc(dist_iota, 1)
            pool.wait_ge(dist_iota, 2)
            pool.affine_select(out=band, in_=band, compare_op=ALU.is_ge, fill=FAR, base=2 * WINDOW,
                               pattern=[[-1, 3 * WINDOW]], channel_multiplier=1)
            pool.affine_select(out=band0, in_=band0, compare_op=ALU.is_ge, fill=FAR, base=WINDOW,
                               pattern=[[-1, 2 * WINDOW]], channel_multiplier=1).then_inc(dist_ready, 1)
            token_rstd(2)
            token_rstd(3)

        @block.tensor
        def _(pe):
            def passes(bank, wide, c, t0, nk, hi, lo, k0, first, last, wait_k=None):
                outs = halves(bank, wide)
                for k in range(nk):
                    if wait_k is not None:
                        pe.wait_ge(wait_k, k + 1)
                    todo = ((wh, hi), (wh, lo), (wl, hi))
                    for n, (w, xt) in enumerate(todo):
                        for ps, tok in outs:
                            if xt.shape[-1] == SEQ:
                                tok = slice(0, SEQ)
                            ins = pe.matmul(ps, w[:, c.slot, t0 + k, :], xt[:, k0 + k, tok],
                                            start=first and k == 0 and n == 0,
                                            stop=last and k == nk - 1 and n == 2)
                return ins

            def chunk_ready(c):
                pe.wait_ge(w_hi, c.plus(1))
                pe.wait_ge(w_lo, c.plus(1 + OPEN))

            def sum_squares(n):
                s = norms[n]
                pe.wait_ge(s["sum_ready"], KD + 1)
                for t in range(5):
                    t0 = 0 if t == 0 else META + (t - 1) * P
                    ins = pe.matmul(PS[:, 4, t:t + 1], ssum[:, t0:t0 + P], ones[:, 0:1], start=True, stop=True)
                ins.then_inc(s["ssq_mm"], 1)

            def spread_rstd(n):
                s = norms[n]
                pe.wait_ge(s["diag_ready"], 1)
                pe.matmul(PS[:, 6, 0:META], ones[0:META, :], diag[0:META, 0, 0:META], start=True, stop=True)
                for t in range(1, 5):
                    o = PS[:, 6, META + (t - 1) * P:META + t * P] if t < 3 else PS[:, 7, (t - 3) * P:(t - 2) * P]
                    ins = pe.matmul(o, ones[:], diag[:, t, :], start=True, stop=True)
                ins.then_inc(s["bcast_mm"], 1)

            def up_chunk(c, n, f, wide, with_norm):
                s = ups[n]
                chunk_ready(c)
                b = f.base % 2
                gate_bank, up_bank = (4 * b, 4 * b + 2) if wide else (2 * b, 2 * b + 1)
                pe.wait_ge(s["gate_scaled"], f.plus(OPEN - 1))
                passes(gate_bank, wide, c, 0, KD, xh, xl, 0, True, True,
                       norms[2 * n]["xl_ready"] if with_norm else None).then_inc(s["gate_mm"], 1)
                if with_norm:
                    sum_squares(2 * n)
                pe.wait_ge(s["up_scaled"], f.plus(OPEN - 1))
                passes(up_bank, wide, c, KD, KD, xh, xl, 0, True, True).then_inc(chunk_done, 1)
                if with_norm:
                    spread_rstd(2 * n)
                    pe.wait_ge(norms[2 * n]["rstd_ready"], 1)

            def ffn(n, c_up, c_down, wide):
                s, g = ups[n], ffn_mem[n]
                for j in (0, 1):
                    up_chunk(At(c_up + j), n, At(j), wide, j == 0)
                with pe.Fori(1, KF // 2) as i:
                    for j in (0, 1):
                        up_chunk(At(c_up + j, i, 2), n, At(j, i, 2), wide, False)
                pe.wait_ge(s["gate_scaled"], KF + OPEN)
                pe.wait_ge(s["up_scaled"], KF + OPEN)
                with pe.Fori(0, KD // 2) as i:
                    for m in (0, 1):
                        pe.wait_ge(norms[2 * n + 1]["h_ready"], At(m, i, 2).plus(OPEN - 1))
                        for h in (0, 1):
                            c = At(c_down + 2 * m + h, i, 4)
                            chunk_ready(c)
                            pe.wait_ge(s["gl_ready"], KF if h else KF // 2)
                            passes(4 * m, wide, c, 0, KF // 2, g["gh"], g["gl"], h * (KF // 2),
                                   h == 0, h == 1).then_inc(chunk_done, 1)

            pe.sem_inc(chunk_done, OPEN)
            pe.sem_inc(y_mm, 1)
            pe.sem_inc(pv_mm, OPEN)

            pe.wait_ge(consts_made, 4)
            pe.wait_ge(x_loaded, 32)
            for k in range(KD):
                ins = pe.transpose(PS[:, 0, k * META:(k + 1) * META], m_nat[:, k * P:(k + 1) * P],
                                   ident[0:META, 0:META])
            ins.then_inc(x_tr, 1)
            for k in range(KD):
                if k == KD - 1:
                    pe.wait_ge(meta_in, 1)
                for t in range(4):
                    ins = pe.transpose(PS[:, (k + 1) % 8, t * P:(t + 1) * P],
                                       x_nat[:, t, k * P:(k + 1) * P], ident[:])
                ins.then_inc(x_tr, 1)
            pe.wait_ge(norms[0]["h_ready"], KD + OPEN)

            ffn(0, C_UP1, C_DOWN1, True)

            pe.wait_ge(norms[1]["h_ready"], KD - 1 + OPEN)
            for j in range(KS // 2):
                c = At(C_U + j)
                chunk_ready(c)
                for t in (0, 1):
                    bt = 2 * j + t
                    ins = passes(2 * bt, True, c, t * KD, KD, xh, xl, 0, True, True,
                                 norms[1]["xl_ready"] if bt == 0 else None)
                    ins.then_inc(chunk_done if t else u_mm, 1)
                    if bt == 0:
                        sum_squares(1)
                    if bt == 1:
                        spread_rstd(1)
                        pe.wait_ge(norms[1]["rstd_ready"], 1)

            pe.wait_ge(u_ready, 1)
            pe.wait_ge(late_loaded, 48)
            pe.wait_ge(lam_dt, 1)
            for q in range(3):
                ins = pe.transpose(PS[:, 0, q * GROUPS:(q + 1) * GROUPS],
                                   lam_raw[:, q].rearrange("g d p -> g (d p)"), ident[0:GROUPS, 0:GROUPS])
            ins.then_inc(lam_tr, 1)
            pe.wait_ge(prep_done, 1)
            pe.wait_ge(u_ready, KS)
            with pe.Fori(0, KS) as i:
                pe.wait_ge(ssm_in, i * 128 + 128)
                pe.wait_ge(y_ev, i + 1)
                for ri in (0, 1):
                    ins = pe.transpose(PS[:, 0, ri * P:(ri + 1) * P], c_raw[:, ri, :], ident[:])
                ins.then_inc(ct_mm, 1)
                pe.wait_ge(kernels_ready, i + 2)
                F, B = slice(0, STATE), slice(STATE, P)
                for g in range(GB):
                    for q, ri in ((0, 0), (2, 1)):
                        pe.matmul(PS[0:CH, 1, g * CH:(g + 1) * CH], bb[:, q, g, :], cT[:, ri, g * CH:(g + 1) * CH],
                                  start=ri == 0, stop=ri == 1)
                    for bank, part, i0 in ((4 + g // 4, B, 1), (6 + g // 4, F, 0)):
                        o = PS[0:CH, bank, (g % 4) * 7 * CH:(g % 4 + 1) * 7 * CH]
                        for q, ri in ((0, 0), (2, 1)):
                            ins = pe.matmul(o, bb[part, q, g, :],
                                            cp[part, ri, g, i0:i0 + 7, :].rearrange("p i c -> p (i c)"),
                                            start=ri == 0, stop=ri == 1)
                ins.then_inc(krow_mm, 1)
                pe.wait_ge(krow_ev, i * 5 + 1)
                for ri in (0, 1):
                    for g in range(GB):
                        ins = pe.transpose(PS[:, 2 * ri + g // 4, (g % 4) * P:(g % 4 + 1) * P],
                                           w1t[:, ri, g].rearrange("p s c -> p (s c)"), ident[:])
                ins.then_inc(w1t_mm, 1)
                pe.wait_ge(krow_ev, i * 5 + 5)
                pe.wait_ge(w1_ev, i * 2 + 2)
                pe.wait_ge(u_in, i * 128 + 128)
                for ri in (0, 1):
                    for g in range(GB):
                        ins = pe.matmul(PS[:, 4 + 2 * ri + g // 4, (g % 4) * NCH:(g % 4 + 1) * NCH],
                                        w1[:, ri, g, :], U[:, g, :], start=True, stop=True)
                ins.then_inc(sin_mm, 1)
                pe.wait_ge(toep_in, i * 128 + 128)
                pe.wait_ge(sx_ready, i + 1)
                for g in range(GB):
                    o = PS[:, 0, g * OCH:(g + 1) * OCH]
                    pe.matmul(o, toep[:, g, :], U[:, g, MCH:NCH], start=True, stop=False)
                    for ri in (0, 1):
                        ins = pe.matmul(o, cp[:, ri, g].rearrange("p i c -> p (i c)"), sx[:, ri, g, :],
                                        start=False, stop=ri == 1)
                ins.then_inc(y_mm, 1)

            groups = [(n, b) for n in range(NBLK) for b in (0, 1)]
            pe.wait_ge(y_ev, KS + 1)
            with pe.Fori(0, 2) as a:
                pe.wait_ge(yah_ready, a * 4 + OPEN)
                pe.wait_ge(yal_ready, a * 4 + OPEN)
                c = At(C_ATT, a, 4)
                chunk_ready(c)
                passes(0, True, c, 0, KD, xh, xl, 0, True, True).then_inc(chunk_done, 1)
                c = At(C_ATT + 1, a, 4)
                chunk_ready(c)
                for t in range(5):
                    t0 = 0 if t == 0 else META + (t - 1) * P
                    o = PS[:, 2 + t // 4, (t % 4) * P:(t % 4 + 1) * P]
                    for k in range(KD):
                        for q, (xt, w) in enumerate(((xh, wh), (xh, wl), (xl, wh))):
                            ins = pe.matmul(o, xt[:, k, t0:t0 + P], w[:, c.slot, k, :],
                                            start=k == 0 and q == 0, stop=k == KD - 1 and q == 2)
                ins.then_inc(chunk_done, 1)
                for r in range(QG):
                    c = At(C_ATT + 2 + r // 2, a, 4)
                    if r % 2 == 0:
                        chunk_ready(c)
                        pe.wait_ge(proj_ev, a * 6 + 1 + r // 2)
                    passes(r, False, c, (r % 2) * KD, KD, xh, xl, 0, True, True
                           ).then_inc(chunk_done if r % 2 else proj_mm, 1)

                def scores(gi):
                    n, b = groups[gi]
                    part = slice(b * DH, (b + 1) * DH)
                    for r in range(QG):
                        pe.wait_ge(sc_done, a * 32 + (4 * gi + r - 1 + OPEN))
                        q = qT[part, r, n * P:(n + 1) * P]
                        if n < 2:
                            ranges = [(0, META + (n + 2) * P)]
                        else:
                            ranges = [(0, META), (META + (n - 1) * P, min(T, META + (n + 2) * P))]
                        col = 0
                        for lo, hi in ranges:
                            ins = pe.matmul(PS[:, 4 + r % 2, col:col + hi - lo], q, kT[part, lo:hi],
                                            start=True, stop=True)
                            col += hi - lo
                        ins.then_inc(s_mm, 1)

                def transposes(gi):
                    n, b = groups[gi]
                    nb = 2 if n in (0, NBLK - 1) else 3
                    pe.wait_ge(p_ready, a * 8 + gi + 1)
                    for r in range(QG):
                        if r % 2 == 0:
                            pe.wait_ge(pt_act, a * 16 + (2 * gi + r // 2 + 1))
                        if r != 2:
                            pe.wait_ge(pt_dve, a * 24 + (3 * gi + r // 2 + 1))
                        for j in range(nb):
                            pe.transpose(PS[:, 6 + r % 2, j * P:(j + 1) * P],
                                         sc[:, gi % 2, r, META + j * P:META + (j + 1) * P], ident[:])
                        pe.transpose(PS[0:META, 2, r * P:(r + 1) * P], sc[:, gi % 2, r, 0:META], ident[:]
                                     ).then_inc(t_mm, 1)

                def values(gi):
                    n, b = groups[gi]
                    nb = 2 if n in (0, NBLK - 1) else 3
                    kb = max(n - 1, 0)
                    pe.wait_ge(pt_act, a * 16 + (2 * gi + 3))
                    pe.wait_ge(pt_dve, a * 24 + (3 * gi + 4))
                    bank = 0 if n % 2 else 3
                    if b == 0:
                        pe.wait_ge(yah_ready, a * 4 + (n - 1 + OPEN))
                        pe.wait_ge(yal_ready, a * 4 + (n - 1 + OPEN))
                    o = PS[b * DH:(b + 1) * DH, bank, :]
                    for j in range(nb):
                        pe.matmul(o, vt[:, 1 + kb + j, b * DH:(b + 1) * DH],
                                  pt[:, gi % 2, j].rearrange("p r q -> p (r q)"), start=j == 0, stop=False)
                    pe.matmul(o, vt[0:META, 0, b * DH:(b + 1) * DH],
                              ptm[:, gi % 2].rearrange("p r q -> p (r q)"), start=False, stop=True
                              ).then_inc(pv_mm, 1)

                pe.wait_ge(proj_ev, a * 6 + 6)
                for gi in range(9):
                    if gi < 8:
                        scores(gi)
                    if gi > 0:
                        transposes(gi - 1)
                        values(gi - 1)

            c = At(C_GLU)
            chunk_ready(c)
            pe.wait_ge(yah_ready, 8 + OPEN)
            pe.wait_ge(yal_ready, 8 + OPEN)
            for m in range(KS):
                ins = passes(m, False, c, m * KS, KS, zh, zl, 0, True, True, zl_ready if m == 0 else None)
            ins.then_inc(chunk_done, 1)

            pe.wait_ge(ysh_ready, KS)
            with pe.Fori(0, KD // 2) as i:
                for j in (0, 1):
                    pe.wait_ge(mg_ready, At(j, i, 2).plus(OPEN - 1))
                    c = At(C_MERGE + 2 * j, i, 4)
                    chunk_ready(c)
                    passes(4 * j, False, c, 0, KD, xh, xl, 0, True, True)
                    passes(4 * j + 1, False, c, KD, KD, xh, xl, 0, True, True).then_inc(chunk_done, 1)
                    c = At(C_MERGE + 2 * j + 1, i, 4)
                    chunk_ready(c)
                    pe.wait_ge(ysl_ready, KS)
                    passes(4 * j + 2, False, c, 0, KS, ysh, ysl, 0, True, True)
                    passes(4 * j + 3, False, c, KS, KD, yah, yal, 0, True, True).then_inc(chunk_done, 1)

            pe.wait_ge(mgl_ready, KD)
            with pe.Fori(0, KD // 4) as i:
                for j in (0, 1):
                    c = At(C_OUT + j, i, 2)
                    chunk_ready(c)
                    for t in (0, 1):
                        m = At(2 * j + t, i, 4)
                        pe.wait_ge(norms[2]["h_ready"], m.plus(OPEN - 1))
                        passes(2 * j + t, False, c, t * KD, KD, mgh, mgl, 0, True, True
                               ).then_inc(chunk_done if t else out_mm, 1)
            pe.wait_ge(norms[2]["h_ready"], KD + OPEN)

            ffn(1, C_UP2, C_DOWN2, False)

            pe.wait_ge(norms[3]["h_ready"], KD + OPEN)
            for m in range(KD):
                pe.wait_ge(norms[3]["xh_ready"], m + 1)
                if m == KD - 1:
                    pe.wait_ge(norms[3]["sum_ready"], KD + 1)
                    for t in range(5):
                        t0 = 0 if t == 0 else META + (t - 1) * P
                        ins = pe.matmul(PS[:, 7, 3 * P + t:3 * P + t + 1], ssum[:, t0:t0 + P], ones[:, 0:1],
                                        start=True, stop=True)
                    ins.then_inc(norms[3]["ssq_mm"], 1)
                for t in range(4):
                    if m == KD - 1 and t == 3:
                        pe.wait_ge(norms[3]["var_ready"], 1)
                    ins = pe.transpose(PS[:, 2 * t + m // 4, (m % 4) * P:(m % 4 + 1) * P],
                                       hg[:, m, t * P:(t + 1) * P], ident[:])
                    if m == KD - 1:
                        ins.then_inc(fin_mm, 1)

        @block.scalar
        def _(act):
            def split_hi(c):
                act.wait_ge(w_loaded[c.slot], c.loads())
                act.wait_ge(chunk_done, c.plus(OPEN - 1))
                act.activation(wh[:, c.slot], wraw[:, c.slot], ACT.Copy).then_inc(w_hi, 1)

            def norm_step(n, m, wide):
                s = norms[n]
                cols = slice(0, T) if wide else slice(META, T)
                mm = m.plus(0)
                h = hT[:, ds(mm, 1), cols].rearrange("p o n -> p (o n)")
                act.wait_ge(s["h_ready"], m.plus(1 + OPEN))
                act.wait_ge(s["sum_ready"], m.plus(1))
                act.activation(sq[:, cols], h, ACT.Square).then_inc(s["sq_ready"], 1)
                gain = gains[:, n, ds(mm, 1)]
                if n < 3:
                    o = xh[:, ds(mm, 1), cols].rearrange("p o n -> p (o n)")
                else:
                    o = hg[:, ds(mm, 1), :].rearrange("p o n -> p (o n)")
                act.activation(o, h, ACT.Copy, scale=gain).then_inc(s["xh_ready"], 1)

            def rstd_out(n):
                act.wait_ge(norms[n]["bcast_mm"], 1)
                act.activation(rstd_b[:, 0:META + 2 * P], PS[:, 6, 0:META + 2 * P], ACT.Copy)
                act.activation(rstd_b[:, META + 2 * P:T], PS[:, 7, 0:2 * P], ACT.Copy
                               ).then_inc(norms[n]["rstd_ready"], 1)

            def ffn(n, c_up, c_down, wide):
                s, g = ups[n], ffn_mem[n]
                w = T if wide else SEQ

                def up_step(c, f, with_norm):
                    b = f.base % 2
                    split_hi(c.at(1))
                    if with_norm:
                        rstd_out(2 * n)
                    act.wait_ge(s["gate_scaled"], f.plus(1 + OPEN))
                    t1 = g["t1"][:, b, 0:w]
                    act.activation(t1, t1, ACT.Silu).then_inc(s["silu_done"], 1)
                    act.wait_ge(s["gg_ready"], f.plus(1))
                    act.activation(g["gh"][:, ds(f.plus(0), 1), :].rearrange("p o n -> p (o n)"),
                                   g["t2"][:, b, 0:w], ACT.Copy).then_inc(s["gh_ready"], 1)

                for j in (0, 1):
                    up_step(At(c_up + j), At(j), j == 0)
                with act.Fori(1, KF // 2) as i:
                    for j in (0, 1):
                        up_step(At(c_up + j, i, 2), At(j, i, 2), False)

                def down_steps(i):
                    for j in range(4):
                        last = i is None and j == 3 and n == 1
                        c, m = at_end(c_down, KD // 2, 4, j, i), at_end(0, KD // 2, 2, j // 2, i)
                        if not last:
                            split_hi(c.at(1))
                        if j % 2:
                            norm_step(2 * n + 1, m, wide)

                with act.Fori(0, KD // 2 - 1) as i:
                    down_steps(i)
                down_steps(None)

            with nc.allow_non_contiguous_dma("gains, a few KB"):
                for n, g in enumerate((ffn1_norm[0], mix_norm[0], ffn2_norm[0], final_norm)):
                    act.dma_start(gains[:, n, :], g.rearrange("(k p) -> p k", p=P)).then_inc(const_loaded, 16)
                act.dma_start(dskip[:], ssm_d[0].rearrange("(k p) -> p k", p=P)).then_inc(const_loaded, 16)
            act.wait_ge(const_loaded, 80)

            for k in range(KD):
                norm_step(0, At(k), True)
                if k == 1:
                    split_hi(At(0))
            ffn(0, C_UP1, C_DOWN1, True)

            act.wait_ge(chunk_done, C_U + OPEN)
            for q, lam in enumerate((ssm_lam_re, ssm_lam_im)):
                act.dma_start(lam_raw[:, q], lam[0].rearrange("d g p -> g d p")).then_inc(late_loaded, 16)
            with nc.allow_non_contiguous_dma("64 numbers"):
                act.dma_start(dt_raw[:], ssm_log_dt[0].rearrange("d g -> g d")).then_inc(late_loaded, 16)
            split_hi(At(C_U + 1))
            rstd_out(1)
            act.wait_ge(act_small, 1)
            act.activation(prm[:, 2], prm[:, 2], ACT.Exp).then_inc(act_small_done, 1)
            act.wait_ge(act_small, 2)
            act.activation(tiny[:, EXPA], tiny[:, A_], ACT.Exp)
            act.activation(tiny[:, SINH], tiny[:, RH], ACT.Sin)
            act.activation(tiny[:, SINR], tiny[:, R_], ACT.Sin).then_inc(act_small_done, 1)

            act.sem_inc(y_ev, 1)
            act.sem_inc(pt_act, 1)
            act.sem_inc(yah_ready, OPEN)
            with act.Fori(0, KS) as i:
                act.wait_ge(ct_mm, i + 1)
                act.activation(cT[:].rearrange("p a n -> p (a n)"), PS[:, 0, 0:2 * P], ACT.Copy).then_inc(ct_ev, 1)
                act.wait_ge(krow_mm, i + 1)
                act.activation(krow[:, :, 7 * CH:8 * CH], PS[0:CH, 1, 0:P].rearrange("p (g n) -> p g n", g=GB),
                               ACT.Copy).then_inc(krow_ev, 1)
                for q in range(4):
                    lag0 = 0 if q < 2 else 8
                    act.activation(krow[:, 4 * (q % 2):4 * (q % 2) + 4, lag0 * CH:(lag0 + 7) * CH],
                                   PS[0:CH, 4 + q, 0:28 * CH].rearrange("p (g n) -> p g n", g=4), ACT.Copy
                                   ).then_inc(krow_ev, 1)
                act.wait_ge(w1t_mm, i + 1)
                for ri in (0, 1):
                    act.activation(w1[:, ri].rearrange("p (a g) n -> p a (g n)", a=2),
                                   PS[:, 2 * ri:2 * ri + 2, :], ACT.Copy).then_inc(w1_ev, 1)
                act.wait_ge(sin_mm, i + 1)
                for ri in (0, 1):
                    for half in (0, 1):
                        part = slice(half * STATE, (half + 1) * STATE)
                        o = sin_[part, ri, :, ::-1] if half else sin_[part, ri]
                        for q in (0, 1):
                            act.activation(o[:, 4 * q:4 * q + 4, :],
                                           PS[part, 4 + 2 * ri + q, 0:4 * NCH].rearrange("p (g k) -> p g k", g=4),
                                           ACT.Copy).then_inc(sin_ev, 1)
                act.wait_ge(y_mm, i + 2)
                act.activation(Y[:].rearrange("p g k -> p (g k)"), PS[:, 0, :], ACT.Copy).then_inc(y_ev, 1)
                act.wait_ge(gelu_arg, i + 1)
                arg = tb[:, 0, 0:SEQ]
                act.activation(arg, arg, ACT.Sigmoid, scale=2.0 * math.sqrt(2.0 / math.pi)).then_inc(gelu_exp, 1)

            act.wait_ge(z_ready, KS + 1)
            act.dma_start(negsink[:], attn_sink[0:1, :].to_broadcast([P, HEADS])).then_inc(late_loaded, 16)
            split_hi(At(C_ATT))
            groups = [(n, b) for n in range(NBLK) for b in (0, 1)]
            with act.Fori(0, 2) as a:
                for j in range(4):
                    split_hi(At(C_ATT + 1 + j, a, 4))

                def exps(gi):
                    n, b = groups[gi]
                    w = META + (2 if n in (0, NBLK - 1) else 3) * P
                    act.wait_ge(negm_ready, a * 8 + gi + 1)
                    for r in range(QG):
                        tile = sc[:, gi % 2, r, 0:w]
                        act.activation(tile, tile, ACT.Exp, bias=negm[:, gi % 2, r:r + 1],
                                       accum_out=rs[:, gi % 2, r:r + 1])
                    act.activation(sk[:, gi % 2], sk[:, gi % 2], ACT.Exp).then_inc(exp_done, 1)

                def prob_tiles(gi):
                    n, b = groups[gi]
                    nb = 2 if n in (0, NBLK - 1) else 3
                    act.wait_ge(pv_mm, a * 8 + gi + 1)
                    for r in (0, 2):
                        act.wait_ge(t_mm, a * 32 + (4 * gi + r + 1))
                        act.activation(pt[:, gi % 2, 0:nb, r, :],
                                       PS[:, 6, 0:nb * P].rearrange("p (j q) -> p j q", j=nb), ACT.Copy
                                       ).then_inc(pt_act, 1)

                def result(gi):
                    n, b = groups[gi]
                    act.wait_ge(pv_mm, a * 8 + gi + 1 + OPEN)
                    act.activation(yah[:, ds(a * 4, QG), n * P:(n + 1) * P],
                                   PS[:, 0 if n % 2 else 3, :].rearrange("p (r q) -> p r q", r=QG), ACT.Copy
                                   ).then_inc(yah_ready, 1)

                for gi in range(10):
                    if gi < 8:
                        exps(gi)
                    if 0 < gi < 9:
                        prob_tiles(gi - 1)
                    if gi > 1 and groups[gi - 2][1] == 1:
                        result(gi - 2)

            for bt in range(KS):
                act.activation(zh[:, bt], uT[:, bt].rearrange("p s k -> p (s k)")[:, 0:SEQ], ACT.Copy
                               ).then_inc(zh_ready, 1)
            split_hi(At(C_MERGE))
            act.wait_ge(chunk_done, At(C_GLU).plus(1 + OPEN))
            for m in range(KS):
                if m >= 2:
                    act.wait_ge(ysf_ready, m - 1)
                act.activation(sig[:, m % 2], PS[:, m, :], ACT.Sigmoid).then_inc(glu_sig, 1)
                act.wait_ge(ysf_ready, m + 1)
                act.activation(ysh[:, m], ysf[:, m % 2], ACT.Copy).then_inc(ysh_ready, 1)

            with act.Fori(0, KD // 2) as i:
                for j in (0, 1):
                    m = At(j, i, 2)
                    split_hi(At(C_MERGE + 2 * j + 1, i, 4))
                    act.wait_ge(gates_scaled, m.plus(1))
                    gg = gsig[:, j].rearrange("p a n -> p (a n)")
                    act.activation(gg, gg, ACT.Sigmoid).then_inc(gates_sig, 1)
                    split_hi(At(C_MERGE + 2 * j + 2, i, 4))
                    act.wait_ge(mg_ready, m.plus(1 + OPEN))
                    act.activation(mgh[:, ds(m.plus(0), 1), :].rearrange("p o n -> p (o n)"), gsig[:, j, 0],
                                   ACT.Copy).then_inc(mgh_ready, 1)
            with act.Fori(0, KD // 4) as i:
                for j in (0, 1):
                    split_hi(At(C_OUT + j + 1, i, 2))
                    for t in (0, 1):
                        norm_step(2, At(2 * j + t, i, 4), False)
            ffn(1, C_UP2, C_DOWN2, False)
            for t in range(4):
                act.wait_ge(norms[3]["rcol_ready"], 1)
                act.wait_ge(fin_mm, t + 1)
                act.activation(y_nat[:, t, 0:512], PS[:, 2 * t, :], ACT.Copy, scale=rcol[:, t + 1:t + 2]
                               ).then_inc(fin_act, 1)

        @block.vector
        def _(ve):
            link = Chain(ve, chain_sem)

            def as_f32(ap):
                return ap.bitcast(F32)

            def split_lo(c):
                ve.wait_ge(w_hi, c.plus(1))
                ve.tensor_tensor(wl[:, c.slot], wraw[:, c.slot], as_f32(wh[:, c.slot]), ALU.subtract
                                 ).then_inc(w_lo, 1)

            def norm_step(n, m, wide):
                s = norms[n]
                cols = slice(0, T) if wide else slice(META, T)
                mm = m.plus(0)
                ve.wait_ge(s["sq_ready"], m.plus(1))
                ve.wait_ge(s["sum_ready"], m.plus(1))
                ve.tensor_tensor(ssum[:, cols], ssum[:, cols], sq[:, cols], ALU.add).then_inc(s["sum_ready"], 1)
                if n < 3:
                    ve.wait_ge(s["xh_ready"], m.plus(1))
                    h = hT[:, ds(mm, 1), cols].rearrange("p o n -> p (o n)")
                    hi = xh[:, ds(mm, 1), cols].rearrange("p o n -> p (o n)")
                    lo = xl[:, ds(mm, 1), cols].rearrange("p o n -> p (o n)")
                    ve.scalar_tensor_tensor(out=lo, in0=h, scalar=gains[:, n, ds(mm, 1)], in1=as_f32(hi),
                                            op0=ALU.mult, op1=ALU.subtract).then_inc(s["xl_ready"], 1)

            def norm_start(n):
                ve.memset(ssum[:], 0.0).then_inc(norms[n]["sum_ready"], 1)
                ve.sem_inc(norms[n]["h_ready"], OPEN)

            def token_var(n):
                s = norms[n]
                ve.wait_ge(s["ssq_mm"], 1)
                src = PS[:, 4, 0:5] if n < 3 else PS[:, 7, 3 * P:3 * P + 5]
                ve.tensor_scalar(var[:], src, 1.0 / D, EPS, ALU.mult, ALU.add).then_inc(s["var_ready"], 1)

            def token_diag(n):
                s = norms[n]
                ve.wait_ge(s["rcol_ready"], 1)
                for t in range(5):
                    ins = ve.tensor_scalar(diag[:, t, :], ident[:], rcol[:, t:t + 1], None, ALU.mult)
                ins.then_inc(s["diag_ready"], 1)

            def ffn(n, c_up, c_down, wide):
                s, g = ups[n], ffn_mem[n]
                w = T if wide else SEQ

                def shaped(row):
                    return row.rearrange("p (a n) -> p a n", a=2) if wide else row

                rstd = shaped(rstd_b[:]) if wide else rstd_b[:, META:T]

                def up_step(c, f, with_norm):
                    b = f.base % 2
                    gate_bank, up_bank = (4 * b, 4 * b + 2) if wide else (2 * b, 2 * b + 1)
                    t1, t2 = g["t1"][:, b, 0:w], g["t2"][:, b, 0:w]
                    if with_norm:
                        token_var(2 * n)
                        token_diag(2 * n)
                    split_lo(c.at(1))
                    if with_norm:
                        ve.wait_ge(norms[2 * n]["rstd_ready"], 1)
                    ve.wait_ge(s["gate_mm"], f.plus(1))
                    ve.tensor_tensor(shaped(t1), psum_of(gate_bank, wide), rstd, ALU.mult
                                     ).then_inc(s["gate_scaled"], 1)
                    ve.wait_ge(chunk_done, c.plus(1 + OPEN))
                    ve.tensor_tensor(shaped(t2), psum_of(up_bank, wide), rstd, ALU.mult
                                     ).then_inc(s["up_scaled"], 1)
                    ve.wait_ge(s["up_scaled"], f.plus(1 + OPEN))
                    ve.wait_ge(s["silu_done"], f.plus(1))
                    ve.tensor_tensor(t2, t1, t2, ALU.mult).then_inc(s["gg_ready"], 1)
                    ve.wait_ge(s["gh_ready"], f.plus(1))
                    ff = f.plus(0)
                    ve.tensor_tensor(g["gl"][:, ds(ff, 1), :].rearrange("p o n -> p (o n)"), t2,
                                     as_f32(g["gh"][:, ds(ff, 1), :].rearrange("p o n -> p (o n)")),
                                     ALU.subtract).then_inc(s["gl_ready"], 1)

                ve.sem_inc(s["gate_scaled"], OPEN)
                ve.sem_inc(s["up_scaled"], OPEN)
                for j in (0, 1):
                    up_step(At(c_up + j), At(j), j == 0)
                with ve.Fori(1, KF // 2) as i:
                    for j in (0, 1):
                        up_step(At(c_up + j, i, 2), At(j, i, 2), False)
                norm_start(2 * n + 1)

                def down_steps(i):
                    for j in range(4):
                        last = i is None and j == 3 and n == 1
                        c, m = at_end(c_down, KD // 2, 4, j, i), at_end(0, KD // 2, 2, j // 2, i)
                        if not last:
                            split_lo(c.at(1))
                        if j % 2:
                            ve.wait_ge(chunk_done, c.plus(1 + OPEN))
                            row = hT[:, ds(m.plus(0), 1), :].rearrange("p o n -> p (o n)")
                            h = tokens(row, wide)
                            ve.scalar_tensor_tensor(out=h, in0=psum_of(4 * (j // 2), wide), scalar=0.5, in1=h,
                                                    op0=ALU.mult, op1=ALU.add
                                                    ).then_inc(norms[2 * n + 1]["h_ready"], 1)
                            norm_step(2 * n + 1, m, wide)

                with ve.Fori(0, KD // 2 - 1) as i:
                    down_steps(i)
                down_steps(None)

            ve.sem_inc(w_lo, OPEN)
            norm_start(0)
            ve.wait_ge(x_tr, 1)
            ve.tensor_copy(hT[:, :, 0:META], PS[:, 0, 0:KD * META].rearrange("p (k n) -> p k n", k=KD)
                           ).then_inc(meta_in, 1)
            ve.wait_ge(const_loaded, 80)
            for k in range(KD):
                ve.wait_ge(x_tr, k + 2)
                ve.tensor_copy(hT[:, k, META:T], PS[:, (k + 1) % 8, :]).then_inc(norms[0]["h_ready"], 1)
                if k > 0:
                    norm_step(0, At(k - 1), True)
                if k == 4:
                    split_lo(At(0))
            norm_step(0, At(KD - 1), True)
            ffn(0, C_UP1, C_DOWN1, True)

            token_var(1)
            split_lo(At(C_U + 1))
            token_diag(1)
            ve.wait_ge(norms[1]["rstd_ready"], 1)
            for bt in range(KS):
                if bt % 2:
                    ve.wait_ge(chunk_done, At(C_U + bt // 2).plus(1 + OPEN))
                else:
                    ve.wait_ge(u_mm, bt // 2 + 1)
                for hf in (0, 1):
                    ins = ve.tensor_tensor(
                        uT[:, bt, :, hf * (NCH // 2):(hf + 1) * (NCH // 2)].rearrange("p s k -> p k s"),
                        PS[:, 2 * bt + hf, 0:HALF].rearrange("p (k s) -> p k s", s=CHUNK),
                        rstd_b[:, hf * HALF:(hf + 1) * HALF].rearrange("p (k s) -> p k s", s=CHUNK), ALU.mult)
                ins.then_inc(u_ready, 1)

            ve.wait_ge(late_loaded, 48)
            ve.tensor_copy(lam_raw[:, 2], dt_raw[:].unsqueeze(2).to_broadcast([GROUPS, 2, STATE])
                           ).then_inc(lam_dt, 1)
            ve.memset(sx[:], 0.0)
            ve.wait_ge(lam_tr, 1)
            ve.tensor_copy(prm[:].rearrange("p q g -> p (q g)"), PS[:, 0, 0:3 * GROUPS]).then_inc(act_small, 1)
            lr, li, dt = prm[:, 0], prm[:, 1], prm[:, 2]
            c1, c2, c3 = split_two_pi()
            tn = lambda k: tiny[:, k]

            def tt(o, x0, x1, op):
                link(ve.tensor_tensor(o, x0, x1, op))

            def ts(o, x0, s1, op0, s2=None, op1=None):
                if op1 is None:
                    link(ve.tensor_scalar(o, x0, s1, None, op0))
                else:
                    link(ve.tensor_scalar(o, x0, s1, s2, op0, op1))

            def stt(o, x0, s, x1, op0, op1):
                link(ve.scalar_tensor_tensor(out=o, in0=x0, scalar=s, in1=x1, op0=op0, op1=op1))

            def cmul(o, x0, x1, tmp, conj=False):
                ve.tensor_tensor(o[0], x0[0], x1[0], ALU.mult)
                ve.tensor_tensor(tmp[0], x0[1], x1[1], ALU.mult)
                ve.tensor_tensor(o[1], x0[0], x1[1], ALU.mult)
                tt(tmp[1], x0[1], x1[0], ALU.mult)
                ve.tensor_tensor(o[0], o[0], tmp[0], ALU.add if conj else ALU.subtract)
                tt(o[1], o[1], tmp[1], ALU.subtract if conj else ALU.add)

            ve.wait_ge(act_small_done, 1)
            tt(tn(A_), lr, dt, ALU.mult)
            tt(tn(TH), li, dt, ALU.mult)
            ts(tn(NR), tn(TH), 1.0 / (2.0 * math.pi), ALU.mult, 12582912.0, ALU.add)
            ts(tn(NR), tn(NR), 12582912.0, ALU.subtract)
            stt(tn(R_), tn(NR), -c1, tn(TH), ALU.mult, ALU.add)
            stt(tn(R_), tn(NR), -c2, tn(R_), ALU.mult, ALU.add)
            stt(tn(R_), tn(NR), -c3, tn(R_), ALU.mult, ALU.add)
            ts(tn(R_), tn(R_), 3.1415925, ALU.min, -3.1415925, ALU.max)
            ve.tensor_scalar(tn(RH), tn(R_), 0.5, None, ALU.mult).then_inc(act_small, 1)
            ts(tn(AC), tn(A_), 0.35, ALU.min, -0.35, ALU.max)
            ts(tn(E1), tn(AC), 1.0 / 8.0, ALU.mult, 1.0, ALU.add)
            for q in range(7, 1, -1):
                tt(tn(E1), tn(E1), tn(AC), ALU.mult)
                ts(tn(E1), tn(E1), 1.0 / q, ALU.mult, 1.0, ALU.add)
            tt(tn(E1), tn(E1), tn(AC), ALU.mult)
            ts(tn(M0), tn(A_), 0.35, ALU.is_le)
            ts(tn(M1), tn(A_), -0.35, ALU.is_ge)
            tt(tn(M0), tn(M0), tn(M1), ALU.mult)
            ts(tn(M1), tn(M0), -1.0, ALU.mult, 1.0, ALU.add)
            ve.wait_ge(act_small_done, 2)
            ts(tn(EXPA), tn(EXPA), 1.0, ALU.subtract)
            tt(tn(EXPA), tn(EXPA), tn(M1), ALU.mult)
            tt(tn(E1), tn(E1), tn(M0), ALU.mult)
            tt(tn(E1), tn(E1), tn(EXPA), ALU.add)
            tt(tn(COSM1), tn(SINH), tn(SINH), ALU.mult)
            ts(tn(COSM1), tn(COSM1), -2.0, ALU.mult)
            ts(tn(COS), tn(COSM1), 1.0, ALU.add)
            ts(tn(ER), tn(E1), 1.0, ALU.add)
            tt(tn(LBR), tn(ER), tn(COS), ALU.mult)
            tt(tn(LBI), tn(ER), tn(SINR), ALU.mult)
            tt(tn(X_), tn(E1), tn(COS), ALU.mult)
            tt(tn(X_), tn(X_), tn(COSM1), ALU.add)
            tt(tn(DEN), lr, lr, ALU.mult)
            tt(tn(M0), li, li, ALU.mult)
            tt(tn(DEN), tn(DEN), tn(M0), ALU.add)
            link(ve.reciprocal(tn(DEN), tn(DEN)))
            tt(tn(CR), tn(X_), lr, ALU.mult)
            tt(tn(M0), tn(LBI), li, ALU.mult)
            tt(tn(CR), tn(CR), tn(M0), ALU.add)
            tt(tn(CR), tn(CR), tn(DEN), ALU.mult)
            tt(tn(CI), tn(LBI), lr, ALU.mult)
            tt(tn(M0), tn(X_), li, ALU.mult)
            tt(tn(CI), tn(CI), tn(M0), ALU.subtract)
            tt(tn(CI), tn(CI), tn(DEN), ALU.mult)
            tt(tn(R8), tn(ER), tn(ER), ALU.mult)
            tt(tn(R8), tn(R8), tn(R8), ALU.mult)
            tt(tn(R8), tn(R8), tn(R8), ALU.mult)

            def powers(tab, re, im):
                ve.memset(tab[:, 0, 0], 1.0)
                ve.memset(tab[:, 1, 0], 0.0)
                link(ve.tensor_copy(tab[:, 0, 1], re))
                link(ve.tensor_copy(tab[:, 1, 1], im))
                for w in (1, 2, 4):
                    o = [tab[:, q, w + 1:2 * w + 1] for q in (0, 1)]
                    lo = [tab[:, q, 1:w + 1] for q in (0, 1)]
                    top = [tab[:, q, w:w + 1].to_broadcast([P, w, GROUPS]) for q in (0, 1)]
                    tmp = [t[:, 0, 0:w * GROUPS].rearrange("p (w g) -> p w g", w=w) for t in (ta, tb)]
                    cmul(o, lo, top, tmp)

            powers(pw, tn(LBR), tn(LBI))
            u1 = [tn(COS), tn(SINR)]
            u2 = [tn(X_), tn(DEN)]
            tmp = [tn(M0), tn(M1)]
            cmul(u2, u1, u1, tmp)
            cmul(u1, u2, u2, tmp)
            cmul(u2, u1, u1, tmp)
            powers(ub, u2[0], u2[1])
            powers(ua, ub[:, 0, 8], ub[:, 1, 8])
            F, B = slice(0, STATE), slice(STATE, P)
            for q in (0, 1):
                def place(dst, part, order):
                    return ve.tensor_copy(dst[part, q].rearrange("p g i -> p i g"), pw[part, q, order])
                place(cpw, F, slice(1, 9))
                place(cpw, B, slice(8, 0, -1))
                place(bpw, F, slice(7, None, -1))
                ins = place(bpw, B, slice(0, 8))
            ve.sem_inc(kernels_ready, 1)
            ve.sem_inc(z_ready, 1)
            link(ins)
            ve.memset(E[:, 0, 0, 0:1], 0.0).then_inc(prep_done, 1)

            with ve.Fori(0, KS) as i:
                link.loop(i, SSM_STEPS)
                ve.wait_ge(z_ready, i + 1)
                gs = ds(i * GB, GB)
                big = [P, GB, CHUNK, CH]
                long = [t[:].rearrange("p a n -> p (a n)") for t in (ta, tb)]
                t4 = [t[:, 0:GB * P].rearrange("p (g s c) -> p g s c", g=GB, s=CHUNK) for t in long]
                ve.wait_ge(ct_ev, i + 1)
                ve.wait_ge(ssm_in, i * 128 + 128)
                coef = [tiny[:, k, gs].unsqueeze(2).to_broadcast([P, GB, CH]) for k in (CR, CI)]
                cmul([bb[:, 0], bb[:, 1]], coef, [b_raw[:, 0], b_raw[:, 1]],
                     [t[:, 0, 0:P].rearrange("p (g c) -> p g c", g=GB) for t in (ta, tb)])
                ts(bb[:, 2], bb[:, 1], -1.0, ALU.mult)
                cmul([cp[:, 0], cp[:, 1]],
                     [cpw[:, q, gs].unsqueeze(3).to_broadcast(big) for q in (0, 1)],
                     [cT[:, q].rearrange("p (g c) -> p g c", g=GB).unsqueeze(2).to_broadcast(big) for q in (0, 1)],
                     t4)
                cmul([w1t[:, 0], w1t[:, 1]],
                     [bpw[:, q, gs].unsqueeze(3).to_broadcast(big) for q in (0, 1)],
                     [bb[:, q].unsqueeze(2).to_broadcast(big) for q in (0, 1)], t4)
                ve.sem_inc(kernels_ready, 1)
                es = [P, GB, 9, 8]
                cmul([E[:, q].rearrange("p g (j l) -> p g j l", j=9) for q in (0, 1)],
                     [ua[:, q, 0:9, gs].rearrange("p j g -> p g j").unsqueeze(3).to_broadcast(es) for q in (0, 1)],
                     [ub[:, q, 0:8, gs].rearrange("p l g -> p g l").unsqueeze(2).to_broadcast(es) for q in (0, 1)],
                     [t[:, 0:GB * 72].rearrange("p (g j l) -> p g j l", g=GB, j=9) for t in long])
                link(ve.tensor_copy(decay[:], tiny[:, R8, gs].unsqueeze(2).to_broadcast([P, GB, NCH])))
                link(ve.memset(decay[:, :, 0:1], 0.0))
                def gk(t, q):
                    return t[:, q].rearrange("p (g k) -> p g k", g=GB)
                ve.wait_ge(sin_ev, i * 8 + 8)
                e = [E[:, q, :, 0:NCH] for q in (0, 1)]
                cmul([gk(ta, 0), gk(tb, 0)], e, [sin_[:, 0], sin_[:, 1]], [gk(ta, 1), gk(tb, 1)], conj=True)
                dk = decay[:].rearrange("p g k -> p (g k)")
                for q, t in ((0, ta), (1, tb)):
                    link(ve.tensor_tensor_scan(sin_[:, q].rearrange("p g k -> p (g k)"), dk, t[:, 0], 0.0,
                                               ALU.mult, ALU.add))
                ve.tensor_tensor(gk(ta, 0), e[0], sin_[:, 0], ALU.mult)
                ve.tensor_tensor(gk(ta, 1), e[1], sin_[:, 1], ALU.mult)
                ve.tensor_tensor(gk(tb, 0), e[0], sin_[:, 1], ALU.mult)
                tt(gk(tb, 1), e[1], sin_[:, 0], ALU.mult)
                for part, dst, src in ((F, slice(0, OCH), slice(1, OCH + 1)),
                                       (B, slice(OCH - 2, None, -1), slice(0, OCH - 1))):
                    ve.tensor_tensor(sx[part, 0, :, dst], gk(ta, 0)[part, :, src], gk(ta, 1)[part, :, src],
                                     ALU.subtract)
                    ins = ve.scalar_tensor_tensor(out=sx[part, 1, :, dst], in0=gk(tb, 0)[part, :, src], scalar=-1.0,
                                                  in1=gk(tb, 1)[part, :, src], op0=ALU.mult, op1=ALU.subtract)
                ins.then_inc(sx_ready, 1)
                ve.wait_ge(y_in, i * 128 + 128)
                y1, arg = ta[:, 0, 0:SEQ], tb[:, 0, 0:SEQ]
                ui = uT[:, ds(i, 1)].rearrange("p o s k -> p (o s) k")
                def sk3(t):
                    return t.rearrange("p (s k) -> p s k", s=CHUNK)
                stt(sk3(y1), ui[:, :, MCH:NCH], dskip[:, ds(i, 1)], sk3(yT[:]), ALU.mult, ALU.add)
                tt(arg, y1, y1, ALU.mult)
                ts(arg, arg, 0.044715, ALU.mult, 1.0, ALU.add)
                ve.tensor_tensor(arg, arg, y1, ALU.mult).then_inc(gelu_arg, 1)
                ve.wait_ge(gelu_exp, i + 1)
                zi = uT[:, ds(i, 1)].rearrange("p o s k -> p (o s k)")[:, 0:SEQ]
                ve.tensor_tensor(zi, y1, arg, ALU.mult).then_inc(z_ready, 1)
            link.end_loop(KS)

            ve.wait_ge(dist_iota, 1)
            ve.wait_ge(late_loaded, 64)
            ts(negsink[:], negsink[:], -1.0, ALU.mult)
            band, band0 = dist[:, META:], dist0[:, META:]
            ve.scalar_tensor_tensor(out=band, in0=band, scalar=-1.0, in1=band, op0=ALU.mult, op1=ALU.max)
            ve.scalar_tensor_tensor(out=band0, in0=band0, scalar=-1.0, in1=band0, op0=ALU.mult, op1=ALU.max
                                    ).then_inc(dist_abs, 1)
            ve.wait_ge(dist_ready, 1)
            split_lo(At(C_ATT))
            ve.sem_inc(sc_done, OPEN)
            ve.sem_inc(pt_dve, 1)
            ve.sem_inc(yal_ready, OPEN)
            groups = [(n, b) for n in range(NBLK) for b in (0, 1)]
            with ve.Fori(0, 2) as a:
                link.loop(a, 8 * 4)
                split_lo(At(C_ATT + 1, a, 4))
                ve.wait_ge(chunk_done, At(C_ATT, a, 4).plus(1 + OPEN))
                ve.tensor_tensor(kT[:].rearrange("p (h n) -> p h n", h=2), psum_of(0, True),
                                 rstd_b[:].rearrange("p (h n) -> p h n", h=2), ALU.mult).then_inc(proj_ev, 1)
                split_lo(At(C_ATT + 2, a, 4))
                ve.wait_ge(chunk_done, At(C_ATT + 1, a, 4).plus(1 + OPEN))
                for t in range(5):
                    ins = ve.tensor_scalar(vt[:, t, :], PS[:, 2 + t // 4, (t % 4) * P:(t % 4 + 1) * P],
                                           rcol[:, t:t + 1], None, ALU.mult)
                ins.then_inc(proj_ev, 1)
                split_lo(At(C_ATT + 3, a, 4))
                for r in range(QG):
                    if r % 2:
                        ve.wait_ge(chunk_done, At(C_ATT + 2 + r // 2, a, 4).plus(1 + OPEN))
                    else:
                        ve.wait_ge(proj_mm, a * 2 + r // 2 + 1)
                    ve.scalar_tensor_tensor(out=qT[:, r, :], in0=PS[:, r, :], scalar=DH ** -0.5,
                                            in1=rstd_b[:, META:T], op0=ALU.mult, op1=ALU.mult
                                            ).then_inc(proj_ev, 1)
                    if r == 1:
                        split_lo(At(C_ATT + 4, a, 4))

                def biased(gi):
                    n, b = groups[gi]
                    w = META + (2 if n in (0, NBLK - 1) else 3) * P
                    dd = dist0 if n == 0 else dist
                    par = gi % 2
                    for r in range(QG):
                        ve.wait_ge(s_mm, a * 32 + (4 * gi + r + 1))
                        ve.scalar_tensor_tensor(out=sc[:, par, r, 0:w], in0=dd[:, 0:w],
                                                scalar=negslope[:, ds(a * 8 + (QG * b + r), 1)],
                                                in1=PS[:, 4 + r % 2, 0:w], op0=ALU.mult, op1=ALU.add
                                                ).then_inc(sc_done, 1)
                    ve.wait_ge(sc_done, a * 32 + (4 * gi + 4 + OPEN))
                    link(ve.tensor_reduce(mx[:, par], sc[:, par, :, 0:w], AX.X, ALU.max))
                    nsk = negsink[:, ds(a * 8 + QG * b, QG)]
                    stt(negm[:, par], mx[:, par], -1.0, nsk, ALU.mult, ALU.min)
                    ve.tensor_tensor(sk[:, par], negm[:, par], nsk, ALU.subtract).then_inc(negm_ready, 1)

                def normalised(gi):
                    n, b = groups[gi]
                    w = META + (2 if n in (0, NBLK - 1) else 3) * P
                    par = gi % 2
                    ve.wait_ge(exp_done, a * 8 + gi + 1)
                    tt(den[:, par], rs[:, par], sk[:, par], ALU.add)
                    link(ve.reciprocal(den[:, par], den[:, par]))
                    for r in range(QG):
                        ins = ve.tensor_scalar(sc[:, par, r, 0:w], sc[:, par, r, 0:w], den[:, par, r:r + 1], None,
                                               ALU.mult)
                    ins.then_inc(p_ready, 1)

                def prob_tiles(gi):
                    n, b = groups[gi]
                    nb = 2 if n in (0, NBLK - 1) else 3
                    ve.wait_ge(pv_mm, a * 8 + gi + 1)
                    for r in (1, 3):
                        ve.wait_ge(t_mm, a * 32 + (4 * gi + r + 1))
                        ve.tensor_copy(pt[:, gi % 2, 0:nb, r, :],
                                       PS[:, 7, 0:nb * P].rearrange("p (j q) -> p j q", j=nb)).then_inc(pt_dve, 1)
                    ve.tensor_copy(ptm[:, gi % 2].rearrange("p r q -> p (r q)"), PS[0:META, 2, :]
                                   ).then_inc(pt_dve, 1)

                def result(gi):
                    n, b = groups[gi]
                    ve.wait_ge(yah_ready, a * 4 + (n + 1 + OPEN))
                    rows = (slice(None), ds(a * 4, QG), slice(n * P, (n + 1) * P))
                    ve.tensor_tensor(yal[rows], PS[:, 0 if n % 2 else 3, :].rearrange("p (r q) -> p r q", r=QG),
                                     as_f32(yah[rows]), ALU.subtract).then_inc(yal_ready, 1)

                for gi in range(10):
                    if gi < 8:
                        biased(gi)
                    if 0 < gi < 9:
                        normalised(gi - 1)
                        prob_tiles(gi - 1)
                    if gi > 1 and groups[gi - 2][1] == 1:
                        result(gi - 2)
            link.end_loop(2)

            def z_of(bt):
                return uT[:, bt].rearrange("p s k -> p (s k)")[:, 0:SEQ]
            for bt in range(KS):
                ve.wait_ge(zh_ready, bt + 1)
                ve.tensor_tensor(zl[:, bt], z_of(bt), as_f32(zh[:, bt]), ALU.subtract).then_inc(zl_ready, 1)
            split_lo(At(C_MERGE))
            for m in range(KS):
                ve.wait_ge(glu_sig, m + 1)
                if m >= 2:
                    ve.wait_ge(ysh_ready, m - 1)
                ve.tensor_tensor(ysf[:, m % 2].rearrange("p (k t) -> p t k", t=CHUNK),
                                 z_of(m).rearrange("p (t k) -> p t k", t=CHUNK),
                                 sig[:, m % 2].rearrange("p (t k) -> p t k", t=CHUNK), ALU.mult).then_inc(ysf_ready, 1)
                ve.wait_ge(ysh_ready, m + 1)
                ve.tensor_tensor(ysl[:, m], ysf[:, m % 2], as_f32(ysh[:, m]), ALU.subtract).then_inc(ysl_ready, 1)

            ve.sem_inc(mg_ready, OPEN)
            with ve.Fori(0, KD // 2) as i:
                link.loop(i, 2)
                for j in (0, 1):
                    m = At(j, i, 2)
                    split_lo(At(C_MERGE + 2 * j + 1, i, 4))
                    ve.wait_ge(chunk_done, At(C_MERGE + 2 * j, i, 4).plus(1 + OPEN))
                    for q in (0, 1):
                        ins = ve.tensor_tensor(gsig[:, j, q], PS[:, 4 * j + q, :], rstd_b[:, META:T], ALU.mult)
                    ins.then_inc(gates_scaled, 1)
                    split_lo(At(C_MERGE + 2 * j + 2, i, 4))
                    ve.wait_ge(gates_sig, m.plus(1))
                    ve.wait_ge(chunk_done, At(C_MERGE + 2 * j + 1, i, 4).plus(1 + OPEN))
                    ve.tensor_tensor(gsig[:, j, 0], gsig[:, j, 0], PS[:, 4 * j + 2, :], ALU.mult)
                    tt(gsig[:, j, 1], gsig[:, j, 1], PS[:, 4 * j + 3, :], ALU.mult)
                    ve.tensor_tensor(gsig[:, j, 0], gsig[:, j, 0], gsig[:, j, 1], ALU.add).then_inc(mg_ready, 1)
                    ve.wait_ge(mgh_ready, m.plus(1))
                    mm = m.plus(0)
                    ve.tensor_tensor(mgl[:, ds(mm, 1), :].rearrange("p o n -> p (o n)"), gsig[:, j, 0],
                                     as_f32(mgh[:, ds(mm, 1), :].rearrange("p o n -> p (o n)")), ALU.subtract
                                     ).then_inc(mgl_ready, 1)
            link.end_loop(KD // 2)

            norm_start(2)
            with ve.Fori(0, KD // 4) as i:
                for j in (0, 1):
                    split_lo(At(C_OUT + j + 1, i, 2))
                    for t in (0, 1):
                        m = At(2 * j + t, i, 4)
                        if t:
                            ve.wait_ge(chunk_done, At(C_OUT + j, i, 2).plus(1 + OPEN))
                        else:
                            ve.wait_ge(out_mm, At(j, i, 2).plus(1))
                        h = hT[:, ds(m.plus(0), 1), META:T].rearrange("p o n -> p (o n)")
                        ve.tensor_tensor(h, PS[:, 2 * j + t, :], h, ALU.add).then_inc(norms[2]["h_ready"], 1)
                        norm_step(2, m, False)
            ffn(1, C_UP2, C_DOWN2, False)
            token_var(3)
            ve.wait_ge(norms[3]["rcol_ready"], 1)
            for t in range(4):
                ve.wait_ge(fin_mm, t + 1)
                ve.tensor_scalar(y_nat[:, t, 512:1024], PS[:, 2 * t + 1, :], rcol[:, t + 1:t + 2], None, ALU.mult
                                 ).then_inc(fin_dve, 1)


_INS = ["x", "meta_tokens", "ffn1_norm", "ffn1_w_gate", "ffn1_w_up", "ffn1_w_down", "mix_norm", "w_in",
        "ssm_lam_re", "ssm_lam_im", "ssm_log_dt", "ssm_b_re", "ssm_b_im", "ssm_c_re", "ssm_c_im", "ssm_d",
        "ssm_w_glu", "attn_sink", "w_branch_ssm", "w_branch_attn", "w_out", "ffn2_norm", "ffn2_w_gate",
        "ffn2_w_up", "ffn2_w_down", "final_norm"]
_OUTS = [((1, 512, 1024), "float32")]


def kernel(**inputs):
    import numpy as _np
    import concourse.bacc as _bacc
    from concourse import mybir as _mybir
    from concourse.bass_utils import run_bass_kernel_spmd as _run

    nc = _bacc.Bacc("TRN2", target_bir_lowering=False, num_devices=1)
    arrays, args = {}, []
    for name in _INS:
        a = _np.ascontiguousarray(inputs[name])
        arrays[f"in_{name}_dram"] = a
        args.append(nc.dram_tensor(f"in_{name}_dram", a.shape, _mybir.dt.from_np(a.dtype), kind="ExternalInput").ap())
    for i, (shape, dtype) in enumerate(_OUTS):
        dt = _mybir.dt.from_np(_np.dtype(dtype))
        args.append(nc.dram_tensor(f"out_{i}_dram", shape, dt, kind="ExternalOutput").ap())
    build(nc, *args)
    r = _run(nc, [arrays], core_ids=[0])
    return r.results[0]["out_0_dram"]
```

```python
import math
from contextlib import ExitStack

import numpy as np

import concourse.bass as bass
from concourse import mybir

F32 = mybir.dt.float32
F32R = mybir.dt.float32r
ALU = mybir.AluOpType
ACT = mybir.ActivationFunctionType
AX = mybir.AxisListType

P = 128
D = 1024
KD = D // P
SEQ, META = 512, 16
T = META + SEQ
FF = 2816
KF = FF // P
HALF = T // 2
EPS = 1e-6
HEADS, KVH, DH, QG = 16, 4, 64, 4
WINDOW = 128
NBLK = SEQ // WINDOW
FAR = 3e32
GROUPS, STATE, CH = 32, 64, 16
SSM = GROUPS * CH
KS = SSM // P
GB = P // CH
CHUNK = 8
NCH = T // CHUNK
MCH = META // CHUNK
OCH = NCH - MCH
COL_Q, COL_K, COL_V = 0, HEADS * DH, (HEADS + KVH) * DH
COL_U = (HEADS + 2 * KVH) * DH
COL_GS = COL_U + SSM
COL_GA = COL_GS + D
DIST = 3 * WINDOW + 2 * META
TILES = 16
LOAD = 80
OPEN = 2

PW, UB, UA = 0, 18, 36
LR, LI, DT, A_, TH, NR, R_, RH, AC, E1, EXPA, SINH, COSM1, ER = range(UA, UA + 14)
CR, CI, R8, LBR, LBI, X_, DEN, COS, SINR, M0, M1, U2I = range(UA + 18, UA + 30)
PRM_ROWS = 66
SSM_STEPS = 19

C_UP1 = 0
C_DOWN1 = C_UP1 + KF
C_U = C_DOWN1 + 2 * KD
C_ATT = C_U + KS // 2
C_GLU = C_ATT + 8
C_MERGE = C_GLU + 1
C_OUT = C_MERGE + 2 * KD
C_UP2 = C_OUT + KD // 2
C_DOWN2 = C_UP2 + KF
C_END = C_DOWN2 + 2 * KD


def split_two_pi():
    c1 = 6.28125
    c2 = math.floor((2 * math.pi - c1) * 2 ** 21) / 2 ** 21
    return c1, c2, 2 * math.pi - c1 - c2


class At:

    def __init__(self, base, i=None, stride=0):
        self.base, self.i, self.stride = base, i, stride

    def plus(self, n):
        return self.base + n if self.i is None else self.i * self.stride + (self.base + n)

    def at(self, n):
        return At(self.base + n, self.i, self.stride)

    @property
    def slot(self):
        return self.base % 2

    def loads(self):
        if self.i is None:
            return LOAD * (self.base // 2 + 1)
        return self.i * (LOAD * self.stride // 2) + LOAD * (self.base // 2 + 1)


def at_end(base, times, stride, n, i):
    return At(base + (times - 1) * stride + n) if i is None else At(base + n, i, stride)


class Chain:

    def __init__(self, eng, sem):
        self.eng, self.sem, self.base, self.n = eng, sem, 0, 0

    def __call__(self, ins):
        self.n += 1
        ins.then_inc(self.sem, 1)
        self.eng.wait_ge(self.sem, self.base + self.n)

    def loop(self, i, steps, first=0):
        self.start, self.n = self.n, self.n - first * steps
        self.base, self.steps, self.first = i * steps, steps, first

    def end_loop(self, times):
        done = self.n - self.start + self.first * self.steps
        assert done == self.steps, (done, self.steps)
        self.base, self.n = 0, self.start + times * self.steps


def build(nc, x, meta_tokens, ffn1_norm, ffn1_w_gate, ffn1_w_up, ffn1_w_down, mix_norm, w_in,
          ssm_lam_re, ssm_lam_im, ssm_log_dt, ssm_b_re, ssm_b_im, ssm_c_re, ssm_c_im, ssm_d,
          ssm_w_glu, attn_sink, w_branch_ssm, w_branch_attn, w_out, ffn2_norm, ffn2_w_gate,
          ffn2_w_up, ffn2_w_down, final_norm, out):
    ds = bass.ds

    with ExitStack() as ctx:
        def sb(name, shape, dt=F32, stack=ctx):
            return stack.enter_context(nc.sbuf_tensor(name, shape, dt))

        def sem(name):
            return ctx.enter_context(nc.semaphore(name))

        hT = sb("hT", [P, KD, T])
        with ExitStack() as sx_:
            xh = sb("xh", [P, KD, T], F32R, sx_)
            xl = sb("xl", [P, KD, T], F32R, sx_)
        final_area = sb("final_area", [P, 2 * KD * T])
        hg = final_area[:, 0:KD * SEQ].rearrange("p (k n) -> p k n", k=KD)
        y_nat = final_area[:, KD * T:KD * T + 4 * D].rearrange("p (t n) -> p t n", t=4)
        wraw = sb("wraw", [P, 2, TILES, P])
        wh = sb("wh", [P, 2, TILES, P], F32R)
        wl = sb("wl", [P, 2, TILES, P], F32R)
        ident = sb("ident", [P, P])
        ones = sb("ones", [P, P])
        gains = sb("gains", [P, 4, KD])
        dskip = sb("dskip", [P, KS])
        ssum = sb("ssum", [P, T])
        sq = sb("sq", [P, T])
        rstd_b = sb("rstd_b", [P, T])
        rcol = sb("rcol", [P, 5])
        var = sb("var", [P, 5])
        expo = sb("expo", [P, 1])
        negslope = sb("negslope", [P, HEADS])
        negsink = sb("negsink", [P, HEADS])
        diag = sb("diag", [P, 5, P])
        PS = ctx.enter_context(nc.psum_tensor("PS", [P, 8, 512], F32))

        shared = sb("shared", [P, 4 * T])
        gate_buf = shared[:, 0:2 * T].rearrange("p (a n) -> p a n", a=2)
        up_buf = shared[:, 2 * T:4 * T].rearrange("p (a n) -> p a n", a=2)
        prm = shared[:, 0:PRM_ROWS * GROUPS].rearrange("p (r g) -> p r g", g=GROUPS)
        gsig = shared[:, 0:4 * SEQ].rearrange("p (j q n) -> p j q n", j=2, q=2)
        diag_row = diag[:].rearrange("p t n -> p (t n)")
        lam_raw = diag_row[0:GROUPS, 0:3 * 2 * STATE].rearrange("g (q d p) -> g q d p", q=3, d=2)
        dt_raw = diag_row[0:GROUPS, 3 * P:3 * P + 2]
        Y = diag_row[:, 0:SEQ].rearrange("p (g k) -> p g k", g=GB)
        y1, arg = ssum[:, 0:SEQ], sq[:, 0:SEQ]
        dist_made, dist = diag_row[:, 0:DIST], shared[:, 0:DIST]
        power_tmp = [diag_row[:, (3 + q) * P:(4 + q) * P] for q in (0, 1)]

        with ExitStack() as s0:
            x_nat = sb("x_nat", [P, 4, D], stack=s0)
            m_nat = sb("m_nat", [META, D], stack=s0)
        ffn_mem = []
        for n in (1, 2):
            with ExitStack() as s1:
                ffn_mem.append(dict(
                    gh=sb(f"g_hi{n}", [P, KF, T if n == 1 else SEQ], F32R, s1),
                    gl=sb(f"g_lo{n}", [P, KF, T if n == 1 else SEQ], F32R, s1), t1=gate_buf, t2=up_buf))
        with ExitStack() as s2:
            uT = sb("uT", [P, KS, CHUNK, NCH], stack=s2)
            with ExitStack() as s3:
                cp = sb("cp", [P, 2, GB, CHUNK, CH], stack=s3)
                toep = sb("toep", [P, GB, P], stack=s3)
                U = sb("U", [P, GB, NCH], stack=s3)
                sx = sb("sx", [P, 2, GB, OCH], stack=s3)
                yT = sb("yT", [P, CHUNK * OCH], stack=s3)
                krow = sb("krow", [CH, GB, 15 * CH], stack=s3)
                bb = sb("bb", [P, 3, GB, CH], stack=s3)
                cT = sb("cT", [P, 2, P], stack=s3)
                c_raw = sb("c_raw", [P, 2, P], stack=s3)
                b_raw = sb("b_raw", [P, 2, GB, CH], stack=s3)
                cpw = sb("cpw", [P, 2, GROUPS, CHUNK], stack=s3)
                bpw = sb("bpw", [P, 2, GROUPS, CHUNK], stack=s3)
                w1t = sb("w1t", [P, 2, GB, CHUNK, CH], stack=s3)
                w1 = sb("w1", [P, 2, GB, P], stack=s3)
                E = sb("E", [P, 2, GB, 72], stack=s3)
                decay = sb("decay", [P, GB, NCH], stack=s3)
                sin_ = sb("sin_", [P, 2, GB, NCH], stack=s3)
                ta = sb("ta", [P, 2, GB * NCH], stack=s3)
                tb = sb("tb", [P, 2, GB * NCH], stack=s3)
                kT = sb("kT", [P, T], stack=s3)
                vt = sb("vt", [P, 5, P], stack=s3)
                qT = sb("qT", [P, QG, SEQ], stack=s3)
            yah = sb("yah", [P, KD, SEQ], F32R, s2)
            yal = sb("yal", [P, KD, SEQ], F32R, s2)
            with ExitStack() as s3:
                sc = sb("sc", [P, 2, QG, META + 3 * WINDOW], stack=s3)
                mx = sb("mx", [P, 2, QG], stack=s3)
                negm = sb("negm", [P, 2, QG], stack=s3)
                sk = sb("sk", [P, 2, QG], stack=s3)
                den = sb("den", [P, 2, QG], stack=s3)
                rs = sb("rs", [P, 2, QG], stack=s3)
                pt = sb("pt", [P, 2, 3, QG, P], stack=s3)
                ptm = sb("ptm", [META, 2, QG, P], stack=s3)
            ysh = sb("ysh", [P, KS, SEQ], F32R, s2)
            ysl = sb("ysl", [P, KS, SEQ], F32R, s2)
            with ExitStack() as s3:
                zh = sb("zh", [P, KS, SEQ], F32R, s3)
                zl = sb("zl", [P, KS, SEQ], F32R, s3)
                sig = sb("sig", [P, 2, SEQ], stack=s3)
                ysf = sb("ysf", [P, 2, SEQ], stack=s3)
            with ExitStack() as s3:
                mgh = sb("mgh", [P, KD, SEQ], F32R, s3)
                mgl = sb("mgl", [P, KD, SEQ], F32R, s3)

        u_dram = nc.dram_tensor("u_regroup", [KS, GB, CH, CHUNK, NCH], F32, kind="Internal").ap()
        y_dram = nc.dram_tensor("y_regroup", [KS, CHUNK, CH, GB, OCH], F32, kind="Internal").ap()
        dist_dram = nc.dram_tensor("dist", [P, DIST], F32, kind="Internal").ap()

        x_loaded, const_loaded, consts_made = sem("x_loaded"), sem("const_loaded"), sem("consts_made")
        w_loaded = [sem("w_loaded0"), sem("w_loaded1")]
        w_hi, w_lo, chunk_done = sem("w_hi"), sem("w_lo"), sem("chunk_done")
        chain_sem, pool_chain = sem("dve_chain"), sem("pool_chain")
        x_late = sem("x_late")
        x_tr = sem("x_transposed")
        meta_in = sem("meta_in")
        dist_iota, dist_abs, dist_ready = sem("dist_iota"), sem("dist_abs"), sem("dist_ready")
        dist_out, dist_in = sem("dist_out"), sem("dist_in")
        late_loaded = sem("late_loaded")
        sp_paced = sem("sp_paced")
        norms = [{k: sem(f"{k}_{n}") for k in ("h_ready", "sq_ready", "xh_ready", "sum_ready", "xl_ready",
                                               "ssq_mm", "var_ready", "rcol_ready", "diag_ready",
                                               "bcast_mm", "rstd_ready")} for n in range(4)]
        ups = [{k: sem(f"{k}_{n}") for k in ("gate_mm", "gate_scaled", "silu_done", "up_scaled",
                                             "gg_ready", "gh_ready", "gl_ready")} for n in (1, 2)]
        out_mm = sem("out_mm")
        u_mm, u_ready = sem("u_mm"), sem("u_ready")
        lam_tr, powers_ready = sem("lam_tr"), sem("powers_ready")
        act_small, act_small_done = sem("act_small"), sem("act_small_done")
        lam_dt = sem("lam_dt")
        u_out, y_out, state_mm = sem("u_out"), sem("y_out"), sem("state_mm")
        (ssm_in, ct_mm, ct_ev, kernels_ready, krow_mm, krow_ev, w1t_ready, w1t_mm, w1_ev, toep_in, u_in,
         sin_mm, sin_ev, sx_ready, y_mm, y_ev, y_in, gelu_arg, gelu_exp, z_ready) = (sem(n) for n in (
            "ssm_in", "ct_mm", "ct_ev", "kernels_ready", "krow_mm", "krow_ev", "w1t_ready", "w1t_mm", "w1_ev",
            "toep_in", "u_in", "sin_mm", "sin_ev", "sx_ready", "y_mm", "y_ev", "y_in", "gelu_arg",
            "gelu_exp", "z_ready"))
        (proj_mm, proj_ev, s_mm, sc_done, negm_ready, exp_done, p_ready, t_mm, pt_act, pt_dve, pv_mm,
         yah_ready, yal_ready) = (sem(n) for n in (
            "proj_mm", "proj_ev", "s_mm", "sc_done", "negm_ready", "exp_done", "p_ready", "t_mm", "pt_act",
            "pt_dve", "pv_mm", "yah_ready", "yal_ready"))
        zh_ready, zl_ready, glu_mm, glu_sig, ysf_ready, ysh_ready, ysl_ready = (sem(n) for n in (
            "zh_ready", "zl_ready", "glu_mm", "glu_sig", "ysf_ready", "ysh_ready", "ysl_ready"))
        gates_mm, branch_mm, gates_scaled, gates_sig, mg_ready, mgh_ready, mgl_ready = (sem(n) for n in (
            "gates_mm", "branch_mm", "gates_scaled", "gates_sig", "mg_ready", "mgh_ready", "mgl_ready"))
        hg_ready, fin_mm, fin_act, fin_dve, stored = (sem(n) for n in (
            "hg_ready", "fin_mm", "fin_act", "fin_dve", "stored"))

        block = ctx.enter_context(nc.Block())

        def halves(base_bank, wide):
            if wide:
                return [(PS[:, base_bank + a, 0:HALF], slice(a * HALF, (a + 1) * HALF)) for a in (0, 1)]
            return [(PS[:, base_bank, 0:SEQ], slice(META, T))]

        def psum_of(bank, wide):
            return PS[:, bank:bank + 2, 0:HALF] if wide else PS[:, bank, 0:SEQ]

        def tokens(row, wide):
            return row.rearrange("p (a n) -> p a n", a=2) if wide else row[:, META:T]

        groups = [(n, b) for n in range(NBLK) for b in (0, 1)]
        last_group = len(groups) - 1

        def blocks(n):
            return 2 if n in (0, NBLK - 1) else 3

        def width(n):
            return META + blocks(n) * P

        def band_at(n):
            return (0, blocks(n) * P) if n == 0 else (META, 0)

        def prob_bank(r):
            return (6, 7, 1, 6)[r]

        @block.sync
        def _(sp):
            def weight_chunk(c, parts, settle=False):
                sp.wait_ge(w_lo, c.plus(OPEN - 1))
                if settle:
                    sp.sem_inc(sp_paced, 1)
                for n, (dst, src) in enumerate(parts):
                    inc = 16 if n + 1 < len(parts) else LOAD - 16 * n
                    sp.dma_start(dst, src).then_inc(w_loaded[c.slot], inc)

            def kview(w):
                return w.rearrange("(k p) n -> p k n", p=P)

            def tiles_of(c, t0, w, col):
                nk = w.shape[0] // P
                return wraw[:, c.slot, t0:t0 + nk, :], kview(w)[:, :, ds(col, P)]

            def ffn_stream(c_up, c_down, wg, wu, wd):
                with sp.Fori(0, KF // 2) as i:
                    for j in (0, 1):
                        c, col = At(c_up + j, i, 2), i * (2 * P) + j * P
                        weight_chunk(c, [tiles_of(c, 0, wg, col), tiles_of(c, KD, wu, col)])
                with sp.Fori(0, KD // 2) as i:
                    for j in range(4):
                        c = At(c_down + j, i, 4)
                        k0 = (j % 2) * (KF // 2)
                        src = kview(wd)[:, k0:k0 + KF // 2, ds(i * (2 * P) + (j // 2) * P, P)]
                        weight_chunk(c, [(wraw[:, c.slot, 0:6, :], src[:, 0:6, :]),
                                         (wraw[:, c.slot, 6:11, :], src[:, 6:11, :])])

            sp.dma_start(m_nat[:], meta_tokens).then_inc(x_loaded, 16)
            for half, done in ((slice(0, D // 2), x_loaded), (slice(D // 2, D), x_late)):
                sp.dma_start(x_nat[:, :, half], x[0].rearrange("(t p) n -> p t n", p=P)[:, :, half]
                             ).then_inc(done, 16)
            sp.wait_ge(dist_ready, 1)
            sp.dma_start(dist_dram, dist_made).then_inc(dist_out, 16)
            ffn_stream(C_UP1, C_DOWN1, ffn1_w_gate[0], ffn1_w_up[0], ffn1_w_down[0])
            win = w_in[0]
            for j in range(KS // 2):
                c, col = At(C_U + j), COL_U + 2 * j * P
                weight_chunk(c, [tiles_of(c, 0, win, col), tiles_of(c, KD, win, col + P)])

            def att_chunk(a, j):
                c = At(C_ATT + 4 * a + j)
                if j < 2:
                    weight_chunk(c, [tiles_of(c, 0, win, (COL_K, COL_V)[j] + a * P)])
                else:
                    weight_chunk(c, [
                        (wraw[:, c.slot, t * KD:(t + 1) * KD, b * DH:(b + 1) * DH],
                         kview(win)[:, :, ds((2 * QG * a + b * QG + 2 * (j - 2) + t) * DH, DH)])
                        for t in (0, 1) for b in (0, 1)])

            def state_params(i):
                for ri, c_par in enumerate((ssm_c_re, ssm_c_im)):
                    for dr in (0, 1):
                        sp.dma_start(c_raw[:, ri, dr * STATE:(dr + 1) * STATE],
                                     c_par[0, dr].rearrange("g c p -> (g c) p")[ds(i * P, P), :]
                                     ).then_inc(ssm_in, 16)
                for ri, b_par in enumerate((ssm_b_re, ssm_b_im)):
                    for dr in (0, 1):
                        sp.dma_start(b_raw[dr * STATE:(dr + 1) * STATE, ri],
                                     b_par[0, dr].rearrange("g p c -> p g c")[:, ds(i * GB, GB), :]
                                     ).then_inc(ssm_in, 16)

            sp.wait_ge(chunk_done, C_U + OPEN)
            state_params(0)
            for j in range(3):
                att_chunk(0, j)
            sp.wait_ge(u_ready, KS)
            sp.dma_start(u_dram.rearrange("b g c s k -> (g c) b (s k)"),
                         uT[:].rearrange("p b s k -> p b (s k)")).then_inc(u_out, 16)

            def load_u(i):
                for s in range(CHUNK):
                    sp.dma_start(U[s * CH:(s + 1) * CH, :, :],
                                 u_dram[ds(i, 1)].rearrange("o g c s k -> s c (o g) k")[s]).then_inc(u_in, 16)

            def ssm_batch(i, more):
                if more:
                    sp.wait_ge(kernels_ready, i + 1)
                    sp.sem_inc(sp_paced, 1)
                    state_params(i + 1)
                sp.wait_ge(krow_ev, i * 5 + 5)
                for s in range(CHUNK):
                    c0 = (CHUNK - 1 - s) * CH
                    sp.dma_start(toep[s * CH:(s + 1) * CH, :, :], krow[:, :, c0:c0 + P]).then_inc(toep_in, 16)
                if not more:
                    sp.wait_ge(kernels_ready, KS)
                    sp.wait_ge(dist_out, 16)
                    sp.dma_start(dist, dist_dram).then_inc(dist_in, 16)
                sp.wait_ge(y_ev, i + 1)
                sp.sem_inc(sp_paced, 1)
                sp.dma_start(y_dram[ds(i, 1)].rearrange("o t c g k -> (o t c) (g k)"),
                             Y.rearrange("p g k -> p (g k)")).then_inc(y_out, 16)
                if more:
                    load_u(i + 1)
                sp.wait_ge(y_out, i * 16 + 16)
                sp.sem_inc(sp_paced, 1)
                for g in range(GB):
                    sp.dma_start(yT[g * CH:(g + 1) * CH, :].rearrange("c (t k) -> c t k", t=CHUNK),
                                 y_dram[ds(i, 1)].rearrange("o t c g k -> g c (o t) k")[g]).then_inc(y_in, 16)

            sp.wait_ge(u_out, 16)
            load_u(0)
            att_chunk(0, 3)
            att_chunk(1, 0)
            att_chunk(1, 1)
            with sp.Fori(0, KS - 1) as i:
                ssm_batch(i, True)
            ssm_batch(KS - 1, False)
            att_chunk(1, 2)
            att_chunk(1, 3)
            c = At(C_GLU)
            weight_chunk(c, [(wraw[:, c.slot, m * KS:(m + 1) * KS, :],
                              kview(ssm_w_glu[0])[:, :, m * P:(m + 1) * P]) for m in range(KS)])
            with sp.Fori(0, KD // 2) as i:
                col_end = sp.snap(i * (2 * P) + 2 * P)
                for j in (0, 1):
                    col = col_end + (j - 2) * P
                    c = At(C_MERGE + 2 * j, i, 4)
                    weight_chunk(c, [tiles_of(c, 0, win, col + COL_GS), tiles_of(c, KD, win, col + COL_GA)])
                    c = At(C_MERGE + 2 * j + 1, i, 4)
                    wa = w_branch_attn[0].rearrange("(a b r d) n -> a b d r n", a=2, b=2, r=QG)
                    weight_chunk(c, [tiles_of(c, 0, w_branch_ssm[0], col)] + [
                        (wraw[b * DH:(b + 1) * DH, c.slot, KS + a * QG:KS + (a + 1) * QG, :],
                         wa[a, b][:, :, ds(col, P)]) for a in (0, 1) for b in (0, 1)], settle=True)
            with sp.Fori(0, KD // 4) as i:
                for j in (0, 1):
                    c, col = At(C_OUT + j, i, 2), i * (4 * P) + j * 2 * P
                    weight_chunk(c, [tiles_of(c, 0, w_out[0], col), tiles_of(c, KD, w_out[0], col + P)])
            ffn_stream(C_UP2, C_DOWN2, ffn2_w_gate[0], ffn2_w_up[0], ffn2_w_down[0])

            for t in range(4):
                sp.wait_ge(fin_act, t + 1)
                sp.wait_ge(fin_dve, t + 1)
                sp.dma_start(out[0, t * P:(t + 1) * P, :], y_nat[:, t, :]).then_inc(stored, 16)
            sp.wait_ge(stored, 64)

        @block.gpsimd
        def _(pool):
            pool.memset(ident[:], 0.0).then_inc(consts_made, 1)
            pool.memset(ones[:], 1.0).then_inc(consts_made, 1)
            pool.memset(expo[:], -0.5).then_inc(consts_made, 1)
            pool.wait_ge(consts_made, 3)
            pool.affine_select(out=ident[:], in_=ident[:], compare_op=ALU.not_equal, fill=1.0, base=0,
                               pattern=[[-1, P]], channel_multiplier=1).then_inc(consts_made, 1)

            for h in range(HEADS):
                pool.memset(negslope[:, h:h + 1], -float(np.float32(2.0 ** (-8.0 * (h + 1) / HEADS))))
            pool.memset(dist_made[:, 0:META], 0.0)
            pool.memset(dist_made[:, DIST - META:DIST], 0.0)
            band = dist_made[:, META:DIST - META]
            pool.iota(band, pattern=[[-1, 3 * WINDOW]], base=WINDOW, channel_multiplier=1,
                      allow_small_or_imprecise_dtypes=True).then_inc(dist_iota, 1)
            pool.wait_ge(dist_abs, 1)
            pool.affine_select(out=band, in_=band, compare_op=ALU.is_ge, fill=FAR, base=0,
                               pattern=[[1, 3 * WINDOW]], channel_multiplier=-1).then_inc(dist_iota, 1)
            pool.wait_ge(dist_iota, 2)
            pool.affine_select(out=band, in_=band, compare_op=ALU.is_ge, fill=FAR, base=2 * WINDOW,
                               pattern=[[-1, 3 * WINDOW]], channel_multiplier=1).then_inc(dist_ready, 1)

            def token_rstd(n):
                pool.wait_ge(norms[n]["var_ready"], 1)
                pool.tensor_tensor(rcol[:], var[:], expo[:].to_broadcast([P, 5]), ALU.pow
                                   ).then_inc(norms[n]["rcol_ready"], 1)

            def tt(o, x0, x1, op):
                step(pool.tensor_tensor(o, x0, x1, op))

            def ts(o, x0, s1, op0, s2=None, op1=None):
                if op1 is None:
                    step(pool.tensor_scalar(o, x0, s1, None, op0))
                else:
                    step(pool.tensor_scalar(o, x0, s1, s2, op0, op1))

            def cmul(o, x0, x1, tmp):
                pool.tensor_tensor(o[0], x0[0], x1[0], ALU.mult)
                pool.tensor_tensor(tmp[0], x0[1], x1[1], ALU.mult)
                pool.tensor_tensor(o[1], x0[0], x1[1], ALU.mult)
                tt(tmp[1], x0[1], x1[0], ALU.mult)
                pool.tensor_tensor(o[0], o[0], tmp[0], ALU.subtract)
                tt(o[1], o[1], tmp[1], ALU.add)

            def tn(k):
                return prm[:, k]

            def powers(tab, re, im):
                pool.memset(tn(tab), 1.0)
                pool.memset(tn(tab + 9), 0.0)
                pool.tensor_copy(tn(tab + 1), re)
                step(pool.tensor_copy(tn(tab + 10), im))
                for w in (1, 2, 4):
                    o = [prm[:, q + w + 1:q + 2 * w + 1] for q in (tab, tab + 9)]
                    lo = [prm[:, q + 1:q + w + 1] for q in (tab, tab + 9)]
                    top = [prm[:, q + w:q + w + 1].to_broadcast([P, w, GROUPS]) for q in (tab, tab + 9)]
                    cmul(o, lo, top, [t[:, 0:w * GROUPS].rearrange("p (w g) -> p w g", w=w) for t in power_tmp])

            token_rstd(0)

            step = Chain(pool, pool_chain)
            pool.wait_ge(late_loaded, 64)
            pool.tensor_copy(lam_raw[:, 2], dt_raw.unsqueeze(2).to_broadcast([GROUPS, 2, STATE])
                             ).then_inc(lam_dt, 1)
            pool.wait_ge(act_small_done, 1)
            c1, c2, c3 = split_two_pi()
            tt(tn(A_), tn(LR), tn(DT), ALU.mult)
            tt(tn(TH), tn(LI), tn(DT), ALU.mult)
            ts(tn(NR), tn(TH), 1.0 / (2.0 * math.pi), ALU.mult, 12582912.0, ALU.add)
            ts(tn(NR), tn(NR), 12582912.0, ALU.subtract)
            for c, src in ((c1, TH), (c2, R_), (c3, R_)):
                ts(tn(RH), tn(NR), -c, ALU.mult)
                tt(tn(R_), tn(RH), tn(src), ALU.add)
            ts(tn(R_), tn(R_), 3.1415925, ALU.min, -3.1415925, ALU.max)
            pool.tensor_scalar(tn(RH), tn(R_), 0.5, None, ALU.mult).then_inc(act_small, 1)
            ts(tn(AC), tn(A_), 0.35, ALU.min, -0.35, ALU.max)
            ts(tn(E1), tn(AC), 1.0 / 8.0, ALU.mult, 1.0, ALU.add)
            for q in range(7, 1, -1):
                tt(tn(E1), tn(E1), tn(AC), ALU.mult)
                ts(tn(E1), tn(E1), 1.0 / q, ALU.mult, 1.0, ALU.add)
            tt(tn(E1), tn(E1), tn(AC), ALU.mult)
            ts(tn(M0), tn(A_), 0.35, ALU.is_le)
            ts(tn(M1), tn(A_), -0.35, ALU.is_ge)
            tt(tn(M0), tn(M0), tn(M1), ALU.mult)
            ts(tn(M1), tn(M0), -1.0, ALU.mult, 1.0, ALU.add)
            pool.wait_ge(act_small_done, 2)
            ts(tn(EXPA), tn(EXPA), 1.0, ALU.subtract)
            tt(tn(EXPA), tn(EXPA), tn(M1), ALU.mult)
            tt(tn(E1), tn(E1), tn(M0), ALU.mult)
            tt(tn(E1), tn(E1), tn(EXPA), ALU.add)
            tt(tn(COSM1), tn(SINH), tn(SINH), ALU.mult)
            ts(tn(COSM1), tn(COSM1), -2.0, ALU.mult)
            ts(tn(COS), tn(COSM1), 1.0, ALU.add)
            ts(tn(ER), tn(E1), 1.0, ALU.add)
            tt(tn(LBR), tn(ER), tn(COS), ALU.mult)
            tt(tn(LBI), tn(ER), tn(SINR), ALU.mult)
            tt(tn(X_), tn(E1), tn(COS), ALU.mult)
            tt(tn(X_), tn(X_), tn(COSM1), ALU.add)
            tt(tn(DEN), tn(LR), tn(LR), ALU.mult)
            tt(tn(M0), tn(LI), tn(LI), ALU.mult)
            tt(tn(DEN), tn(DEN), tn(M0), ALU.add)
            tt(tn(CR), tn(X_), tn(LR), ALU.mult)
            tt(tn(M0), tn(LBI), tn(LI), ALU.mult)
            tt(tn(CR), tn(CR), tn(M0), ALU.add)
            tt(tn(CI), tn(LBI), tn(LR), ALU.mult)
            tt(tn(M0), tn(X_), tn(LI), ALU.mult)
            tt(tn(CI), tn(CI), tn(M0), ALU.subtract)
            tt(tn(R8), tn(ER), tn(ER), ALU.mult)
            tt(tn(R8), tn(R8), tn(R8), ALU.mult)
            tt(tn(R8), tn(R8), tn(R8), ALU.mult)
            powers(PW, tn(LBR), tn(LBI))
            u1, u2, tmp = [tn(COS), tn(SINR)], [tn(X_), tn(U2I)], [tn(M0), tn(M1)]
            cmul(u2, u1, u1, tmp)
            cmul(u1, u2, u2, tmp)
            cmul(u2, u1, u1, tmp)
            powers(UB, u2[0], u2[1])
            powers(UA, tn(UB + 8), tn(UB + 17))
            pool.sem_inc(powers_ready, 1)

            token_rstd(1)
            token_rstd(2)
            token_rstd(3)

        @block.tensor
        def _(pe):
            def passes(bank, wide, c, t0, nk, hi, lo, k0, first, last, wait_k=None):
                outs = halves(bank, wide)
                for k in range(nk):
                    if wait_k is not None:
                        pe.wait_ge(wait_k, k + 1)
                    todo = ((wh, hi), (wh, lo), (wl, hi))
                    for n, (w, xt) in enumerate(todo):
                        for ps, tok in outs:
                            if xt.shape[-1] == SEQ:
                                tok = slice(0, SEQ)
                            ins = pe.matmul(ps, w[:, c.slot, t0 + k, :], xt[:, k0 + k, tok],
                                            start=first and k == 0 and n == 0,
                                            stop=last and k == nk - 1 and n == 2)
                return ins

            def chunk_ready(c):
                pe.wait_ge(w_hi, c.plus(1))
                pe.wait_ge(w_lo, c.plus(1 + OPEN))

            def sum_squares(n):
                s = norms[n]
                pe.wait_ge(s["sum_ready"], KD + 1)
                for t in range(5):
                    t0 = 0 if t == 0 else META + (t - 1) * P
                    ins = pe.matmul(PS[:, 4, t:t + 1], ssum[:, t0:t0 + P], ones[:, 0:1], start=True, stop=True)
                ins.then_inc(s["ssq_mm"], 1)

            def spread_rstd(n):
                s = norms[n]
                pe.wait_ge(s["diag_ready"], 1)
                pe.matmul(PS[:, 6, 0:META], ones[0:META, :], diag[0:META, 0, 0:META], start=True, stop=True)
                for t in range(1, 5):
                    o = PS[:, 6, META + (t - 1) * P:META + t * P] if t < 3 else PS[:, 7, (t - 3) * P:(t - 2) * P]
                    ins = pe.matmul(o, ones[:], diag[:, t, :], start=True, stop=True)
                ins.then_inc(s["bcast_mm"], 1)

            def up_chunk(c, n, f, wide, with_norm):
                s = ups[n]
                chunk_ready(c)
                b = f.base % 2
                gate_bank, up_bank = (4 * b, 4 * b + 2) if wide else (2 * b, 2 * b + 1)
                pe.wait_ge(s["gate_scaled"], f.plus(OPEN - 1))
                passes(gate_bank, wide, c, 0, KD, xh, xl, 0, True, True,
                       norms[2 * n]["xl_ready"] if with_norm else None).then_inc(s["gate_mm"], 1)
                if with_norm:
                    sum_squares(2 * n)
                pe.wait_ge(s["up_scaled"], f.plus(OPEN - 1))
                passes(up_bank, wide, c, KD, KD, xh, xl, 0, True, True).then_inc(chunk_done, 1)
                if with_norm:
                    spread_rstd(2 * n)
                    pe.wait_ge(norms[2 * n]["rstd_ready"], 1)

            def ffn(n, c_up, c_down, wide):
                s, g = ups[n], ffn_mem[n]
                for j in (0, 1):
                    up_chunk(At(c_up + j), n, At(j), wide, j == 0)
                with pe.Fori(1, KF // 2) as i:
                    for j in (0, 1):
                        up_chunk(At(c_up + j, i, 2), n, At(j, i, 2), wide, False)
                pe.wait_ge(s["gate_scaled"], KF + OPEN)
                pe.wait_ge(s["up_scaled"], KF + OPEN)
                if n == 0:
                    pe.wait_ge(late_loaded, 64)
                    pe.wait_ge(lam_dt, 1)
                    for q in range(3):
                        ins = pe.transpose(PS[:, 2, q * GROUPS:(q + 1) * GROUPS],
                                           lam_raw[:, q].rearrange("g d p -> g (d p)"), ident[0:GROUPS, 0:GROUPS])
                    ins.then_inc(lam_tr, 1)
                with pe.Fori(0, KD // 2) as i:
                    for m in (0, 1):
                        pe.wait_ge(norms[2 * n + 1]["h_ready"], At(m, i, 2).plus(OPEN - 1))
                        for h in (0, 1):
                            c = At(c_down + 2 * m + h, i, 4)
                            chunk_ready(c)
                            pe.wait_ge(s["gl_ready"], KF if h else KF // 2)
                            passes(4 * m, wide, c, 0, KF // 2, g["gh"], g["gl"], h * (KF // 2),
                                   h == 0, h == 1).then_inc(chunk_done, 1)

            pe.sem_inc(chunk_done, OPEN)
            pe.sem_inc(pv_mm, OPEN)

            pe.wait_ge(consts_made, 4)
            pe.wait_ge(x_loaded, 32)
            for k in range(KD):
                ins = pe.transpose(PS[:, 0, k * META:(k + 1) * META], m_nat[:, k * P:(k + 1) * P],
                                   ident[0:META, 0:META])
            ins.then_inc(x_tr, 1)
            for k in range(KD):
                if k == KD // 2:
                    pe.wait_ge(x_late, 16)
                if k == KD - 1:
                    pe.wait_ge(meta_in, 1)
                for t in range(4):
                    ins = pe.transpose(PS[:, (k + 1) % 8, t * P:(t + 1) * P],
                                       x_nat[:, t, k * P:(k + 1) * P], ident[:])
                ins.then_inc(x_tr, 1)
            pe.wait_ge(norms[0]["h_ready"], KD + OPEN)

            ffn(0, C_UP1, C_DOWN1, True)

            F, B = slice(0, STATE), slice(STATE, P)

            def c_transposes(i, bank, col):
                pe.wait_ge(ssm_in, i * 128 + 128)
                for ri in (0, 1):
                    ins = pe.transpose(PS[:, bank, col + ri * P:col + (ri + 1) * P], c_raw[:, ri, :], ident[:])
                ins.then_inc(ct_mm, 1)

            def w1_transposes(i):
                pe.wait_ge(w1t_ready, i + 1)
                for ri in (0, 1):
                    for g in range(GB):
                        ins = pe.transpose(PS[:, 2 * ri + g // 4, (g % 4) * P:(g % 4 + 1) * P],
                                           w1t[:, ri, g].rearrange("p s c -> p (s c)"), ident[:])
                ins.then_inc(w1t_mm, 1)

            def ssm_batch(i, more):
                pe.wait_ge(u_in, i * 128 + 128)
                for ri in (0, 1):
                    pe.wait_ge(w1_ev, i * 2 + 1 + ri)
                    for g in range(GB):
                        ins = pe.matmul(PS[:, 4 + 2 * ri + g // 4, (g % 4) * NCH:(g % 4 + 1) * NCH],
                                        w1[:, ri, g, :], U[:, g, :], start=True, stop=True)
                ins.then_inc(sin_mm, 1)
                pe.wait_ge(kernels_ready, i + 1)
                pe.wait_ge(sin_ev, i * 8 + 8)
                for g in range(GB):
                    for q, ri in ((0, 0), (2, 1)):
                        pe.matmul(PS[0:CH, 1, g * CH:(g + 1) * CH], bb[:, q, g, :], cT[:, ri, g * CH:(g + 1) * CH],
                                  start=ri == 0, stop=ri == 1)
                if more:
                    c_transposes(i + 1, 2, 0)
                for g in range(GB):
                    for bank, part, i0 in ((4 + g // 4, B, 1), (6 + g // 4, F, 0)):
                        o = PS[0:CH, bank, (g % 4) * 7 * CH:(g % 4 + 1) * 7 * CH]
                        for q, ri in ((0, 0), (2, 1)):
                            ins = pe.matmul(o, bb[part, q, g, :],
                                            cp[part, ri, g, i0:i0 + 7, :].rearrange("p i c -> p (i c)"),
                                            start=ri == 0, stop=ri == 1)
                ins.then_inc(krow_mm, 1)
                def y_of(g):
                    return PS[:, 0, g * OCH:(g + 1) * OCH]
                pe.wait_ge(sx_ready, i + 1)
                for g in range(GB):
                    for ri in (0, 1):
                        ins = pe.matmul(y_of(g), cp[:, ri, g].rearrange("p i c -> p (i c)"), sx[:, ri, g, :],
                                        start=g == 0 and ri == 0, stop=False)
                ins.then_inc(state_mm, 1)
                pe.wait_ge(toep_in, i * 128 + 128)
                for g in range(GB):
                    ins = pe.matmul(y_of(g), toep[:, g, :], U[:, g, MCH:NCH], start=False,
                                    stop=g == GB - 1)
                ins.then_inc(y_mm, 1)
                if more:
                    pe.wait_ge(y_ev, i + 1)
                    pe.wait_ge(krow_ev, i * 5 + 5)
                    w1_transposes(i + 1)

            def project(a):
                c = At(C_ATT + 4 * a)
                chunk_ready(c)
                passes(4, True, c, 0, KD, xh, xl, 0, True, True).then_inc(chunk_done, 1)
                c = At(C_ATT + 4 * a + 1)
                chunk_ready(c)
                for t in range(5):
                    t0 = 0 if t == 0 else META + (t - 1) * P
                    o = PS[:, 6 + t // 4, (t % 4) * P:(t % 4 + 1) * P]
                    for k in range(KD):
                        for q, (xt, w) in enumerate(((xh, wh), (xh, wl), (xl, wh))):
                            ins = pe.matmul(o, xt[:, k, t0:t0 + P], w[:, c.slot, k, :],
                                            start=k == 0 and q == 0, stop=k == KD - 1 and q == 2)
                ins.then_inc(chunk_done, 1)
                if a == 0:
                    w1_transposes(0)
                    pe.wait_ge(w1_ev, 2)
                else:
                    pe.wait_ge(yah_ready, 4 + OPEN)
                    pe.wait_ge(yal_ready, 4 + OPEN)
                for r in range(QG):
                    c = At(C_ATT + 4 * a + 2 + r // 2)
                    if r % 2 == 0:
                        chunk_ready(c)
                    passes(r, False, c, (r % 2) * KD, KD, xh, xl, 0, True, True
                           ).then_inc(chunk_done if r % 2 else proj_mm, 1)

            pe.wait_ge(norms[1]["h_ready"], KD - 1 + OPEN)
            for j in range(KS // 2):
                c = At(C_U + j)
                chunk_ready(c)
                for t in (0, 1):
                    bt = 2 * j + t
                    ins = passes(2 * bt, True, c, t * KD, KD, xh, xl, 0, True, True,
                                 norms[1]["xl_ready"] if bt == 0 else None)
                    ins.then_inc(chunk_done if t else u_mm, 1)
                    if bt == 0:
                        sum_squares(1)
                        c_transposes(0, 5, 0)
                    if bt == 1:
                        spread_rstd(1)
                        pe.wait_ge(norms[1]["rstd_ready"], 1)
                        pe.wait_ge(ct_ev, 1)

            pe.wait_ge(u_ready, KS)
            project(0)
            pe.wait_ge(proj_ev, 6)
            with pe.Fori(0, KS - 1) as i:
                ssm_batch(i, True)
            ssm_batch(KS - 1, False)

            def groups_of(a):
                def scores(gi, heads):
                    n, b = groups[gi]
                    part = slice(b * DH, (b + 1) * DH)
                    band, meta = band_at(n)
                    for r in heads:
                        pe.wait_ge(sc_done, a * 32 + (4 * gi + r - 1 + OPEN))
                        q = qT[part, r, n * P:(n + 1) * P]
                        k0 = META + max(n - 1, 0) * P
                        pe.matmul(PS[:, 4 + r % 2, band:band + blocks(n) * P], q, kT[part, k0:k0 + blocks(n) * P],
                                  start=True, stop=True)
                        pe.matmul(PS[:, 4 + r % 2, meta:meta + META], q, kT[part, 0:META], start=True, stop=True
                                  ).then_inc(s_mm, 1)

                def transposes(gi):
                    n, b = groups[gi]
                    band, meta = band_at(n)
                    pe.wait_ge(p_ready, a * 8 + gi + 1)
                    pe.wait_ge(pt_dve, a * 24 + 3 * gi + 1)
                    for r in range(QG):
                        if r >= 2:
                            pe.wait_ge(pt_act, a * 16 + 2 * gi + r - 1)
                        for j in range(blocks(n)):
                            pe.transpose(PS[:, prob_bank(r), j * P:(j + 1) * P],
                                         sc[:, gi % 2, r, band + j * P:band + (j + 1) * P], ident[:])
                        pe.transpose(PS[0:META, 2, r * P:(r + 1) * P], sc[:, gi % 2, r, meta:meta + META], ident[:]
                                     ).then_inc(t_mm, 1)

                def values(gi):
                    n, b = groups[gi]
                    kb = max(n - 1, 0)
                    pe.wait_ge(pt_act, a * 16 + (2 * gi + 3))
                    pe.wait_ge(pt_dve, a * 24 + (3 * gi + 4))
                    if b == 0:
                        pe.wait_ge(yah_ready, a * 4 + (n - 1 + OPEN))
                        pe.wait_ge(yal_ready, a * 4 + (n - 1 + OPEN))
                    o = PS[b * DH:(b + 1) * DH, 0 if n % 2 else 3, :]
                    for j in range(blocks(n)):
                        pe.matmul(o, vt[:, 1 + kb + j, b * DH:(b + 1) * DH],
                                  pt[:, gi % 2, j].rearrange("p r q -> p (r q)"), start=j == 0, stop=False)
                    pe.matmul(o, vt[0:META, 0, b * DH:(b + 1) * DH],
                              ptm[:, gi % 2].rearrange("p r q -> p (r q)"), start=False, stop=True
                              ).then_inc(pv_mm, 1)

                pe.wait_ge(proj_ev, a * 6 + 6)
                for gi in range(-1, last_group + 2):
                    if (a, gi) == (0, 0):
                        pe.wait_ge(y_ev, KS)
                    if gi < last_group:
                        scores(gi + 1, (0, 1))
                    if gi > 0:
                        values(gi - 1)
                    if gi < last_group:
                        scores(gi + 1, (2, 3))
                    if 0 <= gi <= last_group:
                        transposes(gi)

            pe.wait_ge(krow_ev, KS * 5)
            groups_of(0)
            pe.wait_ge(sc_done, 32 + OPEN)
            project(1)
            groups_of(1)

            c = At(C_GLU)
            chunk_ready(c)
            pe.wait_ge(yah_ready, 8 + OPEN)
            pe.wait_ge(yal_ready, 8 + OPEN)
            for m in range(KS):
                ins = passes(m, False, c, m * KS, KS, zh, zl, 0, True, True, zl_ready if m == 0 else None)
            ins.then_inc(chunk_done, 1)

            pe.wait_ge(ysh_ready, KS)
            with pe.Fori(0, KD // 2) as i:
                for j in (0, 1):
                    pe.wait_ge(mg_ready, At(j, i, 2).plus(OPEN - 1))
                    c = At(C_MERGE + 2 * j, i, 4)
                    chunk_ready(c)
                    passes(4 * j, False, c, 0, KD, xh, xl, 0, True, True)
                    passes(4 * j + 1, False, c, KD, KD, xh, xl, 0, True, True).then_inc(chunk_done, 1)
                    c = At(C_MERGE + 2 * j + 1, i, 4)
                    chunk_ready(c)
                    pe.wait_ge(ysl_ready, KS)
                    passes(4 * j + 2, False, c, 0, KS, ysh, ysl, 0, True, True)
                    passes(4 * j + 3, False, c, KS, KD, yah, yal, 0, True, True).then_inc(chunk_done, 1)

            pe.wait_ge(mgl_ready, KD)
            with pe.Fori(0, KD // 4) as i:
                for j in (0, 1):
                    c = At(C_OUT + j, i, 2)
                    chunk_ready(c)
                    for t in (0, 1):
                        m = At(2 * j + t, i, 4)
                        pe.wait_ge(norms[2]["h_ready"], m.plus(OPEN - 1))
                        passes(2 * j + t, False, c, t * KD, KD, mgh, mgl, 0, True, True
                               ).then_inc(chunk_done if t else out_mm, 1)
            pe.wait_ge(norms[2]["h_ready"], KD + OPEN)

            ffn(1, C_UP2, C_DOWN2, False)

            pe.wait_ge(norms[3]["h_ready"], KD + OPEN)
            for m in range(KD):
                pe.wait_ge(norms[3]["xh_ready"], m + 1)
                if m == KD - 1:
                    pe.wait_ge(norms[3]["sum_ready"], KD + 1)
                    for t in range(5):
                        t0 = 0 if t == 0 else META + (t - 1) * P
                        ins = pe.matmul(PS[:, 7, 3 * P + t:3 * P + t + 1], ssum[:, t0:t0 + P], ones[:, 0:1],
                                        start=True, stop=True)
                    ins.then_inc(norms[3]["ssq_mm"], 1)
                for t in range(4):
                    if m == KD - 1 and t == 3:
                        pe.wait_ge(norms[3]["var_ready"], 1)
                    ins = pe.transpose(PS[:, 2 * t + m // 4, (m % 4) * P:(m % 4 + 1) * P],
                                       hg[:, m, t * P:(t + 1) * P], ident[:])
                    if m == KD - 1:
                        ins.then_inc(fin_mm, 1)

        @block.scalar
        def _(act):
            def tn(k):
                return prm[:, k]

            def split_hi(c):
                act.wait_ge(w_loaded[c.slot], c.loads())
                act.wait_ge(chunk_done, c.plus(OPEN - 1))
                act.activation(wh[:, c.slot], wraw[:, c.slot], ACT.Copy).then_inc(w_hi, 1)

            def norm_step(n, m, wide):
                s = norms[n]
                cols = slice(0, T) if wide else slice(META, T)
                mm = m.plus(0)
                h = hT[:, ds(mm, 1), cols].rearrange("p o n -> p (o n)")
                act.wait_ge(s["h_ready"], m.plus(1 + OPEN))
                act.wait_ge(s["sum_ready"], m.plus(1))
                act.activation(sq[:, cols], h, ACT.Square).then_inc(s["sq_ready"], 1)
                gain = gains[:, n, ds(mm, 1)]
                if n < 3:
                    o = xh[:, ds(mm, 1), cols].rearrange("p o n -> p (o n)")
                else:
                    o = hg[:, ds(mm, 1), :].rearrange("p o n -> p (o n)")
                act.activation(o, h, ACT.Copy, scale=gain).then_inc(s["xh_ready"], 1)

            def rstd_out(n):
                act.wait_ge(norms[n]["bcast_mm"], 1)
                act.activation(rstd_b[:, 0:META + 2 * P], PS[:, 6, 0:META + 2 * P], ACT.Copy)
                act.activation(rstd_b[:, META + 2 * P:T], PS[:, 7, 0:2 * P], ACT.Copy
                               ).then_inc(norms[n]["rstd_ready"], 1)

            def ffn(n, c_up, c_down, wide):
                s, g = ups[n], ffn_mem[n]
                w = T if wide else SEQ

                def up_step(c, f, with_norm):
                    b = f.base % 2
                    split_hi(c.at(1))
                    if with_norm:
                        rstd_out(2 * n)
                    act.wait_ge(s["gate_scaled"], f.plus(1 + OPEN))
                    t1 = g["t1"][:, b, 0:w]
                    act.activation(t1, t1, ACT.Silu).then_inc(s["silu_done"], 1)
                    act.wait_ge(s["gg_ready"], f.plus(1))
                    act.activation(g["gh"][:, ds(f.plus(0), 1), :].rearrange("p o n -> p (o n)"),
                                   g["t2"][:, b, 0:w], ACT.Copy).then_inc(s["gh_ready"], 1)

                for j in (0, 1):
                    up_step(At(c_up + j), At(j), j == 0)
                if n == 0:
                    for q, lam in enumerate((ssm_lam_re, ssm_lam_im)):
                        act.dma_start(lam_raw[:, q], lam[0].rearrange("d g p -> g d p")).then_inc(late_loaded, 16)
                    with nc.allow_non_contiguous_dma("64 numbers"):
                        act.dma_start(dt_raw, ssm_log_dt[0].rearrange("d g -> g d")).then_inc(late_loaded, 16)
                with act.Fori(1, KF // 2) as i:
                    for j in (0, 1):
                        up_step(At(c_up + j, i, 2), At(j, i, 2), False)
                if n == 0:
                    act.wait_ge(s["gl_ready"], KF)
                    act.wait_ge(lam_tr, 1)
                    act.activation(prm[:, LR:LI + 1].rearrange("p q g -> p (q g)"), PS[:, 2, 0:2 * GROUPS], ACT.Copy)
                    act.activation(tn(DT), PS[:, 2, 2 * GROUPS:3 * GROUPS], ACT.Exp).then_inc(act_small_done, 1)

                def down_steps(i):
                    for j in range(4):
                        last = i is None and j == 3 and n == 1
                        c, m = at_end(c_down, KD // 2, 4, j, i), at_end(0, KD // 2, 2, j // 2, i)
                        if not last:
                            split_hi(c.at(1))
                        if j % 2:
                            norm_step(2 * n + 1, m, wide)

                down_steps(0)
                if n == 0:
                    act.wait_ge(act_small, 1)
                    act.activation(tn(EXPA), tn(A_), ACT.Exp)
                    act.activation(tn(SINH), tn(RH), ACT.Sin)
                    act.activation(tn(SINR), tn(R_), ACT.Sin).then_inc(act_small_done, 1)
                with act.Fori(1, KD // 2 - 1) as i:
                    down_steps(i)
                down_steps(None)

            with nc.allow_non_contiguous_dma("gains, a few KB"):
                for n, g in enumerate((ffn1_norm[0], mix_norm[0], ffn2_norm[0], final_norm)):
                    act.dma_start(gains[:, n, :], g.rearrange("(k p) -> p k", p=P)).then_inc(const_loaded, 16)
                act.dma_start(dskip[:], ssm_d[0].rearrange("(k p) -> p k", p=P)).then_inc(const_loaded, 16)
            act.dma_start(negsink[:], attn_sink[0:1, :].to_broadcast([P, HEADS])).then_inc(late_loaded, 16)
            act.wait_ge(const_loaded, 80)

            for k in range(KD):
                norm_step(0, At(k), True)
                if k == 1:
                    split_hi(At(0))
            ffn(0, C_UP1, C_DOWN1, True)

            def c_transposed(i, bank, col):
                act.wait_ge(ct_mm, i + 1)
                act.activation(cT[:].rearrange("p a n -> p (a n)"), PS[:, bank, col:col + 2 * P], ACT.Copy
                               ).then_inc(ct_ev, 1)

            def input_to_state(i):
                act.wait_ge(w1t_mm, i + 1)
                for ri in (0, 1):
                    act.activation(w1[:, ri].rearrange("p (a g) n -> p a (g n)", a=2),
                                   PS[:, 2 * ri:2 * ri + 2, :], ACT.Copy).then_inc(w1_ev, 1)

            def gelu_factor(i):
                act.wait_ge(gelu_arg, i + 1)
                act.activation(arg, arg, ACT.Sigmoid, scale=2.0 * math.sqrt(2.0 / math.pi)
                               ).then_inc(gelu_exp, 1)

            def ssm_batch(i, first, more):
                act.wait_ge(sin_mm, i + 1)
                for ri in (0, 1):
                    for half in (0, 1):
                        part = slice(half * STATE, (half + 1) * STATE)
                        o = sin_[part, ri, :, ::-1] if half else sin_[part, ri]
                        for q in (0, 1):
                            act.activation(o[:, 4 * q:4 * q + 4, :],
                                           PS[part, 4 + 2 * ri + q, 0:4 * NCH].rearrange("p (g k) -> p g k", g=4),
                                           ACT.Copy).then_inc(sin_ev, 1)
                if not first:
                    gelu_factor(i - 1)
                if more:
                    c_transposed(i + 1, 2, 0)
                act.wait_ge(krow_mm, i + 1)
                act.activation(krow[:, :, 7 * CH:8 * CH], PS[0:CH, 1, 0:P].rearrange("p (g n) -> p g n", g=GB),
                               ACT.Copy).then_inc(krow_ev, 1)
                for q in range(4):
                    lag0 = 0 if q < 2 else 8
                    act.activation(krow[:, 4 * (q % 2):4 * (q % 2) + 4, lag0 * CH:(lag0 + 7) * CH],
                                   PS[0:CH, 4 + q, 0:28 * CH].rearrange("p (g n) -> p g n", g=4), ACT.Copy
                                   ).then_inc(krow_ev, 1)
                act.wait_ge(y_mm, i + 1)
                act.activation(Y.rearrange("p g k -> p (g k)"), PS[:, 0, :], ACT.Copy).then_inc(y_ev, 1)
                if more:
                    input_to_state(i + 1)

            split_hi(At(C_U + 1))
            c_transposed(0, 5, 0)
            rstd_out(1)
            act.sem_inc(pt_act, 1)
            act.sem_inc(yah_ready, OPEN)
            for j in range(4):
                split_hi(At(C_ATT + j))
            input_to_state(0)
            split_hi(At(C_ATT + 4))
            ssm_batch(0, True, True)
            with act.Fori(1, KS - 1) as i:
                ssm_batch(i, False, True)
            ssm_batch(KS - 1, False, False)

            def exps(a, gi):
                n, b = groups[gi]
                act.wait_ge(negm_ready, a * 8 + gi + 1)
                for r in range(QG):
                    tile = sc[:, gi % 2, r, 0:width(n)]
                    act.activation(tile, tile, ACT.Exp, bias=negm[:, gi % 2, r:r + 1],
                                   accum_out=rs[:, gi % 2, r:r + 1])
                act.activation(sk[:, gi % 2], sk[:, gi % 2], ACT.Exp).then_inc(exp_done, 1)

            def prob_tiles(a, gi):
                n, b = groups[gi]
                act.wait_ge(pv_mm, a * 8 + gi + 1)
                for r in (0, 2):
                    act.wait_ge(t_mm, a * 32 + (4 * gi + r + 1))
                    act.activation(pt[:, gi % 2, 0:blocks(n), r, :],
                                   PS[:, prob_bank(r), 0:blocks(n) * P].rearrange("p (j q) -> p j q", q=P), ACT.Copy
                                   ).then_inc(pt_act, 1)

            def result(a, gi):
                n, b = groups[gi]
                act.wait_ge(pv_mm, a * 8 + gi + 1 + OPEN)
                act.activation(yah[:, a * 4:a * 4 + QG, n * P:(n + 1) * P],
                               PS[:, 0 if n % 2 else 3, :].rearrange("p (r q) -> p r q", r=QG), ACT.Copy
                               ).then_inc(yah_ready, 1)

            for a in (0, 1):
                if a == 1:
                    for j in range(4):
                        split_hi(At(C_ATT + 5 + j))
                for gi in range(-1, last_group + 2):
                    if 0 <= gi <= last_group:
                        prob_tiles(a, gi)
                    if gi > 0 and groups[gi - 1][1] == 1:
                        result(a, gi - 1)
                    if gi < last_group:
                        exps(a, gi + 1)
                    if (a, gi) == (0, -1):
                        gelu_factor(KS - 1)

            act.wait_ge(z_ready, KS)
            for bt in range(KS):
                act.activation(zh[:, bt], uT[:, bt].rearrange("p s k -> p (s k)")[:, 0:SEQ], ACT.Copy
                               ).then_inc(zh_ready, 1)
            split_hi(At(C_MERGE))
            act.wait_ge(chunk_done, At(C_GLU).plus(1 + OPEN))
            for m in range(KS):
                if m >= 2:
                    act.wait_ge(ysf_ready, m - 1)
                act.activation(sig[:, m % 2], PS[:, m, :], ACT.Sigmoid).then_inc(glu_sig, 1)
                act.wait_ge(ysf_ready, m + 1)
                act.activation(ysh[:, m], ysf[:, m % 2], ACT.Copy).then_inc(ysh_ready, 1)

            with act.Fori(0, KD // 2) as i:
                for j in (0, 1):
                    m = At(j, i, 2)
                    split_hi(At(C_MERGE + 2 * j + 1, i, 4))
                    act.wait_ge(gates_scaled, m.plus(1))
                    gg = gsig[:, j].rearrange("p a n -> p (a n)")
                    act.activation(gg, gg, ACT.Sigmoid).then_inc(gates_sig, 1)
                    split_hi(At(C_MERGE + 2 * j + 2, i, 4))
                    act.wait_ge(mg_ready, m.plus(1 + OPEN))
                    act.activation(mgh[:, ds(m.plus(0), 1), :].rearrange("p o n -> p (o n)"), gsig[:, j, 0],
                                   ACT.Copy).then_inc(mgh_ready, 1)
            with act.Fori(0, KD // 4) as i:
                for j in (0, 1):
                    split_hi(At(C_OUT + j + 1, i, 2))
                    for t in (0, 1):
                        norm_step(2, At(2 * j + t, i, 4), False)
            ffn(1, C_UP2, C_DOWN2, False)
            for t in range(4):
                act.wait_ge(norms[3]["rcol_ready"], 1)
                act.wait_ge(fin_mm, t + 1)
                act.activation(y_nat[:, t, 0:512], PS[:, 2 * t, :], ACT.Copy, scale=rcol[:, t + 1:t + 2]
                               ).then_inc(fin_act, 1)

        @block.vector
        def _(ve):
            link = Chain(ve, chain_sem)

            def as_f32(ap):
                return ap.bitcast(F32)

            def split_lo(c):
                ve.wait_ge(w_hi, c.plus(1))
                ve.tensor_tensor(wl[:, c.slot], wraw[:, c.slot], as_f32(wh[:, c.slot]), ALU.subtract
                                 ).then_inc(w_lo, 1)

            def norm_step(n, m, wide):
                s = norms[n]
                cols = slice(0, T) if wide else slice(META, T)
                mm = m.plus(0)
                ve.wait_ge(s["sq_ready"], m.plus(1))
                ve.wait_ge(s["sum_ready"], m.plus(1))
                ve.tensor_tensor(ssum[:, cols], ssum[:, cols], sq[:, cols], ALU.add).then_inc(s["sum_ready"], 1)
                if n < 3:
                    ve.wait_ge(s["xh_ready"], m.plus(1))
                    h = hT[:, ds(mm, 1), cols].rearrange("p o n -> p (o n)")
                    hi = xh[:, ds(mm, 1), cols].rearrange("p o n -> p (o n)")
                    lo = xl[:, ds(mm, 1), cols].rearrange("p o n -> p (o n)")
                    ve.scalar_tensor_tensor(out=lo, in0=h, scalar=gains[:, n, ds(mm, 1)], in1=as_f32(hi),
                                            op0=ALU.mult, op1=ALU.subtract).then_inc(s["xl_ready"], 1)

            def norm_start(n):
                ve.memset(ssum[:], 0.0).then_inc(norms[n]["sum_ready"], 1)
                ve.sem_inc(norms[n]["h_ready"], OPEN)

            def token_var(n):
                s = norms[n]
                ve.wait_ge(s["ssq_mm"], 1)
                src = PS[:, 4, 0:5] if n < 3 else PS[:, 7, 3 * P:3 * P + 5]
                ve.tensor_scalar(var[:], src, 1.0 / D, EPS, ALU.mult, ALU.add).then_inc(s["var_ready"], 1)

            def token_diag(n):
                s = norms[n]
                ve.wait_ge(s["rcol_ready"], 1)
                if n == 0:
                    ve.wait_ge(dist_out, 16)
                for t in range(5):
                    ins = ve.tensor_scalar(diag[:, t, :], ident[:], rcol[:, t:t + 1], None, ALU.mult)
                ins.then_inc(s["diag_ready"], 1)

            def ffn(n, c_up, c_down, wide):
                s, g = ups[n], ffn_mem[n]
                w = T if wide else SEQ

                def shaped(row):
                    return row.rearrange("p (a n) -> p a n", a=2) if wide else row

                rstd = shaped(rstd_b[:]) if wide else rstd_b[:, META:T]

                def up_step(c, f, with_norm):
                    b = f.base % 2
                    gate_bank, up_bank = (4 * b, 4 * b + 2) if wide else (2 * b, 2 * b + 1)
                    t1, t2 = g["t1"][:, b, 0:w], g["t2"][:, b, 0:w]
                    if with_norm:
                        token_var(2 * n)
                        token_diag(2 * n)
                    split_lo(c.at(1))
                    if with_norm:
                        ve.wait_ge(norms[2 * n]["rstd_ready"], 1)
                    ve.wait_ge(s["gate_mm"], f.plus(1))
                    ve.tensor_tensor(shaped(t1), psum_of(gate_bank, wide), rstd, ALU.mult
                                     ).then_inc(s["gate_scaled"], 1)
                    ve.wait_ge(chunk_done, c.plus(1 + OPEN))
                    ve.tensor_tensor(shaped(t2), psum_of(up_bank, wide), rstd, ALU.mult
                                     ).then_inc(s["up_scaled"], 1)
                    ve.wait_ge(s["up_scaled"], f.plus(1 + OPEN))
                    ve.wait_ge(s["silu_done"], f.plus(1))
                    ve.tensor_tensor(t2, t1, t2, ALU.mult).then_inc(s["gg_ready"], 1)
                    ve.wait_ge(s["gh_ready"], f.plus(1))
                    ff = f.plus(0)
                    ve.tensor_tensor(g["gl"][:, ds(ff, 1), :].rearrange("p o n -> p (o n)"), t2,
                                     as_f32(g["gh"][:, ds(ff, 1), :].rearrange("p o n -> p (o n)")),
                                     ALU.subtract).then_inc(s["gl_ready"], 1)

                ve.sem_inc(s["gate_scaled"], OPEN)
                ve.sem_inc(s["up_scaled"], OPEN)
                for j in (0, 1):
                    up_step(At(c_up + j), At(j), j == 0)
                with ve.Fori(1, KF // 2) as i:
                    for j in (0, 1):
                        up_step(At(c_up + j, i, 2), At(j, i, 2), False)
                norm_start(2 * n + 1)

                def down_steps(i):
                    for j in range(4):
                        last = i is None and j == 3 and n == 1
                        c, m = at_end(c_down, KD // 2, 4, j, i), at_end(0, KD // 2, 2, j // 2, i)
                        if not last:
                            split_lo(c.at(1))
                        if j % 2:
                            ve.wait_ge(chunk_done, c.plus(1 + OPEN))
                            row = hT[:, ds(m.plus(0), 1), :].rearrange("p o n -> p (o n)")
                            h = tokens(row, wide)
                            ve.scalar_tensor_tensor(out=h, in0=psum_of(4 * (j // 2), wide), scalar=0.5, in1=h,
                                                    op0=ALU.mult, op1=ALU.add
                                                    ).then_inc(norms[2 * n + 1]["h_ready"], 1)
                            norm_step(2 * n + 1, m, wide)

                with ve.Fori(0, KD // 2 - 1) as i:
                    down_steps(i)
                down_steps(None)

            ve.sem_inc(w_lo, OPEN)
            norm_start(0)
            ve.wait_ge(dist_iota, 1)
            band = dist_made[:, META:DIST - META]
            ve.scalar_tensor_tensor(out=band, in0=band, scalar=-1.0, in1=band, op0=ALU.mult, op1=ALU.max
                                    ).then_inc(dist_abs, 1)
            ve.wait_ge(x_tr, 1)
            ve.tensor_copy(hT[:, :, 0:META], PS[:, 0, 0:KD * META].rearrange("p (k n) -> p k n", k=KD)
                           ).then_inc(meta_in, 1)
            ve.wait_ge(const_loaded, 80)
            for k in range(KD):
                ve.wait_ge(x_tr, k + 2)
                ve.tensor_copy(hT[:, k, META:T], PS[:, (k + 1) % 8, :]).then_inc(norms[0]["h_ready"], 1)
                if k > 0:
                    norm_step(0, At(k - 1), True)
                if k == 1:
                    split_lo(At(0))
            norm_step(0, At(KD - 1), True)
            ffn(0, C_UP1, C_DOWN1, True)

            def tt(o, x0, x1, op):
                link(ve.tensor_tensor(o, x0, x1, op))

            def ts(o, x0, s1, op0, s2=None, op1=None):
                if op1 is None:
                    link(ve.tensor_scalar(o, x0, s1, None, op0))
                else:
                    link(ve.tensor_scalar(o, x0, s1, s2, op0, op1))

            def stt(o, x0, s, x1, op0, op1):
                link(ve.scalar_tensor_tensor(out=o, in0=x0, scalar=s, in1=x1, op0=op0, op1=op1))

            def cmul(o, x0, x1, tmp, conj=False):
                ve.tensor_tensor(o[0], x0[0], x1[0], ALU.mult)
                ve.tensor_tensor(tmp[0], x0[1], x1[1], ALU.mult)
                ve.tensor_tensor(o[1], x0[0], x1[1], ALU.mult)
                tt(tmp[1], x0[1], x1[0], ALU.mult)
                ve.tensor_tensor(o[0], o[0], tmp[0], ALU.add if conj else ALU.subtract)
                tt(o[1], o[1], tmp[1], ALU.subtract if conj else ALU.add)

            F, B = slice(0, STATE), slice(STATE, P)
            big = [P, GB, CHUNK, CH]
            long = [t[:].rearrange("p a n -> p (a n)") for t in (ta, tb)]
            t4 = [t[:, 0:GB * P].rearrange("p (g s c) -> p g s c", g=GB, s=CHUNK) for t in long]

            def table(k):
                return [prm[:, k + 9 * q:k + 9 * q + 9] for q in (0, 1)]

            def input_kernels(i, again):
                gs = ds(i * GB, GB)
                if again:
                    ve.wait_ge(krow_mm, i)
                ve.wait_ge(ct_ev, i + 1)
                ve.wait_ge(ssm_in, i * 128 + 128)
                coef = [prm[:, k, gs].unsqueeze(2).to_broadcast([P, GB, CH]) for k in (CR, CI)]
                cmul([bb[:, 0], bb[:, 1]], coef, [b_raw[:, 0], b_raw[:, 1]],
                     [t[:, 0, 0:P].rearrange("p (g c) -> p g c", g=GB) for t in (ta, tb)])
                ts(bb[:, 2], bb[:, 1], -1.0, ALU.mult)
                cmul([w1t[:, 0], w1t[:, 1]],
                     [bpw[:, q, gs].unsqueeze(3).to_broadcast(big) for q in (0, 1)],
                     [bb[:, q].unsqueeze(2).to_broadcast(big) for q in (0, 1)], t4)
                ve.sem_inc(w1t_ready, 1)

            def phases(i):
                gs = ds(i * GB, GB)
                es = [P, GB, 9, 8]
                ua, ub = table(UA), table(UB)
                cmul([E[:, q].rearrange("p g (j l) -> p g j l", j=9) for q in (0, 1)],
                     [ua[q][:, :, gs].rearrange("p j g -> p g j").unsqueeze(3).to_broadcast(es) for q in (0, 1)],
                     [ub[q][:, 0:8, gs].rearrange("p l g -> p g l").unsqueeze(2).to_broadcast(es) for q in (0, 1)],
                     [t[:, 0:GB * 72].rearrange("p (g j l) -> p g j l", g=GB, j=9) for t in long])
                link(ve.tensor_copy(decay[:], prm[:, R8, gs].unsqueeze(2).to_broadcast([P, GB, NCH])))
                link(ve.memset(decay[:, :, 0:1], 0.0))

            def output_kernels(i, again):
                gs = ds(i * GB, GB)
                if again:
                    ve.wait_ge(state_mm, i)
                cmul([cp[:, 0], cp[:, 1]],
                     [cpw[:, q, gs].unsqueeze(3).to_broadcast(big) for q in (0, 1)],
                     [cT[:, q].rearrange("p (g c) -> p g c", g=GB).unsqueeze(2).to_broadcast(big) for q in (0, 1)],
                     t4)
                ve.sem_inc(kernels_ready, 1)

            def gelu_out(i):
                ve.wait_ge(gelu_exp, i + 1)
                zi = uT[:, ds(i, 1)].rearrange("p o s k -> p (o s k)")[:, 0:SEQ]
                ve.tensor_tensor(zi, y1, arg, ALU.mult).then_inc(z_ready, 1)

            def ssm_batch(i, first, more):
                def gk(t, q):
                    return t[:, q].rearrange("p (g k) -> p g k", g=GB)
                ve.wait_ge(sin_ev, i * 8 + 8)
                e = [E[:, q, :, 0:NCH] for q in (0, 1)]
                cmul([gk(ta, 0), gk(tb, 0)], e, [sin_[:, 0], sin_[:, 1]], [gk(ta, 1), gk(tb, 1)], conj=True)
                dk = decay[:].rearrange("p g k -> p (g k)")
                for q, t in ((0, ta), (1, tb)):
                    link(ve.tensor_tensor_scan(sin_[:, q].rearrange("p g k -> p (g k)"), dk, t[:, 0], 0.0,
                                               ALU.mult, ALU.add))
                ve.tensor_tensor(gk(ta, 0), e[0], sin_[:, 0], ALU.mult)
                ve.tensor_tensor(gk(ta, 1), e[1], sin_[:, 1], ALU.mult)
                ve.tensor_tensor(gk(tb, 0), e[0], sin_[:, 1], ALU.mult)
                tt(gk(tb, 1), e[1], sin_[:, 0], ALU.mult)
                for part, dst, src in ((F, slice(0, OCH), slice(1, OCH + 1)),
                                       (B, slice(OCH - 2, None, -1), slice(0, OCH - 1))):
                    ve.tensor_tensor(sx[part, 0, :, dst], gk(ta, 0)[part, :, src], gk(ta, 1)[part, :, src],
                                     ALU.subtract)
                    ins = ve.scalar_tensor_tensor(out=sx[part, 1, :, dst], in0=gk(tb, 0)[part, :, src], scalar=-1.0,
                                                  in1=gk(tb, 1)[part, :, src], op0=ALU.mult, op1=ALU.subtract)
                ins.then_inc(sx_ready, 1)
                ve.wait_ge(sx_ready, i + 1)
                if not first:
                    gelu_out(i - 1)
                if more:
                    input_kernels(i + 1, True)
                    phases(i + 1)
                    output_kernels(i + 1, True)
                    gelu_in(i, first)

            def gelu_in(i, first):
                ve.wait_ge(y_in, i * 128 + 128)
                if not first:
                    ve.wait_ge(z_ready, i)
                ui = uT[:, ds(i, 1)].rearrange("p o s k -> p (o s) k")
                def sk3(t):
                    return t.rearrange("p (s k) -> p s k", s=CHUNK)
                stt(sk3(y1), ui[:, :, MCH:NCH], dskip[:, ds(i, 1)], sk3(yT[:]), ALU.mult, ALU.add)
                tt(arg, y1, y1, ALU.mult)
                ts(arg, arg, 0.044715, ALU.mult, 1.0, ALU.add)
                ve.tensor_tensor(arg, arg, y1, ALU.mult).then_inc(gelu_arg, 1)

            ve.wait_ge(powers_ready, 1)
            ve.memset(sx[:], 0.0)
            link(ve.reciprocal(prm[:, DEN], prm[:, DEN]))
            tt(prm[:, CR], prm[:, CR], prm[:, DEN], ALU.mult)
            tt(prm[:, CI], prm[:, CI], prm[:, DEN], ALU.mult)
            pw = table(PW)
            for q in (0, 1):
                def place(dst, part, order):
                    return ve.tensor_copy(dst[part, q].rearrange("p g i -> p i g"), pw[q][part, order])
                place(cpw, F, slice(1, 9))
                place(cpw, B, slice(8, 0, -1))
                place(bpw, F, slice(7, None, -1))
                ins = place(bpw, B, slice(0, 8))
            link(ins)

            token_var(1)
            split_lo(At(C_U + 1))
            token_diag(1)
            ve.wait_ge(norms[1]["rstd_ready"], 1)
            for bt in range(KS):
                if bt == 2:
                    split_lo(At(C_ATT))
                    input_kernels(0, False)
                if bt % 2:
                    ve.wait_ge(chunk_done, At(C_U + bt // 2).plus(1 + OPEN))
                else:
                    ve.wait_ge(u_mm, bt // 2 + 1)
                for hf in (0, 1):
                    ins = ve.tensor_tensor(
                        uT[:, bt, :, hf * (NCH // 2):(hf + 1) * (NCH // 2)].rearrange("p s k -> p k s"),
                        PS[:, 2 * bt + hf, 0:HALF].rearrange("p (k s) -> p k s", s=CHUNK),
                        rstd_b[:, hf * HALF:(hf + 1) * HALF].rearrange("p (k s) -> p k s", s=CHUNK), ALU.mult)
                ins.then_inc(u_ready, 1)

            def projected(a):
                split_lo(At(C_ATT + 4 * a + 1))
                ve.wait_ge(chunk_done, At(C_ATT + 4 * a).plus(1 + OPEN))
                ve.tensor_tensor(kT[:].rearrange("p (h n) -> p h n", h=2), psum_of(4, True),
                                 rstd_b[:].rearrange("p (h n) -> p h n", h=2), ALU.mult).then_inc(proj_ev, 1)
                split_lo(At(C_ATT + 4 * a + 2))
                if a == 0:
                    phases(0)
                ve.wait_ge(chunk_done, At(C_ATT + 4 * a + 1).plus(1 + OPEN))
                for t in range(5):
                    ins = ve.tensor_scalar(vt[:, t, :], PS[:, 6 + t // 4, (t % 4) * P:(t % 4 + 1) * P],
                                           rcol[:, t:t + 1], None, ALU.mult)
                ins.then_inc(proj_ev, 1)
                split_lo(At(C_ATT + 4 * a + 3))
                if a == 0:
                    output_kernels(0, False)
                for r in range(QG):
                    if r % 2:
                        ve.wait_ge(chunk_done, At(C_ATT + 4 * a + 2 + r // 2).plus(1 + OPEN))
                    else:
                        ve.wait_ge(proj_mm, a * 2 + r // 2 + 1)
                    ve.scalar_tensor_tensor(out=qT[:, r, :], in0=PS[:, r, :], scalar=DH ** -0.5,
                                            in1=rstd_b[:, META:T], op0=ALU.mult, op1=ALU.mult
                                            ).then_inc(proj_ev, 1)
                    if r == 1:
                        split_lo(At(C_ATT + 4 * a + 4))

            projected(0)

            ssm_batch(0, True, True)
            with ve.Fori(1, KS - 1) as i:
                link.loop(i, SSM_STEPS, first=1)
                ssm_batch(i, False, True)
            link.end_loop(KS - 2)
            ssm_batch(KS - 1, False, False)

            ve.wait_ge(late_loaded, 64)
            ts(negsink[:], negsink[:], -1.0, ALU.mult)
            ve.wait_ge(dist_in, 16)
            ve.sem_inc(sc_done, OPEN)
            ve.sem_inc(pt_dve, 1)
            ve.sem_inc(yal_ready, OPEN)
            groups = [(n, b) for n in range(NBLK) for b in (0, 1)]
            def biased(a, gi, heads):
                n, b = groups[gi]
                d0 = META + P if n == 0 else 0
                for r in heads:
                    ve.wait_ge(s_mm, a * 32 + (4 * gi + r + 1))
                    h = a * 8 + QG * b + r
                    ve.scalar_tensor_tensor(out=sc[:, gi % 2, r, 0:width(n)], in0=dist[:, d0:d0 + width(n)],
                                            scalar=negslope[:, h:h + 1], in1=PS[:, 4 + r % 2, 0:width(n)],
                                            op0=ALU.mult, op1=ALU.add).then_inc(sc_done, 1)

            def maxima(a, gi):
                n, b = groups[gi]
                par = gi % 2
                ve.wait_ge(sc_done, a * 32 + (4 * gi + 4 + OPEN))
                link(ve.tensor_reduce(mx[:, par], sc[:, par, :, 0:width(n)], AX.X, ALU.max))
                nsk = negsink[:, a * 8 + QG * b:a * 8 + QG * b + QG]
                stt(negm[:, par], mx[:, par], -1.0, nsk, ALU.mult, ALU.min)
                ve.tensor_tensor(sk[:, par], negm[:, par], nsk, ALU.subtract).then_inc(negm_ready, 1)

            def normalised(a, gi):
                n, b = groups[gi]
                par = gi % 2
                ve.wait_ge(exp_done, a * 8 + gi + 1)
                tt(den[:, par], rs[:, par], sk[:, par], ALU.add)
                link(ve.reciprocal(den[:, par], den[:, par]))
                for r in range(QG):
                    tile = sc[:, par, r, 0:width(n)]
                    ins = ve.tensor_scalar(tile, tile, den[:, par, r:r + 1], None, ALU.mult)
                ins.then_inc(p_ready, 1)

            def prob_tiles(a, gi):
                n, b = groups[gi]
                ve.wait_ge(pv_mm, a * 8 + gi + 1)
                for r in (1, 3):
                    ve.wait_ge(t_mm, a * 32 + (4 * gi + r + 1))
                    ve.tensor_copy(pt[:, gi % 2, 0:blocks(n), r, :],
                                   PS[:, prob_bank(r), 0:blocks(n) * P].rearrange("p (j q) -> p j q", q=P)
                                   ).then_inc(pt_dve, 1)
                ve.tensor_copy(ptm[:, gi % 2].rearrange("p r q -> p (r q)"), PS[0:META, 2, :]
                               ).then_inc(pt_dve, 1)

            def result(a, gi):
                n, b = groups[gi]
                ve.wait_ge(yah_ready, a * 4 + (n + 1 + OPEN))
                rows = (slice(None), slice(a * 4, a * 4 + QG), slice(n * P, (n + 1) * P))
                ve.tensor_tensor(yal[rows], PS[:, 0 if n % 2 else 3, :].rearrange("p (r q) -> p r q", r=QG),
                                 as_f32(yah[rows]), ALU.subtract).then_inc(yal_ready, 1)

            for a in (0, 1):
                if a == 1:
                    projected(1)
                for gi in range(-1, last_group + 2):
                    if gi < last_group:
                        biased(a, gi + 1, (0, 1))
                    if 0 <= gi <= last_group:
                        normalised(a, gi)
                    if gi < last_group:
                        biased(a, gi + 1, (2, 3))
                        maxima(a, gi + 1)
                    if 0 <= gi <= last_group:
                        prob_tiles(a, gi)
                    if gi > 0 and groups[gi - 1][1] == 1:
                        result(a, gi - 1)
                    if (a, gi) == (0, -1):
                        gelu_in(KS - 1, False)
                    if (a, gi) == (0, 0):
                        gelu_out(KS - 1)

            def z_of(bt):
                return uT[:, bt].rearrange("p s k -> p (s k)")[:, 0:SEQ]
            for bt in range(KS):
                ve.wait_ge(zh_ready, bt + 1)
                ve.tensor_tensor(zl[:, bt], z_of(bt), as_f32(zh[:, bt]), ALU.subtract).then_inc(zl_ready, 1)
            split_lo(At(C_MERGE))
            for m in range(KS):
                ve.wait_ge(glu_sig, m + 1)
                if m >= 2:
                    ve.wait_ge(ysh_ready, m - 1)
                ve.tensor_tensor(ysf[:, m % 2].rearrange("p (k t) -> p t k", t=CHUNK),
                                 z_of(m).rearrange("p (t k) -> p t k", t=CHUNK),
                                 sig[:, m % 2].rearrange("p (t k) -> p t k", t=CHUNK), ALU.mult).then_inc(ysf_ready, 1)
                ve.wait_ge(ysh_ready, m + 1)
                ve.tensor_tensor(ysl[:, m], ysf[:, m % 2], as_f32(ysh[:, m]), ALU.subtract).then_inc(ysl_ready, 1)

            ve.sem_inc(mg_ready, OPEN)
            with ve.Fori(0, KD // 2) as i:
                link.loop(i, 2)
                for j in (0, 1):
                    m = At(j, i, 2)
                    split_lo(At(C_MERGE + 2 * j + 1, i, 4))
                    ve.wait_ge(chunk_done, At(C_MERGE + 2 * j, i, 4).plus(1 + OPEN))
                    for q in (0, 1):
                        ins = ve.tensor_tensor(gsig[:, j, q], PS[:, 4 * j + q, :], rstd_b[:, META:T], ALU.mult)
                    ins.then_inc(gates_scaled, 1)
                    split_lo(At(C_MERGE + 2 * j + 2, i, 4))
                    ve.wait_ge(gates_sig, m.plus(1))
                    ve.wait_ge(chunk_done, At(C_MERGE + 2 * j + 1, i, 4).plus(1 + OPEN))
                    ve.tensor_tensor(gsig[:, j, 0], gsig[:, j, 0], PS[:, 4 * j + 2, :], ALU.mult)
                    tt(gsig[:, j, 1], gsig[:, j, 1], PS[:, 4 * j + 3, :], ALU.mult)
                    ve.tensor_tensor(gsig[:, j, 0], gsig[:, j, 0], gsig[:, j, 1], ALU.add).then_inc(mg_ready, 1)
                    ve.wait_ge(mgh_ready, m.plus(1))
                    mm = m.plus(0)
                    ve.tensor_tensor(mgl[:, ds(mm, 1), :].rearrange("p o n -> p (o n)"), gsig[:, j, 0],
                                     as_f32(mgh[:, ds(mm, 1), :].rearrange("p o n -> p (o n)")), ALU.subtract
                                     ).then_inc(mgl_ready, 1)
            link.end_loop(KD // 2)

            norm_start(2)
            with ve.Fori(0, KD // 4) as i:
                for j in (0, 1):
                    split_lo(At(C_OUT + j + 1, i, 2))
                    for t in (0, 1):
                        m = At(2 * j + t, i, 4)
                        if t:
                            ve.wait_ge(chunk_done, At(C_OUT + j, i, 2).plus(1 + OPEN))
                        else:
                            ve.wait_ge(out_mm, At(j, i, 2).plus(1))
                        h = hT[:, ds(m.plus(0), 1), META:T].rearrange("p o n -> p (o n)")
                        ve.tensor_tensor(h, PS[:, 2 * j + t, :], h, ALU.add).then_inc(norms[2]["h_ready"], 1)
                        norm_step(2, m, False)
            ffn(1, C_UP2, C_DOWN2, False)
            token_var(3)
            ve.wait_ge(norms[3]["rcol_ready"], 1)
            for t in range(4):
                ve.wait_ge(fin_mm, t + 1)
                ve.tensor_scalar(y_nat[:, t, 512:1024], PS[:, 2 * t + 1, :], rcol[:, t + 1:t + 2], None, ALU.mult
                                 ).then_inc(fin_dve, 1)


_INS = ["x", "meta_tokens", "ffn1_norm", "ffn1_w_gate", "ffn1_w_up", "ffn1_w_down", "mix_norm", "w_in",
        "ssm_lam_re", "ssm_lam_im", "ssm_log_dt", "ssm_b_re", "ssm_b_im", "ssm_c_re", "ssm_c_im", "ssm_d",
        "ssm_w_glu", "attn_sink", "w_branch_ssm", "w_branch_attn", "w_out", "ffn2_norm", "ffn2_w_gate",
        "ffn2_w_up", "ffn2_w_down", "final_norm"]
_OUTS = [((1, 512, 1024), "float32")]


def kernel(**inputs):
    import numpy as _np
    import concourse.bacc as _bacc
    from concourse import mybir as _mybir
    from concourse.bass_utils import run_bass_kernel_spmd as _run

    nc = _bacc.Bacc("TRN2", target_bir_lowering=False, num_devices=1)
    arrays, args = {}, []
    for name in _INS:
        a = _np.ascontiguousarray(inputs[name])
        arrays[f"in_{name}_dram"] = a
        args.append(nc.dram_tensor(f"in_{name}_dram", a.shape, _mybir.dt.from_np(a.dtype), kind="ExternalInput").ap())
    for i, (shape, dtype) in enumerate(_OUTS):
        dt = _mybir.dt.from_np(_np.dtype(dtype))
        args.append(nc.dram_tensor(f"out_{i}_dram", shape, dt, kind="ExternalOutput").ap())
    build(nc, *args)
    r = _run(nc, [arrays], core_ids=[0])
    return r.results[0]["out_0_dram"]
```

```python
import math
from contextlib import ExitStack

import numpy as np

import concourse.bass as bass
from concourse import mybir

F32 = mybir.dt.float32
F32R = mybir.dt.float32r
ALU = mybir.AluOpType
ACT = mybir.ActivationFunctionType
AX = mybir.AxisListType

P = 128
D = 1024
KD = D // P
SEQ, META = 512, 16
T = META + SEQ
FF = 2816
KF = FF // P
HALF = T // 2
EPS = 1e-6
HEADS, KVH, DH, QG = 16, 4, 64, 4
WINDOW = 128
NBLK = SEQ // WINDOW
FAR = 3e32
GROUPS, STATE, CH = 32, 64, 16
SSM = GROUPS * CH
KS = SSM // P
GB = P // CH
CHUNK = 8
NCH = T // CHUNK
MCH = META // CHUNK
OCH = NCH - MCH
COL_Q, COL_K, COL_V = 0, HEADS * DH, (HEADS + KVH) * DH
COL_U = (HEADS + 2 * KVH) * DH
COL_GS = COL_U + SSM
COL_GA = COL_GS + D
GELU_CUBIC = 0.044715
DIST = 3 * WINDOW + 2 * META
TILES = 16
LOAD = 80
OPEN = 2

PW, UB, UA = 0, 18, 36
LR, LI, DT, A_, TH, NR, R_, RH, AC, E1, EXPA, SINH, COSM1, ER = range(UA, UA + 14)
CR, CI, R8, LBR, LBI, X_, DEN, COS, SINR, M0, M1, U2I = range(UA + 18, UA + 30)
PRM_ROWS = 66
SSM_STEPS = 17

C_UP1 = 0
C_DOWN1 = C_UP1 + KF
C_U = C_DOWN1 + 2 * KD
C_ATT = C_U + KS // 2
C_GATE0 = C_ATT + 8
C_GLU, C_GATE1, C_BRANCH0, C_BRANCH1 = range(C_GATE0 + 1, C_GATE0 + 5)
C_MERGE = C_BRANCH1 - 3
C_OUT = C_MERGE + 2 * KD
C_UP2 = C_OUT + KD // 2
C_DOWN2 = C_UP2 + KF


def tiles_in(c):
    first = c.base
    if C_DOWN1 <= first < C_U or C_DOWN2 <= first:
        return KF // 2
    if c.i is None and first in (C_ATT, C_ATT + 1, C_ATT + 4, C_ATT + 5):
        return KD
    return TILES


def split_two_pi():
    c1 = 6.28125
    c2 = math.floor((2 * math.pi - c1) * 2 ** 21) / 2 ** 21
    return c1, c2, 2 * math.pi - c1 - c2


class At:

    def __init__(self, base, i=None, stride=0):
        self.base, self.i, self.stride = base, i, stride

    def plus(self, n):
        return self.base + n if self.i is None else self.i * self.stride + (self.base + n)

    def at(self, n):
        return At(self.base + n, self.i, self.stride)

    @property
    def slot(self):
        return self.base % 2

    def loads(self):
        if self.i is None:
            return LOAD * (self.base // 2 + 1)
        return self.i * (LOAD * self.stride // 2) + LOAD * (self.base // 2 + 1)


def at_end(base, times, stride, n, i):
    return At(base + (times - 1) * stride + n) if i is None else At(base + n, i, stride)


class Chain:

    def __init__(self, eng, sem):
        self.eng, self.sem, self.base, self.n = eng, sem, 0, 0

    def __call__(self, ins):
        self.n += 1
        ins.then_inc(self.sem, 1)
        self.eng.wait_ge(self.sem, self.base + self.n)

    def loop(self, i, steps, first=0):
        self.start, self.n = self.n, self.n - first * steps
        self.base, self.steps, self.first = i * steps, steps, first

    def end_loop(self, times):
        done = self.n - self.start + self.first * self.steps
        assert done == self.steps, (done, self.steps)
        self.base, self.n = 0, self.start + times * self.steps


def build(nc, x, meta_tokens, ffn1_norm, ffn1_w_gate, ffn1_w_up, ffn1_w_down, mix_norm, w_in,
          ssm_lam_re, ssm_lam_im, ssm_log_dt, ssm_b_re, ssm_b_im, ssm_c_re, ssm_c_im, ssm_d,
          ssm_w_glu, attn_sink, w_branch_ssm, w_branch_attn, w_out, ffn2_norm, ffn2_w_gate,
          ffn2_w_up, ffn2_w_down, final_norm, out):
    ds = bass.ds

    with ExitStack() as ctx:
        def sb(name, shape, dt=F32, stack=ctx):
            return stack.enter_context(nc.sbuf_tensor(name, shape, dt))

        def sem(name):
            return ctx.enter_context(nc.semaphore(name))

        hT = sb("hT", [P, KD, T])
        with ExitStack() as sx_:
            xh = sb("xh", [P, KD, T], F32R, sx_)
            xl = sb("xl", [P, KD, T], F32R, sx_)
        final_area = sb("final_area", [P, 2 * KD * T])
        hg = final_area[:, 0:KD * SEQ].rearrange("p (k n) -> p k n", k=KD)
        y_nat = final_area[:, KD * T:KD * T + 4 * D].rearrange("p (t n) -> p t n", t=4)
        wraw = sb("wraw", [P, 2, TILES, P])
        wh = sb("wh", [P, 2, TILES, P], F32R)
        wl = sb("wl", [P, 2, TILES, P], F32R)
        ident = sb("ident", [P, P])
        ones = sb("ones", [P, P])
        gains = sb("gains", [P, 4, KD])
        dskip = sb("dskip", [P, GROUPS])
        ssum = sb("ssum", [P, T])
        sq = sb("sq", [P, T])
        rstd_b = sb("rstd_b", [P, T])
        rcol = sb("rcol", [P, 5])
        var = sb("var", [P, 5])
        expo = sb("expo", [P, 1])
        negslope = sb("negslope", [P, HEADS])
        negsink = sb("negsink", [P, HEADS])
        diag = sb("diag", [P, 5, P])
        PS = ctx.enter_context(nc.psum_tensor("PS", [P, 8, 512], F32))

        shared = sb("shared", [P, 4 * T])
        gate_buf = shared[:, 0:2 * T].rearrange("p (a n) -> p a n", a=2)
        up_buf = shared[:, 2 * T:4 * T].rearrange("p (a n) -> p a n", a=2)
        prm = shared[:, 0:PRM_ROWS * GROUPS].rearrange("p (r g) -> p r g", g=GROUPS)
        gsig = shared[:, 0:4 * SEQ].rearrange("p (j q n) -> p j q n", j=2, q=2)
        diag_row = diag[:].rearrange("p t n -> p (t n)")
        lam_raw = diag_row[0:GROUPS, 0:3 * 2 * STATE].rearrange("g (q d p) -> g q d p", q=3, d=2)
        dt_raw = diag_row[0:GROUPS, 3 * P:3 * P + 2]
        Z, y1, arg = diag_row[:, 0:SEQ], ssum[:, 0:SEQ], sq[:, 0:SEQ]
        dist_made, dist = diag_row[:, 0:DIST], shared[:, 0:DIST]
        power_tmp = [diag_row[:, (3 + q) * P:(4 + q) * P] for q in (0, 1)]

        with ExitStack() as s0:
            x_nat = sb("x_nat", [P, 4, D], stack=s0)
            m_nat = sb("m_nat", [META, D], stack=s0)
        ffn_mem = []
        for n in (1, 2):
            with ExitStack() as s1:
                ffn_mem.append(dict(
                    gh=sb(f"g_hi{n}", [P, KF, T if n == 1 else SEQ], F32R, s1),
                    gl=sb(f"g_lo{n}", [P, KF, T if n == 1 else SEQ], F32R, s1), t1=gate_buf, t2=up_buf))
        with ExitStack() as s2:
            uT = sb("uT", [P, KS, CHUNK, NCH], stack=s2)
            with ExitStack() as s3:
                cp = sb("cp", [P, 2, GB, CHUNK, CH], stack=s3)
                toep = sb("toep", [P, GB, P], stack=s3)
                U = sb("U", [P, GB, NCH], stack=s3)
                sx = sb("sx", [P, 2, GB, OCH], stack=s3)
                d_diag = sb("d_diag", [P, GB, CH], stack=s3)
                krow = sb("krow", [CH, GB, 15 * CH], stack=s3)
                bb = sb("bb", [P, 3, GB, CH], stack=s3)
                cT = sb("cT", [P, 2, P], stack=s3)
                c_raw = sb("c_raw", [P, 2, P], stack=s3)
                b_raw = sb("b_raw", [P, 2, GB, CH], stack=s3)
                cpw = sb("cpw", [P, 2, GROUPS, CHUNK], stack=s3)
                bpw = sb("bpw", [P, 2, GROUPS, CHUNK], stack=s3)
                w1t = sb("w1t", [P, 2, GB, CHUNK, CH], stack=s3)
                w1 = sb("w1", [P, 2, GB, P], stack=s3)
                E = sb("E", [P, 2, GB, 72], stack=s3)
                decay = sb("decay", [P, GB, NCH], stack=s3)
                sin_ = sb("sin_", [P, 2, GB, NCH], stack=s3)
                ta = sb("ta", [P, 2, GB * NCH], stack=s3)
                tb = sb("tb", [P, 2, GB * NCH], stack=s3)
                kT = sb("kT", [P, T], stack=s3)
                vt = sb("vt", [P, 5, P], stack=s3)
                qT = sb("qT", [P, QG, SEQ], stack=s3)
                vT = qT[:].rearrange("p r n -> p (r n)")[:, 2 * SEQ:2 * SEQ + T]
            yah = sb("yah", [P, KD, SEQ], F32R, s2)
            yal = sb("yal", [P, KD, SEQ], F32R, s2)
            with ExitStack() as s3:
                sc = sb("sc", [P, 2, QG, META + 3 * WINDOW], stack=s3)
                mx = sb("mx", [P, 2, QG], stack=s3)
                negm = sb("negm", [P, 2, QG], stack=s3)
                sk = sb("sk", [P, 2, QG], stack=s3)
                den = sb("den", [P, 2, QG], stack=s3)
                rs = sb("rs", [P, 2, QG], stack=s3)
                pt = sb("pt", [P, 2, 3, QG, P], stack=s3)
                ptm = sb("ptm", [META, 2, QG, P], stack=s3)
            ysh = sb("ysh", [P, KS, SEQ], F32R, s2)
            ysl = sb("ysl", [P, KS, SEQ], F32R, s2)
            with ExitStack() as s3:
                zh = sb("zh", [P, KS, SEQ], F32R, s3)
                zl = sb("zl", [P, KS, SEQ], F32R, s3)
                sig = sb("sig", [P, 2, SEQ], stack=s3)
                ysf = sb("ysf", [P, 2, SEQ], stack=s3)
            with ExitStack() as s3:
                mgh = sb("mgh", [P, KD, SEQ], F32R, s3)
                mgl = sb("mgl", [P, KD, SEQ], F32R, s3)

        u_dram = nc.dram_tensor("u_regroup", [KS, GB, CH, CHUNK, NCH], F32, kind="Internal").ap()
        z_dram = nc.dram_tensor("z_regroup", [KS, CHUNK, CH, GB, OCH], F32, kind="Internal").ap()
        dist_dram = nc.dram_tensor("dist", [P, DIST], F32, kind="Internal").ap()

        x_loaded, const_loaded, consts_made = sem("x_loaded"), sem("const_loaded"), sem("consts_made")
        w_loaded = [sem("w_loaded0"), sem("w_loaded1")]
        w_hi, w_lo, chunk_done = sem("w_hi"), sem("w_lo"), sem("chunk_done")
        chain_sem, pool_chain = sem("dve_chain"), sem("pool_chain")
        x_late = sem("x_late")
        x_tr = sem("x_transposed")
        meta_in = sem("meta_in")
        dist_iota, dist_abs, dist_ready = sem("dist_iota"), sem("dist_abs"), sem("dist_ready")
        v_tr = sem("v_transposed")
        dist_out, dist_in = sem("dist_out"), sem("dist_in")
        late_loaded = sem("late_loaded")
        sp_paced = sem("sp_paced")
        norms = [{k: sem(f"{k}_{n}") for k in ("h_ready", "sq_ready", "xh_ready", "sum_ready", "xl_ready",
                                               "ssq_mm", "var_ready", "rcol_ready", "diag_ready",
                                               "bcast_mm", "rstd_ready")} for n in range(4)]
        ups = [{k: sem(f"{k}_{n}") for k in ("gate_mm", "gate_scaled", "silu_done", "up_scaled",
                                             "gg_ready", "gh_ready", "gl_ready")} for n in (1, 2)]
        out_mm = sem("out_mm")
        u_mm, u_ready = sem("u_mm"), sem("u_ready")
        lam_tr, powers_ready = sem("lam_tr"), sem("powers_ready")
        act_small, act_small_done = sem("act_small"), sem("act_small_done")
        lam_dt = sem("lam_dt")
        u_out, z_out, state_mm = sem("u_out"), sem("z_out"), sem("state_mm")
        (ssm_in, ct_mm, ct_ev, kernels_ready, krow_mm, krow_ev, w1t_ready, w1t_mm, w1_ev, toep_in, u_in,
         sin_mm, sin_ev, sx_ready, y_mm, y_ev, z_in, gelu_arg, gelu_exp, z_ready) = (sem(n) for n in (
            "ssm_in", "ct_mm", "ct_ev", "kernels_ready", "krow_mm", "krow_ev", "w1t_ready", "w1t_mm", "w1_ev",
            "toep_in", "u_in", "sin_mm", "sin_ev", "sx_ready", "y_mm", "y_ev", "z_in", "gelu_arg",
            "gelu_exp", "z_ready"))
        (proj_mm, proj_ev, s_mm, sc_done, negm_ready, exp_done, p_ready, t_mm, pt_act, pt_dve, pv_mm,
         yah_ready, yal_ready) = (sem(n) for n in (
            "proj_mm", "proj_ev", "s_mm", "sc_done", "negm_ready", "exp_done", "p_ready", "t_mm", "pt_act",
            "pt_dve", "pv_mm", "yah_ready", "yal_ready"))
        zh_ready, zl_ready, glu_mm, glu_sig, ysf_ready, ysh_ready, ysl_ready = (sem(n) for n in (
            "zh_ready", "zl_ready", "glu_mm", "glu_sig", "ysf_ready", "ysh_ready", "ysl_ready"))
        gates_mm, branch_mm, gates_scaled, gates_sig, mg_ready, mgh_ready, mgl_ready = (sem(n) for n in (
            "gates_mm", "branch_mm", "gates_scaled", "gates_sig", "mg_ready", "mgh_ready", "mgl_ready"))
        hg_ready, fin_mm, fin_act, fin_dve, stored = (sem(n) for n in (
            "hg_ready", "fin_mm", "fin_act", "fin_dve", "stored"))

        block = ctx.enter_context(nc.Block())

        def halves(base_bank, wide):
            if wide:
                return [(PS[:, base_bank + a, 0:HALF], slice(a * HALF, (a + 1) * HALF)) for a in (0, 1)]
            return [(PS[:, base_bank, 0:SEQ], slice(META, T))]

        def psum_of(bank, wide):
            return PS[:, bank:bank + 2, 0:HALF] if wide else PS[:, bank, 0:SEQ]

        def tokens(row, wide):
            return row.rearrange("p (a n) -> p a n", a=2) if wide else row[:, META:T]

        def y_bank(more):
            return 4 if more else 0

        def x_bank(k):
            return k + 1 if k < KD - 1 else 2

        groups = [(n, b) for n in range(NBLK) for b in (0, 1)]
        last_group = len(groups) - 1

        def blocks(n):
            return 2 if n in (0, NBLK - 1) else 3

        def width(n):
            return META + blocks(n) * P

        def band_at(n):
            return (0, blocks(n) * P) if n == 0 else (META, 0)

        def merge_bank(m):
            return 4 - 4 * (m % 2)

        def q_bank(r):
            return (0, 1, 6, 7)[r]

        def prob_bank(r):
            return (6, 7, 1, 6)[r]

        @block.sync
        def _(sp):
            def weight_chunk(c, parts, settle=False):
                sp.wait_ge(w_lo, c.plus(OPEN - 1))
                if settle:
                    sp.sem_inc(sp_paced, 1)
                for n, (dst, src) in enumerate(parts):
                    inc = 16 if n + 1 < len(parts) else LOAD - 16 * n
                    sp.dma_start(dst, src).then_inc(w_loaded[c.slot], inc)

            def kview(w):
                return w.rearrange("(k p) n -> p k n", p=P)

            def tiles_of(c, t0, w, col):
                nk = w.shape[0] // P
                return wraw[:, c.slot, t0:t0 + nk, :], kview(w)[:, :, ds(col, P)]

            def ffn_stream(c_up, c_down, wg, wu, wd):
                with sp.Fori(0, KF // 2) as i:
                    for j in (0, 1):
                        c, col = At(c_up + j, i, 2), i * (2 * P) + j * P
                        weight_chunk(c, [tiles_of(c, 0, wg, col), tiles_of(c, KD, wu, col)])
                with sp.Fori(0, KD // 2) as i:
                    for j in range(4):
                        c = At(c_down + j, i, 4)
                        k0 = (j % 2) * (KF // 2)
                        src = kview(wd)[:, k0:k0 + KF // 2, ds(i * (2 * P) + (j // 2) * P, P)]
                        weight_chunk(c, [(wraw[:, c.slot, 0:6, :], src[:, 0:6, :]),
                                         (wraw[:, c.slot, 6:11, :], src[:, 6:11, :])])

            sp.dma_start(m_nat[:], meta_tokens).then_inc(x_loaded, 16)
            for half, done in ((slice(0, D // 2), x_loaded), (slice(D // 2, D), x_late)):
                sp.dma_start(x_nat[:, :, half], x[0].rearrange("(t p) n -> p t n", p=P)[:, :, half]
                             ).then_inc(done, 16)
            sp.wait_ge(dist_ready, 1)
            sp.dma_start(dist_dram, dist_made).then_inc(dist_out, 16)
            ffn_stream(C_UP1, C_DOWN1, ffn1_w_gate[0], ffn1_w_up[0], ffn1_w_down[0])
            win = w_in[0]
            for j in range(KS // 2):
                c, col = At(C_U + j), COL_U + 2 * j * P
                weight_chunk(c, [tiles_of(c, 0, win, col), tiles_of(c, KD, win, col + P)])

            def att_chunk(a, j):
                c = At(C_ATT + 4 * a + j)
                if j < 2:
                    weight_chunk(c, [tiles_of(c, 0, win, (COL_K, COL_V)[j] + a * P)])
                else:
                    weight_chunk(c, [
                        (wraw[:, c.slot, t * KD:(t + 1) * KD, b * DH:(b + 1) * DH],
                         kview(win)[:, :, ds((2 * QG * a + b * QG + 2 * (j - 2) + t) * DH, DH)])
                        for t in (0, 1) for b in (0, 1)])

            def state_params(i):
                for ri, c_par in enumerate((ssm_c_re, ssm_c_im)):
                    for dr in (0, 1):
                        sp.dma_start(c_raw[:, ri, dr * STATE:(dr + 1) * STATE],
                                     c_par[0, dr].rearrange("g c p -> (g c) p")[ds(i * P, P), :]
                                     ).then_inc(ssm_in, 16)
                for ri, b_par in enumerate((ssm_b_re, ssm_b_im)):
                    for dr in (0, 1):
                        sp.dma_start(b_raw[dr * STATE:(dr + 1) * STATE, ri],
                                     b_par[0, dr].rearrange("g p c -> p g c")[:, ds(i * GB, GB), :]
                                     ).then_inc(ssm_in, 16)

            sp.wait_ge(chunk_done, C_U + OPEN)
            state_params(0)
            for j in range(3):
                att_chunk(0, j)
            sp.wait_ge(u_ready, KS)
            sp.dma_start(u_dram.rearrange("b g c s k -> (g c) b (s k)"),
                         uT[:].rearrange("p b s k -> p b (s k)")).then_inc(u_out, 16)

            def load_u(i):
                for s in range(CHUNK):
                    sp.dma_start(U[s * CH:(s + 1) * CH, :, :],
                                 u_dram[ds(i, 1)].rearrange("o g c s k -> s c (o g) k")[s]).then_inc(u_in, 16)

            def store_z(i):
                sp.wait_ge(z_ready, i + 1)
                sp.sem_inc(sp_paced, 1)
                sp.dma_start(z_dram[ds(i, 1)].rearrange("o t c g k -> (o t c) (g k)"), Z).then_inc(z_out, 16)

            def load_z(i):
                sp.wait_ge(z_out, i * 16 + 32)
                sp.sem_inc(sp_paced, 1)
                for g in range(GB):
                    o = uT[g * CH:(g + 1) * CH, ds(i, 1)].rearrange("c o s k -> c (o s k)")[:, 0:SEQ]
                    sp.dma_start(o.rearrange("c (t k) -> c t k", t=CHUNK),
                                 z_dram[ds(i, 1)].rearrange("o t c g k -> g c (o t) k")[g]).then_inc(z_in, 16)

            def ssm_batch(i, first, more):
                if more:
                    sp.wait_ge(kernels_ready, i + 1)
                    sp.sem_inc(sp_paced, 1)
                    state_params(i + 1)
                else:
                    sp.wait_ge(kernels_ready, KS)
                    sp.wait_ge(dist_out, 16)
                    sp.dma_start(dist, dist_dram).then_inc(dist_in, 16)
                sp.wait_ge(krow_ev, i * 5 + 5)
                for s in range(CHUNK):
                    c0 = (CHUNK - 1 - s) * CH
                    sp.dma_start(toep[s * CH:(s + 1) * CH, :, :], krow[:, :, c0:c0 + P]).then_inc(toep_in, 16)
                if not first:
                    store_z(i - 1)
                if more:
                    sp.wait_ge(y_mm, i + 1)
                    sp.sem_inc(sp_paced, 1)
                    load_u(i + 1)
                if not first:
                    load_z(i - 1)

            sp.wait_ge(u_out, 16)
            load_u(0)
            att_chunk(0, 3)
            att_chunk(1, 0)
            att_chunk(1, 1)
            ssm_batch(0, True, True)
            with sp.Fori(1, KS - 1) as i:
                ssm_batch(i, False, True)
            ssm_batch(KS - 1, False, False)
            store_z(KS - 1)
            load_z(KS - 1)
            att_chunk(1, 2)
            att_chunk(1, 3)
            def gates_chunk(c, col):
                weight_chunk(c, [tiles_of(c, 0, win, col + COL_GS), tiles_of(c, KD, win, col + COL_GA)])

            def branch_chunk(c, col):
                wa = w_branch_attn[0].rearrange("(a b r d) n -> a b d r n", a=2, b=2, r=QG)
                weight_chunk(c, [tiles_of(c, 0, w_branch_ssm[0], col)] + [
                    (wraw[b * DH:(b + 1) * DH, c.slot, KS + a * QG:KS + (a + 1) * QG, :],
                     wa[a, b][:, :, ds(col, P)]) for a in (0, 1) for b in (0, 1)], settle=True)

            gates_chunk(At(C_GATE0), 0)
            c = At(C_GLU)
            weight_chunk(c, [(wraw[:, c.slot, m * KS:(m + 1) * KS, :],
                              kview(ssm_w_glu[0])[:, :, m * P:(m + 1) * P]) for m in range(KS)])
            gates_chunk(At(C_GATE1), P)
            branch_chunk(At(C_BRANCH0), 0)
            branch_chunk(At(C_BRANCH1), P)
            with sp.Fori(1, KD // 2) as i:
                col_end = sp.snap(i * (2 * P) + 2 * P)
                for j in (0, 1):
                    col = col_end + (j - 2) * P
                    gates_chunk(At(C_MERGE + 2 * j, i, 4), col)
                    branch_chunk(At(C_MERGE + 2 * j + 1, i, 4), col)
            with sp.Fori(0, KD // 4) as i:
                for j in (0, 1):
                    c, col = At(C_OUT + j, i, 2), i * (4 * P) + j * 2 * P
                    weight_chunk(c, [tiles_of(c, 0, w_out[0], col), tiles_of(c, KD, w_out[0], col + P)])
            ffn_stream(C_UP2, C_DOWN2, ffn2_w_gate[0], ffn2_w_up[0], ffn2_w_down[0])

            for t in range(4):
                sp.wait_ge(fin_act, t + 1)
                sp.wait_ge(fin_dve, t + 1)
                sp.dma_start(out[0, t * P:(t + 1) * P, :], y_nat[:, t, :]).then_inc(stored, 16)
            sp.wait_ge(stored, 64)

        @block.gpsimd
        def _(pool):
            pool.memset(dskip[:], 0.0)
            pool.memset(ident[:], 0.0).then_inc(consts_made, 1)
            pool.memset(ones[:], 1.0).then_inc(consts_made, 1)
            pool.memset(expo[:], -0.5).then_inc(consts_made, 1)
            pool.wait_ge(consts_made, 3)
            pool.affine_select(out=ident[:], in_=ident[:], compare_op=ALU.not_equal, fill=1.0, base=0,
                               pattern=[[-1, P]], channel_multiplier=1).then_inc(consts_made, 1)

            for h in range(HEADS):
                pool.memset(negslope[:, h:h + 1], -float(np.float32(2.0 ** (-8.0 * (h + 1) / HEADS))))
            pool.memset(dist_made[:, 0:META], 0.0)
            pool.memset(dist_made[:, DIST - META:DIST], 0.0)
            band = dist_made[:, META:DIST - META]
            pool.iota(band, pattern=[[-1, 3 * WINDOW]], base=WINDOW, channel_multiplier=1,
                      allow_small_or_imprecise_dtypes=True).then_inc(dist_iota, 1)
            pool.wait_ge(dist_abs, 1)
            pool.affine_select(out=band, in_=band, compare_op=ALU.is_ge, fill=FAR, base=0,
                               pattern=[[1, 3 * WINDOW]], channel_multiplier=-1).then_inc(dist_iota, 1)
            pool.wait_ge(dist_iota, 2)
            pool.affine_select(out=band, in_=band, compare_op=ALU.is_ge, fill=FAR, base=2 * WINDOW,
                               pattern=[[-1, 3 * WINDOW]], channel_multiplier=1).then_inc(dist_ready, 1)

            def token_rstd(n):
                pool.wait_ge(norms[n]["var_ready"], 1)
                pool.tensor_tensor(rcol[:], var[:], expo[:].to_broadcast([P, 5]), ALU.pow
                                   ).then_inc(norms[n]["rcol_ready"], 1)

            def tt(o, x0, x1, op):
                step(pool.tensor_tensor(o, x0, x1, op))

            def ts(o, x0, s1, op0, s2=None, op1=None):
                if op1 is None:
                    step(pool.tensor_scalar(o, x0, s1, None, op0))
                else:
                    step(pool.tensor_scalar(o, x0, s1, s2, op0, op1))

            def cmul(o, x0, x1, tmp):
                pool.tensor_tensor(o[0], x0[0], x1[0], ALU.mult)
                pool.tensor_tensor(tmp[0], x0[1], x1[1], ALU.mult)
                pool.tensor_tensor(o[1], x0[0], x1[1], ALU.mult)
                tt(tmp[1], x0[1], x1[0], ALU.mult)
                pool.tensor_tensor(o[0], o[0], tmp[0], ALU.subtract)
                tt(o[1], o[1], tmp[1], ALU.add)

            def tn(k):
                return prm[:, k]

            def powers(tab, re, im):
                pool.memset(tn(tab), 1.0)
                pool.memset(tn(tab + 9), 0.0)
                pool.tensor_copy(tn(tab + 1), re)
                step(pool.tensor_copy(tn(tab + 10), im))
                for w in (1, 2, 4):
                    o = [prm[:, q + w + 1:q + 2 * w + 1] for q in (tab, tab + 9)]
                    lo = [prm[:, q + 1:q + w + 1] for q in (tab, tab + 9)]
                    top = [prm[:, q + w:q + w + 1].to_broadcast([P, w, GROUPS]) for q in (tab, tab + 9)]
                    cmul(o, lo, top, [t[:, 0:w * GROUPS].rearrange("p (w g) -> p w g", w=w) for t in power_tmp])

            token_rstd(0)

            step = Chain(pool, pool_chain)
            pool.wait_ge(late_loaded, 64)
            pool.tensor_copy(lam_raw[:, 2], dt_raw.unsqueeze(2).to_broadcast([GROUPS, 2, STATE])
                             ).then_inc(lam_dt, 1)
            pool.wait_ge(act_small_done, 1)
            c1, c2, c3 = split_two_pi()
            tt(tn(A_), tn(LR), tn(DT), ALU.mult)
            tt(tn(TH), tn(LI), tn(DT), ALU.mult)
            ts(tn(NR), tn(TH), 1.0 / (2.0 * math.pi), ALU.mult, 12582912.0, ALU.add)
            ts(tn(NR), tn(NR), 12582912.0, ALU.subtract)
            for c, src in ((c1, TH), (c2, R_), (c3, R_)):
                ts(tn(RH), tn(NR), -c, ALU.mult)
                tt(tn(R_), tn(RH), tn(src), ALU.add)
            ts(tn(R_), tn(R_), 3.1415925, ALU.min, -3.1415925, ALU.max)
            pool.tensor_scalar(tn(RH), tn(R_), 0.5, None, ALU.mult).then_inc(act_small, 1)
            ts(tn(AC), tn(A_), 0.35, ALU.min, -0.35, ALU.max)
            ts(tn(E1), tn(AC), 1.0 / 8.0, ALU.mult, 1.0, ALU.add)
            for q in range(7, 1, -1):
                tt(tn(E1), tn(E1), tn(AC), ALU.mult)
                ts(tn(E1), tn(E1), 1.0 / q, ALU.mult, 1.0, ALU.add)
            tt(tn(E1), tn(E1), tn(AC), ALU.mult)
            ts(tn(M0), tn(A_), 0.35, ALU.is_le)
            ts(tn(M1), tn(A_), -0.35, ALU.is_ge)
            tt(tn(M0), tn(M0), tn(M1), ALU.mult)
            ts(tn(M1), tn(M0), -1.0, ALU.mult, 1.0, ALU.add)
            pool.wait_ge(act_small_done, 2)
            ts(tn(EXPA), tn(EXPA), 1.0, ALU.subtract)
            tt(tn(EXPA), tn(EXPA), tn(M1), ALU.mult)
            tt(tn(E1), tn(E1), tn(M0), ALU.mult)
            tt(tn(E1), tn(E1), tn(EXPA), ALU.add)
            tt(tn(COSM1), tn(SINH), tn(SINH), ALU.mult)
            ts(tn(COSM1), tn(COSM1), -2.0, ALU.mult)
            ts(tn(COS), tn(COSM1), 1.0, ALU.add)
            ts(tn(ER), tn(E1), 1.0, ALU.add)
            tt(tn(LBR), tn(ER), tn(COS), ALU.mult)
            tt(tn(LBI), tn(ER), tn(SINR), ALU.mult)
            tt(tn(X_), tn(E1), tn(COS), ALU.mult)
            tt(tn(X_), tn(X_), tn(COSM1), ALU.add)
            tt(tn(DEN), tn(LR), tn(LR), ALU.mult)
            tt(tn(M0), tn(LI), tn(LI), ALU.mult)
            tt(tn(DEN), tn(DEN), tn(M0), ALU.add)
            tt(tn(CR), tn(X_), tn(LR), ALU.mult)
            tt(tn(M0), tn(LBI), tn(LI), ALU.mult)
            tt(tn(CR), tn(CR), tn(M0), ALU.add)
            tt(tn(CI), tn(LBI), tn(LR), ALU.mult)
            tt(tn(M0), tn(X_), tn(LI), ALU.mult)
            tt(tn(CI), tn(CI), tn(M0), ALU.subtract)
            tt(tn(R8), tn(ER), tn(ER), ALU.mult)
            tt(tn(R8), tn(R8), tn(R8), ALU.mult)
            tt(tn(R8), tn(R8), tn(R8), ALU.mult)
            powers(PW, tn(LBR), tn(LBI))
            u1, u2, tmp = [tn(COS), tn(SINR)], [tn(X_), tn(U2I)], [tn(M0), tn(M1)]
            cmul(u2, u1, u1, tmp)
            cmul(u1, u2, u2, tmp)
            cmul(u2, u1, u1, tmp)
            powers(UB, u2[0], u2[1])
            powers(UA, tn(UB + 8), tn(UB + 17))
            pool.sem_inc(powers_ready, 1)

            token_rstd(1)
            token_rstd(2)
            token_rstd(3)

        @block.tensor
        def _(pe):
            def passes(bank, wide, c, t0, nk, hi, lo, k0, first, last, wait_k=None):
                outs = halves(bank, wide)
                for k in range(nk):
                    if wait_k is not None:
                        pe.wait_ge(wait_k, k + 1)
                    todo = ((wh, hi), (wh, lo), (wl, hi))
                    for n, (w, xt) in enumerate(todo):
                        for ps, tok in outs:
                            if xt.shape[-1] == SEQ:
                                tok = slice(0, SEQ)
                            ins = pe.matmul(ps, w[:, c.slot, t0 + k, :], xt[:, k0 + k, tok],
                                            start=first and k == 0 and n == 0,
                                            stop=last and k == nk - 1 and n == 2)
                return ins

            def chunk_ready(c):
                pe.wait_ge(w_hi, c.plus(1))
                pe.wait_ge(w_lo, c.plus(1 + OPEN))

            def sum_squares(n):
                s = norms[n]
                pe.wait_ge(s["sum_ready"], KD + 1)
                for t in range(5):
                    t0 = 0 if t == 0 else META + (t - 1) * P
                    ins = pe.matmul(PS[:, 4, t:t + 1], ssum[:, t0:t0 + P], ones[:, 0:1], start=True, stop=True)
                ins.then_inc(s["ssq_mm"], 1)

            def spread_rstd(n):
                s = norms[n]
                pe.wait_ge(s["diag_ready"], 1)
                pe.matmul(PS[:, 6, 0:META], ones[0:META, :], diag[0:META, 0, 0:META], start=True, stop=True)
                for t in range(1, 5):
                    o = PS[:, 6, META + (t - 1) * P:META + t * P] if t < 3 else PS[:, 7, (t - 3) * P:(t - 2) * P]
                    ins = pe.matmul(o, ones[:], diag[:, t, :], start=True, stop=True)
                ins.then_inc(s["bcast_mm"], 1)

            def up_chunk(c, n, f, wide, with_norm):
                s = ups[n]
                chunk_ready(c)
                b = f.base % 2
                gate_bank, up_bank = (4 * b, 4 * b + 2) if wide else (2 * b, 2 * b + 1)
                pe.wait_ge(s["gate_scaled"], f.plus(OPEN - 1))
                passes(gate_bank, wide, c, 0, KD, xh, xl, 0, True, True,
                       norms[2 * n]["xl_ready"] if with_norm else None).then_inc(s["gate_mm"], 1)
                if with_norm:
                    sum_squares(2 * n)
                pe.wait_ge(s["up_scaled"], f.plus(OPEN - 1))
                passes(up_bank, wide, c, KD, KD, xh, xl, 0, True, True).then_inc(chunk_done, 1)
                if with_norm:
                    spread_rstd(2 * n)
                    pe.wait_ge(norms[2 * n]["rstd_ready"], 1)

            def ffn(n, c_up, c_down, wide):
                s, g = ups[n], ffn_mem[n]
                for j in (0, 1):
                    up_chunk(At(c_up + j), n, At(j), wide, j == 0)
                with pe.Fori(1, KF // 2) as i:
                    for j in (0, 1):
                        up_chunk(At(c_up + j, i, 2), n, At(j, i, 2), wide, False)
                pe.wait_ge(s["gate_scaled"], KF + OPEN)
                pe.wait_ge(s["up_scaled"], KF + OPEN)
                if n == 0:
                    pe.wait_ge(late_loaded, 64)
                    pe.wait_ge(lam_dt, 1)
                    for q in range(3):
                        ins = pe.transpose(PS[:, 2, q * GROUPS:(q + 1) * GROUPS],
                                           lam_raw[:, q].rearrange("g d p -> g (d p)"), ident[0:GROUPS, 0:GROUPS])
                    ins.then_inc(lam_tr, 1)
                with pe.Fori(0, KD // 2) as i:
                    for m in (0, 1):
                        pe.wait_ge(norms[2 * n + 1]["h_ready"], At(m, i, 2).plus(OPEN - 1))
                        for h in (0, 1):
                            c = At(c_down + 2 * m + h, i, 4)
                            chunk_ready(c)
                            pe.wait_ge(s["gl_ready"], KF if h else KF // 2)
                            passes(4 * m, wide, c, 0, KF // 2, g["gh"], g["gl"], h * (KF // 2),
                                   h == 0, h == 1).then_inc(chunk_done, 1)

            pe.sem_inc(chunk_done, OPEN)
            pe.sem_inc(pv_mm, OPEN)

            pe.wait_ge(consts_made, 4)
            pe.wait_ge(x_loaded, 32)
            for k in range(KD):
                ins = pe.transpose(PS[:, 0, k * META:(k + 1) * META], m_nat[:, k * P:(k + 1) * P],
                                   ident[0:META, 0:META])
            ins.then_inc(x_tr, 1)
            for k in range(KD):
                if k == KD // 2:
                    pe.wait_ge(x_late, 16)
                if k == KD - 1:
                    pe.wait_ge(norms[0]["h_ready"], 2 + OPEN)
                for t in range(4):
                    ins = pe.transpose(PS[:, x_bank(k), t * P:(t + 1) * P],
                                       x_nat[:, t, k * P:(k + 1) * P], ident[:])
                ins.then_inc(x_tr, 1)
            pe.wait_ge(meta_in, 1)
            pe.wait_ge(norms[0]["h_ready"], 1 + OPEN)

            ffn(0, C_UP1, C_DOWN1, True)

            F, B = slice(0, STATE), slice(STATE, P)

            def c_transposes(i, bank, col):
                pe.wait_ge(ssm_in, i * 128 + 128)
                for ri in (0, 1):
                    ins = pe.transpose(PS[:, bank, col + ri * P:col + (ri + 1) * P], c_raw[:, ri, :], ident[:])
                ins.then_inc(ct_mm, 1)

            def w1_transposes(i):
                pe.wait_ge(w1t_ready, i + 1)
                for ri in (0, 1):
                    for g in range(GB):
                        ins = pe.transpose(PS[:, 2 * ri + g // 4, (g % 4) * P:(g % 4 + 1) * P],
                                           w1t[:, ri, g].rearrange("p s c -> p (s c)"), ident[:])
                ins.then_inc(w1t_mm, 1)

            def scores(a, gi, heads):
                n, b = groups[gi]
                part = slice(b * DH, (b + 1) * DH)
                band, meta = band_at(n)
                for r in heads:
                    pe.wait_ge(sc_done, a * 32 + (4 * gi + r - 1 + OPEN))
                    q = qT[part, r, n * P:(n + 1) * P]
                    k0 = META + max(n - 1, 0) * P
                    pe.matmul(PS[:, 4 + r % 2, band:band + blocks(n) * P], q, kT[part, k0:k0 + blocks(n) * P],
                              start=True, stop=True)
                    pe.matmul(PS[:, 4 + r % 2, meta:meta + META], q, kT[part, 0:META], start=True, stop=True
                              ).then_inc(s_mm, 1)

            def ssm_batch(i, more):
                pe.wait_ge(u_in, i * 128 + 128)
                for ri in (0, 1):
                    pe.wait_ge(w1_ev, i * 2 + 1 + ri)
                    for g in range(GB):
                        ins = pe.matmul(PS[:, 4 + 2 * ri + g // 4, (g % 4) * NCH:(g % 4 + 1) * NCH],
                                        w1[:, ri, g, :], U[:, g, :], start=True, stop=True)
                    ins.then_inc(sin_mm, 1)
                pe.wait_ge(kernels_ready, i + 1)
                for g in range(GB):
                    for q, ri in ((0, 0), (2, 1)):
                        pe.matmul(PS[0:CH, 1, g * CH:(g + 1) * CH], bb[:, q, g, :], cT[:, ri, g * CH:(g + 1) * CH],
                                  start=g == 0 and ri == 0, stop=False)
                pe.wait_ge(sin_ev, i * 8 + 8)
                pe.matmul(PS[0:CH, 1, 0:P], ident[:, 0:CH], d_diag[:].rearrange("p g c -> p (g c)"),
                          start=False, stop=True)
                if more:
                    c_transposes(i + 1, 2, 0)
                for g in range(GB):
                    for bank, part, i0 in ((4 + g // 4, B, 1), (6 + g // 4, F, 0)):
                        o = PS[0:CH, bank, (g % 4) * 7 * CH:(g % 4 + 1) * 7 * CH]
                        for q, ri in ((0, 0), (2, 1)):
                            ins = pe.matmul(o, bb[part, q, g, :],
                                            cp[part, ri, g, i0:i0 + 7, :].rearrange("p i c -> p (i c)"),
                                            start=ri == 0, stop=ri == 1)
                ins.then_inc(krow_mm, 1)
                def y_of(g):
                    return PS[:, y_bank(more), g * OCH:(g + 1) * OCH]
                pe.wait_ge(sx_ready, i + 1)
                pe.wait_ge(krow_ev, i * 5 + 5)
                if not more:
                    scores(0, 0, (0, 1))
                for g in range(GB):
                    for ri in (0, 1):
                        ins = pe.matmul(y_of(g), cp[:, ri, g].rearrange("p i c -> p (i c)"), sx[:, ri, g, :],
                                        start=g == 0 and ri == 0, stop=False)
                ins.then_inc(state_mm, 1)
                if not more:
                    scores(0, 0, (2, 3))
                pe.wait_ge(toep_in, i * 128 + 128)
                for g in range(GB):
                    ins = pe.matmul(y_of(g), toep[:, g, :], U[:, g, MCH:NCH], start=False,
                                    stop=g == GB - 1)
                ins.then_inc(y_mm, 1)
                if more:
                    w1_transposes(i + 1)
                    pe.wait_ge(y_ev, i * 2 + 2)

            def project(a):
                c = At(C_ATT + 4 * a)
                chunk_ready(c)
                passes(4, True, c, 0, KD, xh, xl, 0, True, True).then_inc(chunk_done, 1)
                c = At(C_ATT + 4 * a + 1)
                chunk_ready(c)
                if a == 0:
                    pe.wait_ge(u_ready, KS)
                passes(6, True, c, 0, KD, xh, xl, 0, True, True).then_inc(chunk_done, 1)
                if a == 1:
                    pe.wait_ge(yah_ready, 4 + OPEN)
                    pe.wait_ge(yal_ready, 4 + OPEN)
                for r in range(QG):
                    c = At(C_ATT + 4 * a + 2 + r // 2)
                    if r % 2 == 0:
                        chunk_ready(c)
                    passes(q_bank(r), False, c, (r % 2) * KD, KD, xh, xl, 0, True, True
                           ).then_inc(chunk_done if r % 2 else proj_mm, 1)
                    if (a, r) == (0, 2):
                        pe.wait_ge(proj_ev, 4)
                        w1_transposes(0)
                    if r == 1:
                        pe.wait_ge(proj_ev, 7 * a + 2)
                        for t in range(5):
                            t0 = 0 if t == 0 else META + (t - 1) * P
                            ins = pe.transpose(PS[:, 4 + t // 4, (t % 4) * P:(t % 4 + 1) * P],
                                               vT[:, t0:t0 + P], ident[:])
                        ins.then_inc(v_tr, 1)

            pe.wait_ge(norms[1]["h_ready"], KD - 1 + OPEN)
            for j in range(KS // 2):
                c = At(C_U + j)
                chunk_ready(c)
                for t in (0, 1):
                    bt = 2 * j + t
                    ins = passes(2 * bt, True, c, t * KD, KD, xh, xl, 0, True, True,
                                 norms[1]["xl_ready"] if bt == 0 else None)
                    ins.then_inc(chunk_done if t else u_mm, 1)
                    if bt == 0:
                        sum_squares(1)
                        c_transposes(0, 5, 0)
                    if bt == 1:
                        spread_rstd(1)
                        pe.wait_ge(norms[1]["rstd_ready"], 1)
                        pe.wait_ge(ct_ev, 1)

            pe.wait_ge(u_ready, KS - 1)
            project(0)
            pe.wait_ge(proj_ev, 7)
            with pe.Fori(0, KS - 1) as i:
                ssm_batch(i, True)
            ssm_batch(KS - 1, False)

            def groups_of(a):
                def transposes(gi):
                    n, b = groups[gi]
                    band, meta = band_at(n)
                    pe.wait_ge(p_ready, a * 8 + gi + 1)
                    pe.wait_ge(pt_dve, a * 24 + 3 * gi + 1)
                    for r in range(QG):
                        if r >= 2:
                            pe.wait_ge(pt_act, a * 16 + 2 * gi + r - 1)
                        for j in range(blocks(n)):
                            pe.transpose(PS[:, prob_bank(r), j * P:(j + 1) * P],
                                         sc[:, gi % 2, r, band + j * P:band + (j + 1) * P], ident[:])
                        pe.transpose(PS[0:META, 2, r * P:(r + 1) * P], sc[:, gi % 2, r, meta:meta + META], ident[:]
                                     ).then_inc(t_mm, 1)

                def values(gi):
                    n, b = groups[gi]
                    kb = max(n - 1, 0)
                    pe.wait_ge(pt_act, a * 16 + (2 * gi + 3))
                    pe.wait_ge(pt_dve, a * 24 + (3 * gi + 4))
                    if b == 0:
                        pe.wait_ge(yah_ready, a * 4 + (n - 1 + OPEN))
                        pe.wait_ge(yal_ready, a * 4 + (n - 1 + OPEN))
                    o = PS[b * DH:(b + 1) * DH, 0 if n % 2 else 3, :]
                    for j in range(blocks(n)):
                        pe.matmul(o, vt[:, 1 + kb + j, b * DH:(b + 1) * DH],
                                  pt[:, gi % 2, j].rearrange("p r q -> p (r q)"), start=j == 0, stop=False)
                    pe.matmul(o, vt[0:META, 0, b * DH:(b + 1) * DH],
                              ptm[:, gi % 2].rearrange("p r q -> p (r q)"), start=False, stop=True
                              ).then_inc(pv_mm, 1)

                pe.wait_ge(proj_ev, a * 7 + 7)
                for gi in range(-1 if a else 0, last_group + 2):
                    if gi < last_group:
                        scores(a, gi + 1, (0, 1))
                    if (a, gi) == (0, 1):
                        pe.wait_ge(y_ev, 2 * KS)
                    if gi > 0:
                        values(gi - 1)
                    if gi < last_group:
                        scores(a, gi + 1, (2, 3))
                    if 0 <= gi <= last_group:
                        transposes(gi)

            groups_of(0)
            pe.wait_ge(sc_done, 32 + OPEN)
            project(1)
            groups_of(1)

            def gates(c, m, bank):
                pe.wait_ge(mg_ready, m.plus(OPEN - 1))
                chunk_ready(c)
                passes(bank, False, c, 0, KD, xh, xl, 0, True, True)
                passes(bank + 1, False, c, KD, KD, xh, xl, 0, True, True).then_inc(chunk_done, 1)

            def branches(c, bank):
                chunk_ready(c)
                passes(bank + 2, False, c, 0, KS, ysh, ysl, 0, True, True)
                passes(bank + 3, False, c, KS, KD, yah, yal, 0, True, True).then_inc(chunk_done, 1)

            pe.wait_ge(sc_done, 64 + OPEN)
            gates(At(C_GATE0), At(0), merge_bank(0))

            c = At(C_GLU)
            chunk_ready(c)
            pe.wait_ge(yah_ready, 8 + OPEN)
            pe.wait_ge(yal_ready, 8 + OPEN)
            for m in range(KS):
                ins = passes(m, False, c, m * KS, KS, zh, zl, 0, True, True, zl_ready if m == 0 else None)
            ins.then_inc(chunk_done, 1)

            pe.wait_ge(glu_sig, 2)
            gates(At(C_GATE1), At(1), merge_bank(1))
            pe.wait_ge(ysl_ready, KS)
            branches(At(C_BRANCH0), merge_bank(0))
            branches(At(C_BRANCH1), merge_bank(1))
            with pe.Fori(1, KD // 2) as i:
                for j in (0, 1):
                    gates(At(C_MERGE + 2 * j, i, 4), At(j, i, 2), merge_bank(j))
                    branches(At(C_MERGE + 2 * j + 1, i, 4), merge_bank(j))

            pe.wait_ge(mgl_ready, KD)
            with pe.Fori(0, KD // 4) as i:
                for j in (0, 1):
                    c = At(C_OUT + j, i, 2)
                    chunk_ready(c)
                    for t in (0, 1):
                        m = At(2 * j + t, i, 4)
                        pe.wait_ge(norms[2]["h_ready"], m.plus(OPEN - 1))
                        passes(2 * j + t, False, c, t * KD, KD, mgh, mgl, 0, True, True
                               ).then_inc(chunk_done if t else out_mm, 1)
            pe.wait_ge(norms[2]["h_ready"], KD + OPEN)

            ffn(1, C_UP2, C_DOWN2, False)

            pe.wait_ge(norms[3]["h_ready"], KD + OPEN)
            for m in range(KD):
                pe.wait_ge(norms[3]["xh_ready"], m + 1)
                if m == KD - 1:
                    pe.wait_ge(norms[3]["sum_ready"], KD + 1)
                    for t in range(5):
                        t0 = 0 if t == 0 else META + (t - 1) * P
                        ins = pe.matmul(PS[:, 7, 3 * P + t:3 * P + t + 1], ssum[:, t0:t0 + P], ones[:, 0:1],
                                        start=True, stop=True)
                    ins.then_inc(norms[3]["ssq_mm"], 1)
                for t in range(4):
                    if m == KD - 1 and t == 3:
                        pe.wait_ge(norms[3]["var_ready"], 1)
                    ins = pe.transpose(PS[:, 2 * t + m // 4, (m % 4) * P:(m % 4 + 1) * P],
                                       hg[:, m, t * P:(t + 1) * P], ident[:])
                    if m == KD - 1:
                        ins.then_inc(fin_mm, 1)

        @block.scalar
        def _(act):
            def tn(k):
                return prm[:, k]

            def split_hi(c):
                act.wait_ge(w_loaded[c.slot], c.loads())
                act.wait_ge(chunk_done, c.plus(OPEN - 1))
                n = tiles_in(c)
                act.activation(wh[:, c.slot, 0:n], wraw[:, c.slot, 0:n], ACT.Copy).then_inc(w_hi, 1)

            def norm_step(n, m, wide):
                s = norms[n]
                cols = slice(0, T) if wide else slice(META, T)
                mm = m.plus(0)
                h = hT[:, ds(mm, 1), cols].rearrange("p o n -> p (o n)")
                act.wait_ge(s["h_ready"], m.plus(1 + OPEN))
                act.wait_ge(s["sum_ready"], m.plus(1))
                act.activation(sq[:, cols], h, ACT.Square).then_inc(s["sq_ready"], 1)
                gain = gains[:, n, ds(mm, 1)]
                if n < 3:
                    o = xh[:, ds(mm, 1), cols].rearrange("p o n -> p (o n)")
                else:
                    o = hg[:, ds(mm, 1), :].rearrange("p o n -> p (o n)")
                act.activation(o, h, ACT.Copy, scale=gain).then_inc(s["xh_ready"], 1)

            def rstd_out(n):
                act.wait_ge(norms[n]["bcast_mm"], 1)
                act.activation(rstd_b[:, 0:META + 2 * P], PS[:, 6, 0:META + 2 * P], ACT.Copy)
                act.activation(rstd_b[:, META + 2 * P:T], PS[:, 7, 0:2 * P], ACT.Copy
                               ).then_inc(norms[n]["rstd_ready"], 1)

            def ffn(n, c_up, c_down, wide):
                s, g = ups[n], ffn_mem[n]
                w = T if wide else SEQ

                def up_step(c, f, with_norm):
                    b = f.base % 2
                    split_hi(c.at(1))
                    if with_norm:
                        rstd_out(2 * n)
                    act.wait_ge(s["gate_scaled"], f.plus(1 + OPEN))
                    t1 = g["t1"][:, b, 0:w]
                    act.activation(t1, t1, ACT.Silu).then_inc(s["silu_done"], 1)
                    act.wait_ge(s["gg_ready"], f.plus(1))
                    act.activation(g["gh"][:, ds(f.plus(0), 1), :].rearrange("p o n -> p (o n)"),
                                   g["t2"][:, b, 0:w], ACT.Copy).then_inc(s["gh_ready"], 1)

                for j in (0, 1):
                    up_step(At(c_up + j), At(j), j == 0)
                if n == 0:
                    for q, lam in enumerate((ssm_lam_re, ssm_lam_im)):
                        act.dma_start(lam_raw[:, q], lam[0].rearrange("d g p -> g d p")).then_inc(late_loaded, 16)
                    with nc.allow_non_contiguous_dma("64 numbers"):
                        act.dma_start(dt_raw, ssm_log_dt[0].rearrange("d g -> g d")).then_inc(late_loaded, 16)
                with act.Fori(1, KF // 2) as i:
                    for j in (0, 1):
                        up_step(At(c_up + j, i, 2), At(j, i, 2), False)
                if n == 0:
                    act.wait_ge(s["gl_ready"], KF)
                    act.wait_ge(lam_tr, 1)
                    act.activation(prm[:, LR:LI + 1].rearrange("p q g -> p (q g)"), PS[:, 2, 0:2 * GROUPS], ACT.Copy)
                    act.activation(tn(DT), PS[:, 2, 2 * GROUPS:3 * GROUPS], ACT.Exp).then_inc(act_small_done, 1)

                def down_steps(i):
                    for j in range(4):
                        last = i is None and j == 3 and n == 1
                        c, m = at_end(c_down, KD // 2, 4, j, i), at_end(0, KD // 2, 2, j // 2, i)
                        if not last:
                            split_hi(c.at(1))
                        if j % 2:
                            norm_step(2 * n + 1, m, wide)

                down_steps(0)
                if n == 0:
                    act.wait_ge(act_small, 1)
                    act.activation(tn(EXPA), tn(A_), ACT.Exp)
                    act.activation(tn(SINH), tn(RH), ACT.Sin)
                    act.activation(tn(SINR), tn(R_), ACT.Sin).then_inc(act_small_done, 1)
                with act.Fori(1, KD // 2 - 1) as i:
                    down_steps(i)
                down_steps(None)

            with nc.allow_non_contiguous_dma("gains, a few KB"):
                for n, g in enumerate((ffn1_norm[0], mix_norm[0], ffn2_norm[0], final_norm)):
                    act.dma_start(gains[:, n, :], g.rearrange("(k p) -> p k", p=P)).then_inc(const_loaded, 16)
                act.wait_ge(consts_made, 4)
                act.dma_start(dskip[0:CH, :], ssm_d[0].rearrange("(g c) -> c g", c=CH)).then_inc(const_loaded, 16)
            act.dma_start(negsink[:], attn_sink[0:1, :].to_broadcast([P, HEADS])).then_inc(late_loaded, 16)
            act.wait_ge(const_loaded, 80)

            for k in range(KD):
                norm_step(0, At(k), True)
                if k == 1:
                    split_hi(At(0))
            ffn(0, C_UP1, C_DOWN1, True)

            def c_transposed(i, bank, col):
                act.wait_ge(ct_mm, i + 1)
                act.activation(cT[:].rearrange("p a n -> p (a n)"), PS[:, bank, col:col + 2 * P], ACT.Copy
                               ).then_inc(ct_ev, 1)

            def input_to_state(i):
                act.wait_ge(w1t_mm, i + 1)
                for ri in (0, 1):
                    act.activation(w1[:, ri].rearrange("p (a g) n -> p a (g n)", a=2),
                                   PS[:, 2 * ri:2 * ri + 2, :], ACT.Copy).then_inc(w1_ev, 1)

            def exps(a, gi):
                n, b = groups[gi]
                act.wait_ge(negm_ready, a * 8 + gi + 1)
                for r in range(QG):
                    tile = sc[:, gi % 2, r, 0:width(n)]
                    act.activation(tile, tile, ACT.Exp, bias=negm[:, gi % 2, r:r + 1],
                                   accum_out=rs[:, gi % 2, r:r + 1])
                act.activation(sk[:, gi % 2], sk[:, gi % 2], ACT.Exp).then_inc(exp_done, 1)

            def gelu_factor(i):
                act.wait_ge(gelu_arg, i + 1)
                act.activation(arg, arg, ACT.Sigmoid, scale=GELU_CUBIC * 2.0 * math.sqrt(2.0 / math.pi)
                               ).then_inc(gelu_exp, 1)

            def ssm_batch(i, first, more):
                for ri in (0, 1):
                    act.wait_ge(sin_mm, i * 2 + 1 + ri)
                    for half in (0, 1):
                        part = slice(half * STATE, (half + 1) * STATE)
                        o = sin_[part, ri, :, ::-1] if half else sin_[part, ri]
                        for q in (0, 1):
                            act.activation(o[:, 4 * q:4 * q + 4, :],
                                           PS[part, 4 + 2 * ri + q, 0:4 * NCH].rearrange("p (g k) -> p g k", g=4),
                                           ACT.Copy).then_inc(sin_ev, 1)
                if not first:
                    gelu_factor(i - 1)
                if more:
                    c_transposed(i + 1, 2, 0)
                act.wait_ge(krow_mm, i + 1)
                act.activation(krow[:, :, 7 * CH:8 * CH], PS[0:CH, 1, 0:P].rearrange("p (g n) -> p g n", g=GB),
                               ACT.Copy).then_inc(krow_ev, 1)
                for q in range(4):
                    lag0 = 0 if q < 2 else 8
                    act.activation(krow[:, 4 * (q % 2):4 * (q % 2) + 4, lag0 * CH:(lag0 + 7) * CH],
                                   PS[0:CH, 4 + q, 0:28 * CH].rearrange("p (g n) -> p g n", g=4), ACT.Copy
                                   ).then_inc(krow_ev, 1)
                if not more:
                    exps(0, 0)
                act.wait_ge(y_mm, i + 1)
                if not first:
                    act.wait_ge(z_ready, i)
                act.activation(y1, PS[:, y_bank(more), :], ACT.Copy).then_inc(y_ev, 1)
                act.activation(arg, PS[:, y_bank(more), :], ACT.Square).then_inc(y_ev, 1)
                if more:
                    input_to_state(i + 1)

            split_hi(At(C_U + 1))
            c_transposed(0, 5, 0)
            rstd_out(1)
            act.sem_inc(pt_act, 1)
            act.sem_inc(yah_ready, OPEN)
            for j in range(4):
                split_hi(At(C_ATT + j))
            input_to_state(0)
            split_hi(At(C_ATT + 4))
            ssm_batch(0, True, True)
            with act.Fori(1, KS - 1) as i:
                ssm_batch(i, False, True)
            ssm_batch(KS - 1, False, False)
            gelu_factor(KS - 1)

            def prob_tiles(a, gi):
                n, b = groups[gi]
                act.wait_ge(pv_mm, a * 8 + gi + 1)
                for r in (0, 2):
                    act.wait_ge(t_mm, a * 32 + (4 * gi + r + 1))
                    act.activation(pt[:, gi % 2, 0:blocks(n), r, :],
                                   PS[:, prob_bank(r), 0:blocks(n) * P].rearrange("p (j q) -> p j q", q=P), ACT.Copy
                                   ).then_inc(pt_act, 1)

            def result(a, gi):
                n, b = groups[gi]
                act.wait_ge(pv_mm, a * 8 + gi + 1 + OPEN)
                act.activation(yah[:, a * 4:a * 4 + QG, n * P:(n + 1) * P],
                               PS[:, 0 if n % 2 else 3, :].rearrange("p (r q) -> p r q", r=QG), ACT.Copy
                               ).then_inc(yah_ready, 1)

            for a in (0, 1):
                if a == 1:
                    for j in range(5):
                        split_hi(At(C_ATT + 5 + j))
                for gi in range(-1 if a else 0, last_group + 2):
                    if 0 <= gi <= last_group:
                        prob_tiles(a, gi)
                    if gi > 0 and groups[gi - 1][1] == 1:
                        result(a, gi - 1)
                    if gi < last_group:
                        exps(a, gi + 1)

            act.wait_ge(z_in, KS * 128)
            for bt in range(KS):
                act.activation(zh[:, bt], uT[:, bt].rearrange("p s k -> p (s k)")[:, 0:SEQ], ACT.Copy
                               ).then_inc(zh_ready, 1)
            def gates_of(m, slot):
                act.wait_ge(gates_scaled, m.plus(1))
                gg = gsig[:, slot].rearrange("p a n -> p (a n)")
                act.activation(gg, gg, ACT.Sigmoid).then_inc(gates_sig, 1)

            def merged_hi(m, slot):
                act.wait_ge(mg_ready, m.plus(1 + OPEN))
                act.activation(mgh[:, ds(m.plus(0), 1), :].rearrange("p o n -> p (o n)"), gsig[:, slot, 0],
                               ACT.Copy).then_inc(mgh_ready, 1)

            split_hi(At(C_GATE1))
            gates_of(At(0), 0)
            act.wait_ge(chunk_done, At(C_GLU).plus(1 + OPEN))
            for m in range(KS):
                if m >= 2:
                    act.wait_ge(ysf_ready, m - 1)
                act.activation(sig[:, m % 2], PS[:, m, :], ACT.Sigmoid).then_inc(glu_sig, 1)
                act.wait_ge(ysf_ready, m + 1)
                act.activation(ysh[:, m], ysf[:, m % 2], ACT.Copy).then_inc(ysh_ready, 1)

            split_hi(At(C_BRANCH0))
            gates_of(At(1), 1)
            split_hi(At(C_BRANCH1))
            split_hi(At(C_MERGE + 4))
            merged_hi(At(0), 0)
            merged_hi(At(1), 1)
            with act.Fori(1, KD // 2) as i:
                for j in (0, 1):
                    m = At(j, i, 2)
                    split_hi(At(C_MERGE + 2 * j + 1, i, 4))
                    gates_of(m, j)
                    split_hi(At(C_MERGE + 2 * j + 2, i, 4))
                    merged_hi(m, j)
            with act.Fori(0, KD // 4) as i:
                for j in (0, 1):
                    split_hi(At(C_OUT + j + 1, i, 2))
                    for t in (0, 1):
                        norm_step(2, At(2 * j + t, i, 4), False)
            ffn(1, C_UP2, C_DOWN2, False)
            for t in range(4):
                act.wait_ge(norms[3]["rcol_ready"], 1)
                act.wait_ge(fin_mm, t + 1)
                act.activation(y_nat[:, t, 0:512], PS[:, 2 * t, :], ACT.Copy, scale=rcol[:, t + 1:t + 2]
                               ).then_inc(fin_act, 1)

        @block.vector
        def _(ve):
            link = Chain(ve, chain_sem)

            def as_f32(ap):
                return ap.bitcast(F32)

            def split_lo(c):
                ve.wait_ge(w_hi, c.plus(1))
                n = tiles_in(c)
                ve.tensor_tensor(wl[:, c.slot, 0:n], wraw[:, c.slot, 0:n], as_f32(wh[:, c.slot, 0:n]), ALU.subtract
                                 ).then_inc(w_lo, 1)

            def norm_step(n, m, wide):
                s = norms[n]
                cols = slice(0, T) if wide else slice(META, T)
                mm = m.plus(0)
                ve.wait_ge(s["sq_ready"], m.plus(1))
                ve.wait_ge(s["sum_ready"], m.plus(1))
                ve.tensor_tensor(ssum[:, cols], ssum[:, cols], sq[:, cols], ALU.add).then_inc(s["sum_ready"], 1)
                if n < 3:
                    ve.wait_ge(s["xh_ready"], m.plus(1))
                    h = hT[:, ds(mm, 1), cols].rearrange("p o n -> p (o n)")
                    hi = xh[:, ds(mm, 1), cols].rearrange("p o n -> p (o n)")
                    lo = xl[:, ds(mm, 1), cols].rearrange("p o n -> p (o n)")
                    ve.scalar_tensor_tensor(out=lo, in0=h, scalar=gains[:, n, ds(mm, 1)], in1=as_f32(hi),
                                            op0=ALU.mult, op1=ALU.subtract).then_inc(s["xl_ready"], 1)

            def norm_start(n):
                ve.memset(ssum[:], 0.0).then_inc(norms[n]["sum_ready"], 1)
                ve.sem_inc(norms[n]["h_ready"], OPEN)

            def token_var(n):
                s = norms[n]
                ve.wait_ge(s["ssq_mm"], 1)
                src = PS[:, 4, 0:5] if n < 3 else PS[:, 7, 3 * P:3 * P + 5]
                ve.tensor_scalar(var[:], src, 1.0 / D, EPS, ALU.mult, ALU.add).then_inc(s["var_ready"], 1)

            def token_diag(n):
                s = norms[n]
                ve.wait_ge(s["rcol_ready"], 1)
                if n == 0:
                    ve.wait_ge(dist_out, 16)
                for t in range(5):
                    ins = ve.tensor_scalar(diag[:, t, :], ident[:], rcol[:, t:t + 1], None, ALU.mult)
                ins.then_inc(s["diag_ready"], 1)

            def ffn(n, c_up, c_down, wide):
                s, g = ups[n], ffn_mem[n]
                w = T if wide else SEQ

                def shaped(row):
                    return row.rearrange("p (a n) -> p a n", a=2) if wide else row

                rstd = shaped(rstd_b[:]) if wide else rstd_b[:, META:T]

                def up_step(c, f, with_norm):
                    b = f.base % 2
                    gate_bank, up_bank = (4 * b, 4 * b + 2) if wide else (2 * b, 2 * b + 1)
                    t1, t2 = g["t1"][:, b, 0:w], g["t2"][:, b, 0:w]
                    if with_norm:
                        token_var(2 * n)
                        token_diag(2 * n)
                    split_lo(c.at(1))
                    if with_norm:
                        ve.wait_ge(norms[2 * n]["rstd_ready"], 1)
                    ve.wait_ge(s["gate_mm"], f.plus(1))
                    ve.tensor_tensor(shaped(t1), psum_of(gate_bank, wide), rstd, ALU.mult
                                     ).then_inc(s["gate_scaled"], 1)
                    ve.wait_ge(chunk_done, c.plus(1 + OPEN))
                    ve.tensor_tensor(shaped(t2), psum_of(up_bank, wide), rstd, ALU.mult
                                     ).then_inc(s["up_scaled"], 1)
                    ve.wait_ge(s["up_scaled"], f.plus(1 + OPEN))
                    ve.wait_ge(s["silu_done"], f.plus(1))
                    ve.tensor_tensor(t2, t1, t2, ALU.mult).then_inc(s["gg_ready"], 1)
                    ve.wait_ge(s["gh_ready"], f.plus(1))
                    ff = f.plus(0)
                    ve.tensor_tensor(g["gl"][:, ds(ff, 1), :].rearrange("p o n -> p (o n)"), t2,
                                     as_f32(g["gh"][:, ds(ff, 1), :].rearrange("p o n -> p (o n)")),
                                     ALU.subtract).then_inc(s["gl_ready"], 1)

                for j in (0, 1):
                    up_step(At(c_up + j), At(j), j == 0)
                with ve.Fori(1, KF // 2) as i:
                    for j in (0, 1):
                        up_step(At(c_up + j, i, 2), At(j, i, 2), False)
                norm_start(2 * n + 1)

                def down_steps(i):
                    for j in range(4):
                        last = i is None and j == 3 and n == 1
                        c, m = at_end(c_down, KD // 2, 4, j, i), at_end(0, KD // 2, 2, j // 2, i)
                        if not last:
                            split_lo(c.at(1))
                        if j % 2:
                            ve.wait_ge(chunk_done, c.plus(1 + OPEN))
                            row = hT[:, ds(m.plus(0), 1), :].rearrange("p o n -> p (o n)")
                            h = tokens(row, wide)
                            ve.scalar_tensor_tensor(out=h, in0=psum_of(4 * (j // 2), wide), scalar=0.5, in1=h,
                                                    op0=ALU.mult, op1=ALU.add
                                                    ).then_inc(norms[2 * n + 1]["h_ready"], 1)
                            norm_step(2 * n + 1, m, wide)

                with ve.Fori(0, KD // 2 - 1) as i:
                    down_steps(i)
                down_steps(None)

            ve.sem_inc(w_lo, OPEN)
            ve.sem_inc(z_out, 16)
            ve.sem_inc(sc_done, OPEN)
            ve.sem_inc(mg_ready, OPEN)
            ve.sem_inc(pt_dve, 1)
            ve.sem_inc(yal_ready, OPEN)
            for s in ups:
                ve.sem_inc(s["gate_scaled"], OPEN)
                ve.sem_inc(s["up_scaled"], OPEN)
            norm_start(0)
            ve.wait_ge(dist_iota, 1)
            band = dist_made[:, META:DIST - META]
            ve.scalar_tensor_tensor(out=band, in0=band, scalar=-1.0, in1=band, op0=ALU.mult, op1=ALU.max
                                    ).then_inc(dist_abs, 1)
            ve.wait_ge(x_tr, 1)
            ve.tensor_copy(hT[:, :, 0:META], PS[:, 0, 0:KD * META].rearrange("p (k n) -> p k n", k=KD)
                           ).then_inc(meta_in, 1)
            ve.wait_ge(const_loaded, 80)
            for k in range(KD):
                ve.wait_ge(x_tr, k + 2)
                ve.tensor_copy(hT[:, k, META:T], PS[:, x_bank(k), :]).then_inc(norms[0]["h_ready"], 1)
                if k > 0:
                    norm_step(0, At(k - 1), True)
                if k == 1:
                    split_lo(At(0))
            norm_step(0, At(KD - 1), True)
            ffn(0, C_UP1, C_DOWN1, True)

            def tt(o, x0, x1, op):
                link(ve.tensor_tensor(o, x0, x1, op))

            def ts(o, x0, s1, op0, s2=None, op1=None):
                if op1 is None:
                    link(ve.tensor_scalar(o, x0, s1, None, op0))
                else:
                    link(ve.tensor_scalar(o, x0, s1, s2, op0, op1))

            def stt(o, x0, s, x1, op0, op1):
                link(ve.scalar_tensor_tensor(out=o, in0=x0, scalar=s, in1=x1, op0=op0, op1=op1))

            def cmul(o, x0, x1, tmp, conj=False):
                ve.tensor_tensor(o[0], x0[0], x1[0], ALU.mult)
                ve.tensor_tensor(tmp[0], x0[1], x1[1], ALU.mult)
                ve.tensor_tensor(o[1], x0[0], x1[1], ALU.mult)
                tt(tmp[1], x0[1], x1[0], ALU.mult)
                ve.tensor_tensor(o[0], o[0], tmp[0], ALU.add if conj else ALU.subtract)
                tt(o[1], o[1], tmp[1], ALU.subtract if conj else ALU.add)

            F, B = slice(0, STATE), slice(STATE, P)
            big = [P, GB, CHUNK, CH]
            long = [t[:].rearrange("p a n -> p (a n)") for t in (ta, tb)]
            t4 = [t[:, 0:GB * P].rearrange("p (g s c) -> p g s c", g=GB, s=CHUNK) for t in long]

            def table(k):
                return [prm[:, k + 9 * q:k + 9 * q + 9] for q in (0, 1)]

            def input_kernels(i, again):
                gs = ds(i * GB, GB)
                if again:
                    ve.wait_ge(krow_mm, i)
                ve.wait_ge(ct_ev, i + 1)
                ve.wait_ge(ssm_in, i * 128 + 128)
                coef = [prm[:, k, gs].unsqueeze(2).to_broadcast([P, GB, CH]) for k in (CR, CI)]
                cmul([bb[:, 0], bb[:, 1]], coef, [b_raw[:, 0], b_raw[:, 1]],
                     [t[:, 0, 0:P].rearrange("p (g c) -> p g c", g=GB) for t in (ta, tb)])
                tt(d_diag[:], ident[:, 0:CH].unsqueeze(1).to_broadcast([P, GB, CH]),
                   dskip[:, gs].unsqueeze(2).to_broadcast([P, GB, CH]), ALU.mult)
                ts(bb[:, 2], bb[:, 1], -1.0, ALU.mult)

            def w1_kernels(i):
                gs = ds(i * GB, GB)
                cmul([w1t[:, 0], w1t[:, 1]],
                     [bpw[:, q, gs].unsqueeze(3).to_broadcast(big) for q in (0, 1)],
                     [bb[:, q].unsqueeze(2).to_broadcast(big) for q in (0, 1)], t4)
                ve.sem_inc(w1t_ready, 1)

            def phases(i):
                gs = ds(i * GB, GB)
                es = [P, GB, 9, 8]
                ua, ub = table(UA), table(UB)
                cmul([E[:, q].rearrange("p g (j l) -> p g j l", j=9) for q in (0, 1)],
                     [ua[q][:, :, gs].rearrange("p j g -> p g j").unsqueeze(3).to_broadcast(es) for q in (0, 1)],
                     [ub[q][:, 0:8, gs].rearrange("p l g -> p g l").unsqueeze(2).to_broadcast(es) for q in (0, 1)],
                     [t[:, 0:GB * 72].rearrange("p (g j l) -> p g j l", g=GB, j=9) for t in long])
                link(ve.tensor_copy(decay[:], prm[:, R8, gs].unsqueeze(2).to_broadcast([P, GB, NCH])))
                link(ve.memset(decay[:, :, 0:1], 0.0))

            def output_kernels(i, again):
                gs = ds(i * GB, GB)
                if again:
                    ve.wait_ge(state_mm, i)
                cmul([cp[:, 0], cp[:, 1]],
                     [cpw[:, q, gs].unsqueeze(3).to_broadcast(big) for q in (0, 1)],
                     [cT[:, q].rearrange("p (g c) -> p g c", g=GB).unsqueeze(2).to_broadcast(big) for q in (0, 1)],
                     t4)
                ve.sem_inc(kernels_ready, 1)

            def gelu_out(i):
                ve.wait_ge(gelu_exp, i + 1)
                ve.wait_ge(z_out, i * 16 + 16)
                ve.tensor_tensor(Z, y1, arg, ALU.mult).then_inc(z_ready, 1)

            def ssm_batch(i, first, more):
                def gk(t, q):
                    return t[:, q].rearrange("p (g k) -> p g k", g=GB)
                ve.wait_ge(sin_ev, i * 8 + 8)
                e = [E[:, q, :, 0:NCH] for q in (0, 1)]
                cmul([gk(ta, 0), gk(tb, 0)], e, [sin_[:, 0], sin_[:, 1]], [gk(ta, 1), gk(tb, 1)], conj=True)
                dk = decay[:].rearrange("p g k -> p (g k)")
                for q, t in ((0, ta), (1, tb)):
                    link(ve.tensor_tensor_scan(sin_[:, q].rearrange("p g k -> p (g k)"), dk, t[:, 0], 0.0,
                                               ALU.mult, ALU.add))
                ve.tensor_tensor(gk(ta, 0), e[0], sin_[:, 0], ALU.mult)
                ve.tensor_tensor(gk(ta, 1), e[1], sin_[:, 1], ALU.mult)
                ve.tensor_tensor(gk(tb, 0), e[0], sin_[:, 1], ALU.mult)
                tt(gk(tb, 1), e[1], sin_[:, 0], ALU.mult)
                for part, dst, src in ((F, slice(0, OCH), slice(1, OCH + 1)),
                                       (B, slice(OCH - 2, None, -1), slice(0, OCH - 1))):
                    ve.tensor_tensor(sx[part, 0, :, dst], gk(ta, 0)[part, :, src], gk(ta, 1)[part, :, src],
                                     ALU.subtract)
                    ins = ve.scalar_tensor_tensor(out=sx[part, 1, :, dst], in0=gk(tb, 0)[part, :, src], scalar=-1.0,
                                                  in1=gk(tb, 1)[part, :, src], op0=ALU.mult, op1=ALU.subtract)
                ins.then_inc(sx_ready, 1)
                ve.wait_ge(sx_ready, i + 1)
                if not first:
                    gelu_out(i - 1)
                if more:
                    phases(i + 1)
                    input_kernels(i + 1, True)
                    w1_kernels(i + 1)
                    output_kernels(i + 1, True)
                    gelu_in(i)

            def gelu_in(i):
                ve.wait_ge(y_ev, i * 2 + 2)
                ve.scalar_tensor_tensor(out=arg, in0=arg, scalar=1.0 / GELU_CUBIC, in1=y1, op0=ALU.add, op1=ALU.mult
                                        ).then_inc(gelu_arg, 1)

            ve.wait_ge(powers_ready, 1)
            ve.memset(sx[:], 0.0)
            link(ve.reciprocal(prm[:, DEN], prm[:, DEN]))
            tt(prm[:, CR], prm[:, CR], prm[:, DEN], ALU.mult)
            tt(prm[:, CI], prm[:, CI], prm[:, DEN], ALU.mult)
            pw = table(PW)
            for q in (0, 1):
                def place(dst, part, order):
                    return ve.tensor_copy(dst[part, q].rearrange("p g i -> p i g"), pw[q][part, order])
                place(cpw, F, slice(1, 9))
                place(cpw, B, slice(8, 0, -1))
                place(bpw, F, slice(7, None, -1))
                ins = place(bpw, B, slice(0, 8))
            link(ins)

            token_var(1)
            split_lo(At(C_U + 1))
            token_diag(1)
            ve.wait_ge(norms[1]["rstd_ready"], 1)
            for bt in range(KS):
                if bt == 2:
                    split_lo(At(C_ATT))
                    input_kernels(0, False)
                if bt % 2:
                    ve.wait_ge(chunk_done, At(C_U + bt // 2).plus(1 + OPEN))
                else:
                    ve.wait_ge(u_mm, bt // 2 + 1)
                for hf in (0, 1):
                    ins = ve.tensor_tensor(
                        uT[:, bt, :, hf * (NCH // 2):(hf + 1) * (NCH // 2)].rearrange("p s k -> p k s"),
                        PS[:, 2 * bt + hf, 0:HALF].rearrange("p (k s) -> p k s", s=CHUNK),
                        rstd_b[:, hf * HALF:(hf + 1) * HALF].rearrange("p (k s) -> p k s", s=CHUNK), ALU.mult)
                ins.then_inc(u_ready, 1)
                if bt == 2:
                    w1_kernels(0)

            def projected(a):
                split_lo(At(C_ATT + 4 * a + 1))
                ve.wait_ge(chunk_done, At(C_ATT + 4 * a).plus(1 + OPEN))
                ve.tensor_tensor(kT[:].rearrange("p (h n) -> p h n", h=2), psum_of(4, True),
                                 rstd_b[:].rearrange("p (h n) -> p h n", h=2), ALU.mult).then_inc(proj_ev, 1)
                split_lo(At(C_ATT + 4 * a + 2))
                if a == 0:
                    phases(0)
                ve.wait_ge(chunk_done, At(C_ATT + 4 * a + 1).plus(1 + OPEN))
                ve.tensor_tensor(vT.rearrange("p (h n) -> p h n", h=2), psum_of(6, True),
                                 rstd_b[:].rearrange("p (h n) -> p h n", h=2), ALU.mult).then_inc(proj_ev, 1)
                split_lo(At(C_ATT + 4 * a + 3))
                if a == 0:
                    output_kernels(0, False)
                for r in range(QG):
                    if r % 2:
                        ve.wait_ge(chunk_done, At(C_ATT + 4 * a + 2 + r // 2).plus(1 + OPEN))
                    else:
                        ve.wait_ge(proj_mm, a * 2 + r // 2 + 1)
                    ve.scalar_tensor_tensor(out=qT[:, r, :], in0=PS[:, q_bank(r), :], scalar=DH ** -0.5,
                                            in1=rstd_b[:, META:T], op0=ALU.mult, op1=ALU.mult
                                            ).then_inc(proj_ev, 1)
                    if r == 1:
                        ve.wait_ge(v_tr, a + 1)
                        ve.tensor_copy(vt[:, 0:4, :].rearrange("p t n -> p (t n)"), PS[:, 4, :])
                        ve.tensor_copy(vt[:, 4, :], PS[:, 5, 0:P]).then_inc(proj_ev, 1)
                        split_lo(At(C_ATT + 4 * a + 4))

            projected(0)

            ssm_batch(0, True, True)
            with ve.Fori(1, KS - 1) as i:
                link.loop(i, SSM_STEPS, first=1)
                ssm_batch(i, False, True)
            link.end_loop(KS - 2)
            ssm_batch(KS - 1, False, False)

            ve.wait_ge(late_loaded, 64)
            ts(negsink[:], negsink[:], -1.0, ALU.mult)
            ve.wait_ge(dist_in, 16)
            groups = [(n, b) for n in range(NBLK) for b in (0, 1)]
            def biased(a, gi, heads):
                n, b = groups[gi]
                d0 = META + P if n == 0 else 0
                for r in heads:
                    ve.wait_ge(s_mm, a * 32 + (4 * gi + r + 1))
                    h = a * 8 + QG * b + r
                    ve.scalar_tensor_tensor(out=sc[:, gi % 2, r, 0:width(n)], in0=dist[:, d0:d0 + width(n)],
                                            scalar=negslope[:, h:h + 1], in1=PS[:, 4 + r % 2, 0:width(n)],
                                            op0=ALU.mult, op1=ALU.add).then_inc(sc_done, 1)

            def maxima(a, gi, heads):
                n, b = groups[gi]
                par, hs = gi % 2, slice(heads[0], heads[1] + 1)
                ve.wait_ge(sc_done, a * 32 + (4 * gi + heads[1] + 1 + OPEN))
                link(ve.tensor_reduce(mx[:, par, hs], sc[:, par, hs, 0:width(n)], AX.X, ALU.max))

            def with_sink(a, gi):
                n, b = groups[gi]
                par = gi % 2
                nsk = negsink[:, a * 8 + QG * b:a * 8 + QG * b + QG]
                stt(negm[:, par], mx[:, par], -1.0, nsk, ALU.mult, ALU.min)
                ve.tensor_tensor(sk[:, par], negm[:, par], nsk, ALU.subtract).then_inc(negm_ready, 1)

            def normalised(a, gi):
                n, b = groups[gi]
                par = gi % 2
                ve.wait_ge(exp_done, a * 8 + gi + 1)
                tt(den[:, par], rs[:, par], sk[:, par], ALU.add)
                link(ve.reciprocal(den[:, par], den[:, par]))
                for r in range(QG):
                    tile = sc[:, par, r, 0:width(n)]
                    ins = ve.tensor_scalar(tile, tile, den[:, par, r:r + 1], None, ALU.mult)
                ins.then_inc(p_ready, 1)

            def prob_tiles(a, gi):
                n, b = groups[gi]
                ve.wait_ge(pv_mm, a * 8 + gi + 1)
                for r in (1, 3):
                    ve.wait_ge(t_mm, a * 32 + (4 * gi + r + 1))
                    ve.tensor_copy(pt[:, gi % 2, 0:blocks(n), r, :],
                                   PS[:, prob_bank(r), 0:blocks(n) * P].rearrange("p (j q) -> p j q", q=P)
                                   ).then_inc(pt_dve, 1)
                ve.tensor_copy(ptm[:, gi % 2].rearrange("p r q -> p (r q)"), PS[0:META, 2, :]
                               ).then_inc(pt_dve, 1)

            def result(a, gi):
                n, b = groups[gi]
                ve.wait_ge(yah_ready, a * 4 + (n + 1 + OPEN))
                rows = (slice(None), slice(a * 4, a * 4 + QG), slice(n * P, (n + 1) * P))
                ve.tensor_tensor(yal[rows], PS[:, 0 if n % 2 else 3, :].rearrange("p (r q) -> p r q", r=QG),
                                 as_f32(yah[rows]), ALU.subtract).then_inc(yal_ready, 1)

            for a in (0, 1):
                if a == 1:
                    projected(1)
                    split_lo(At(C_GLU))
                for gi in range(-1, last_group + 2):
                    if gi < last_group:
                        biased(a, gi + 1, (0, 1))
                    if 0 <= gi <= last_group:
                        normalised(a, gi)
                    if gi < last_group:
                        maxima(a, gi + 1, (0, 1))
                        biased(a, gi + 1, (2, 3))
                        maxima(a, gi + 1, (2, 3))
                        with_sink(a, gi + 1)
                    if 0 <= gi <= last_group:
                        prob_tiles(a, gi)
                    if gi > 0 and groups[gi - 1][1] == 1:
                        result(a, gi - 1)
                    if (a, gi) == (0, -1):
                        gelu_in(KS - 1)
                    if (a, gi) == (0, 0):
                        gelu_out(KS - 1)

            def z_of(bt):
                return uT[:, bt].rearrange("p s k -> p (s k)")[:, 0:SEQ]
            for bt in range(KS):
                ve.wait_ge(zh_ready, bt + 1)
                ve.tensor_tensor(zl[:, bt], z_of(bt), as_f32(zh[:, bt]), ALU.subtract).then_inc(zl_ready, 1)
            def scale_gates(c, m, slot):
                bank = merge_bank(slot)
                ve.wait_ge(chunk_done, c.plus(1 + OPEN))
                for q in (0, 1):
                    ins = ve.tensor_tensor(gsig[:, slot, q], PS[:, bank + q, :], rstd_b[:, META:T], ALU.mult)
                ins.then_inc(gates_scaled, 1)

            def merged(c, m, slot):
                bank = merge_bank(slot)
                ve.wait_ge(gates_sig, m.plus(1))
                ve.wait_ge(chunk_done, c.plus(1 + OPEN))
                ve.tensor_tensor(gsig[:, slot, 0], gsig[:, slot, 0], PS[:, bank + 2, :], ALU.mult)
                tt(gsig[:, slot, 1], gsig[:, slot, 1], PS[:, bank + 3, :], ALU.mult)
                ve.tensor_tensor(gsig[:, slot, 0], gsig[:, slot, 0], gsig[:, slot, 1], ALU.add).then_inc(mg_ready, 1)

            def merged_lo(m, slot):
                ve.wait_ge(mgh_ready, m.plus(1))
                mm = m.plus(0)
                ve.tensor_tensor(mgl[:, ds(mm, 1), :].rearrange("p o n -> p (o n)"), gsig[:, slot, 0],
                                 as_f32(mgh[:, ds(mm, 1), :].rearrange("p o n -> p (o n)")), ALU.subtract
                                 ).then_inc(mgl_ready, 1)

            scale_gates(At(C_GATE0), At(0), 0)
            split_lo(At(C_GATE1))
            for m in range(KS):
                ve.wait_ge(glu_sig, m + 1)
                if m >= 2:
                    ve.wait_ge(ysh_ready, m - 1)
                ve.tensor_tensor(ysf[:, m % 2].rearrange("p (k t) -> p t k", t=CHUNK),
                                 z_of(m).rearrange("p (t k) -> p t k", t=CHUNK),
                                 sig[:, m % 2].rearrange("p (t k) -> p t k", t=CHUNK), ALU.mult).then_inc(ysf_ready, 1)
                ve.wait_ge(ysh_ready, m + 1)
                ve.tensor_tensor(ysl[:, m], ysf[:, m % 2], as_f32(ysh[:, m]), ALU.subtract).then_inc(ysl_ready, 1)

            split_lo(At(C_BRANCH0))
            scale_gates(At(C_GATE1), At(1), 1)
            split_lo(At(C_BRANCH1))
            merged(At(C_BRANCH0), At(0), 0)
            split_lo(At(C_MERGE + 4))
            merged_lo(At(0), 0)
            merged(At(C_BRANCH1), At(1), 1)
            merged_lo(At(1), 1)
            with ve.Fori(1, KD // 2) as i:
                link.loop(i, 2, first=1)
                for j in (0, 1):
                    m = At(j, i, 2)
                    split_lo(At(C_MERGE + 2 * j + 1, i, 4))
                    scale_gates(At(C_MERGE + 2 * j, i, 4), m, j)
                    split_lo(At(C_MERGE + 2 * j + 2, i, 4))
                    merged(At(C_MERGE + 2 * j + 1, i, 4), m, j)
                    merged_lo(m, j)
            link.end_loop(KD // 2 - 1)

            norm_start(2)
            with ve.Fori(0, KD // 4) as i:
                for j in (0, 1):
                    split_lo(At(C_OUT + j + 1, i, 2))
                    for t in (0, 1):
                        m = At(2 * j + t, i, 4)
                        if t:
                            ve.wait_ge(chunk_done, At(C_OUT + j, i, 2).plus(1 + OPEN))
                        else:
                            ve.wait_ge(out_mm, At(j, i, 2).plus(1))
                        h = hT[:, ds(m.plus(0), 1), META:T].rearrange("p o n -> p (o n)")
                        ve.tensor_tensor(h, PS[:, 2 * j + t, :], h, ALU.add).then_inc(norms[2]["h_ready"], 1)
                        norm_step(2, m, False)
            ffn(1, C_UP2, C_DOWN2, False)
            token_var(3)
            ve.wait_ge(norms[3]["rcol_ready"], 1)
            for t in range(4):
                ve.wait_ge(fin_mm, t + 1)
                ve.tensor_scalar(y_nat[:, t, 512:1024], PS[:, 2 * t + 1, :], rcol[:, t + 1:t + 2], None, ALU.mult
                                 ).then_inc(fin_dve, 1)


_INS = ["x", "meta_tokens", "ffn1_norm", "ffn1_w_gate", "ffn1_w_up", "ffn1_w_down", "mix_norm", "w_in",
        "ssm_lam_re", "ssm_lam_im", "ssm_log_dt", "ssm_b_re", "ssm_b_im", "ssm_c_re", "ssm_c_im", "ssm_d",
        "ssm_w_glu", "attn_sink", "w_branch_ssm", "w_branch_attn", "w_out", "ffn2_norm", "ffn2_w_gate",
        "ffn2_w_up", "ffn2_w_down", "final_norm"]
_OUTS = [((1, 512, 1024), "float32")]


def kernel(**inputs):
    import numpy as _np
    import concourse.bacc as _bacc
    from concourse import mybir as _mybir
    from concourse.bass_utils import run_bass_kernel_spmd as _run

    nc = _bacc.Bacc("TRN2", target_bir_lowering=False, num_devices=1)
    arrays, args = {}, []
    for name in _INS:
        a = _np.ascontiguousarray(inputs[name])
        arrays[f"in_{name}_dram"] = a
        args.append(nc.dram_tensor(f"in_{name}_dram", a.shape, _mybir.dt.from_np(a.dtype), kind="ExternalInput").ap())
    for i, (shape, dtype) in enumerate(_OUTS):
        dt = _mybir.dt.from_np(_np.dtype(dtype))
        args.append(nc.dram_tensor(f"out_{i}_dram", shape, dt, kind="ExternalOutput").ap())
    build(nc, *args)
    r = _run(nc, [arrays], core_ids=[0])
    return r.results[0]["out_0_dram"]
```
